# Optimizing a Trainium2 kernel written in Bass

```python
import jax, jax.numpy as jnp
from jax import lax
import numpy as np
import math

D_MODEL = 1024
BATCH = 1
SEQ = 512
DEPTH = 1

D_FF = 2816
ROPE_THETA = 10000.0
NORM_EPS = 1e-6
Q_BLOCK = 128
H_A = 8
Q_LORA = 384
KV_LORA = 256
D_NOPE = 64
D_ROPE_A = 32
D_V_A = 64
H_IDX = 8
D_IDX = 32
TOPK_MAX = 256
DIL_PAIRS = ((128, 1), (512, 4), (2048, 16))
N_GROUPS_B = 3
H_B = 4
D_HEAD_B = 64
N_MOD = 9
COLS = (Q_LORA, KV_LORA, D_ROPE_A, D_IDX, H_IDX, 3 * N_GROUPS_B * H_B * D_HEAD_B, 2 * D_MODEL)
D_IN = sum(COLS)
WIDTH_A = H_A * D_V_A
WIDTH_B = H_B * D_HEAD_B


def rms_norm(x, g):
    xf = x.astype(jnp.float32)
    y = xf * lax.rsqrt(jnp.mean(xf * xf, axis=-1, keepdims=True) + NORM_EPS)
    return (y * g.astype(jnp.float32)).astype(x.dtype)

def rope(x, pos):
    d = x.shape[-1]
    half = d // 2
    inv = ROPE_THETA ** (-jnp.arange(half, dtype=jnp.float32) / half)
    ang = pos.astype(jnp.float32)[..., None] * inv
    ang = ang.reshape(ang.shape[:2] + (1,) * (x.ndim - 3) + (half,))
    cos, sin = jnp.cos(ang), jnp.sin(ang)
    xf = x.astype(jnp.float32)
    x1, x2 = xf[..., :half], xf[..., half:]
    return jnp.concatenate([x1 * cos - x2 * sin, x2 * cos + x1 * sin], axis=-1).astype(x.dtype)

def swiglu(h, w_gate, w_up, w_down):
    return (jax.nn.silu(h @ w_gate) * (h @ w_up)) @ w_down

def dsa_branch(c_q, c_kv, k_rope, k_idx, w_idx, pos, w_uq, w_uk, w_uv, w_iq):
    B, S, _ = c_q.shape
    topk = min(TOPK_MAX, S // 4)
    q = jnp.einsum('bsr,rhe->bshe', c_q, w_uq)
    q_nope, q_rope = q[..., :D_NOPE], rope(q[..., D_NOPE:], pos)
    k_rope = rope(k_rope[:, :, None, :], pos)[:, :, 0]
    q_lat = jnp.einsum('bshn,rhn->bshr', q_nope, w_uk)
    q_idx = rope(jnp.einsum('bsr,rhe->bshe', c_q, w_iq), pos)
    k_idx = rope(k_idx[:, :, None, :], pos)[:, :, 0]
    w_idx = w_idx * (H_IDX ** -0.5)
    attn_scale = (D_NOPE + D_ROPE_A) ** -0.5
    idx_scale = D_IDX ** -0.5
    key_pos = jnp.arange(S)
    gather = jax.vmap(lambda a, i: a[i])

    def block(i):
        t0 = i * Q_BLOCK
        tq = t0 + jnp.arange(Q_BLOCK)
        qi = lax.dynamic_slice_in_dim(q_idx, t0, Q_BLOCK, axis=1)
        wi = lax.dynamic_slice_in_dim(w_idx, t0, Q_BLOCK, axis=1)
        logits = jnp.einsum('bqhe,bse->bqhs', qi, k_idx).astype(jnp.float32) * idx_scale
        iscore = jnp.einsum('bqh,bqhs->bqs', wi.astype(jnp.float32), jax.nn.relu(logits))
        causal = key_pos[None, :] <= tq[:, None]
        iscore = jnp.where(causal[None], iscore, -jnp.inf)
        _, sel = lax.top_k(iscore, topk)
        valid = sel <= tq[None, :, None]
        ckv_sel = gather(c_kv, sel)
        kr_sel = gather(k_rope, sel)
        ql = lax.dynamic_slice_in_dim(q_lat, t0, Q_BLOCK, axis=1)
        qr = lax.dynamic_slice_in_dim(q_rope, t0, Q_BLOCK, axis=1)
        s = (jnp.einsum('bqhr,bqkr->bqhk', ql, ckv_sel)
             + jnp.einsum('bqhe,bqke->bqhk', qr, kr_sel)).astype(jnp.float32) * attn_scale
        s = jnp.where(valid[:, :, None, :], s, -jnp.inf)
        p = jax.nn.softmax(s, axis=-1)
        return jnp.einsum('bqhk,bqkr->bqhr', p.astype(c_kv.dtype), ckv_sel)

    o_lat = lax.map(block, jnp.arange(S // Q_BLOCK))
    o_lat = jnp.moveaxis(o_lat, 0, 1).reshape(B, S, H_A, KV_LORA)
    o = jnp.einsum('bshr,rhv->bshv', o_lat, w_uv)
    return o.reshape(B, S, WIDTH_A)

def dilated_group(q, k, v, window, dilation):
    B, S, H, dh = q.shape
    offs = jnp.arange(window // dilation + 1) * dilation
    scale = dh ** -0.5

    def block(i):
        t0 = i * Q_BLOCK
        tq = t0 + jnp.arange(Q_BLOCK)
        idx = tq[:, None] - offs[None, :]
        valid = idx >= 0
        idxc = jnp.maximum(idx, 0)
        kg = k[:, idxc]
        vg = v[:, idxc]
        qb = lax.dynamic_slice_in_dim(q, t0, Q_BLOCK, axis=1)
        s = jnp.einsum('bqhe,bqnhe->bqhn', qb, kg).astype(jnp.float32) * scale
        s = jnp.where(valid[None, :, None, :], s, -jnp.inf)
        lse = jax.nn.logsumexp(s, axis=-1)
        p = jnp.exp(s - lse[..., None])
        o = jnp.einsum('bqhn,bqnhe->bqhe', p.astype(v.dtype), vg)
        return o, lse

    o, lse = lax.map(block, jnp.arange(S // Q_BLOCK))
    o = jnp.moveaxis(o, 0, 1).reshape(B, S, H, dh)
    lse = jnp.moveaxis(lse, 0, 1).reshape(B, S, H)
    return o, lse

def dilated_branch(qkv, pos):
    B, S = qkv.shape[:2]
    q = rope(qkv[:, :, 0], pos)
    k = rope(qkv[:, :, 1], pos)
    v = qkv[:, :, 2]
    outs, lses = [], []
    for g, (window, dilation) in enumerate(DIL_PAIRS):
        o, lse = dilated_group(q[:, :, g], k[:, :, g], v[:, :, g], window, dilation)
        outs.append(o)
        lses.append(lse)
    wts = jax.nn.softmax(jnp.stack(lses, axis=0), axis=0)
    o = jnp.sum(wts[..., None].astype(v.dtype) * jnp.stack(outs, axis=0), axis=0)
    return o.reshape(B, S, WIDTH_B)

def hybrid_mixer(u, pos, w_in, g_cq, g_ckv, w_uq, w_uk, w_uv, w_iq, w_up_a, w_up_b, w_o):
    B, S, _ = u.shape
    proj = u @ w_in
    splits, acc = [], 0
    for n in COLS[:-1]:
        acc += n
        splits.append(acc)
    c_q, c_kv, k_rope, k_idx, w_idx, qkv_b, gates = jnp.split(proj, splits, axis=-1)
    c_q = rms_norm(c_q, g_cq)
    c_kv = rms_norm(c_kv, g_ckv)
    o_a = dsa_branch(c_q, c_kv, k_rope, k_idx, w_idx, pos, w_uq, w_uk, w_uv, w_iq)
    o_b = dilated_branch(qkv_b.reshape(B, S, 3, N_GROUPS_B, H_B, D_HEAD_B), pos)
    g_a, g_b = jnp.split(gates, 2, axis=-1)
    z = jax.nn.sigmoid(g_a) * (o_a @ w_up_a) + jax.nn.sigmoid(g_b) * (o_b @ w_up_b)
    return z @ w_o

def first_inputs(seed: int = 0) -> dict:
    key = jax.random.key(seed)
    ks = jax.random.split(key, 32)
    L, D = DEPTH, D_MODEL

    def nrm(k, shape, fan_in):
        return jax.random.normal(k, shape, jnp.float32) * (fan_in ** -0.5)

    def gain(k, shape):
        return 1.0 + 0.05 * jax.random.normal(k, shape, jnp.float32)

    x = jax.random.normal(ks[0], (BATCH, SEQ, D), jnp.float32)
    c = jax.random.normal(ks[1], (BATCH, D), jnp.float32)
    positions = (jax.random.randint(ks[2], (BATCH, 1), 0, 512, dtype=jnp.int32)
                 + jnp.arange(SEQ, dtype=jnp.int32)[None, :])
    return {
        "x": x,
        "c": c,
        "positions": positions,
        "w_mod": 0.5 * nrm(ks[3], (L, D, N_MOD * D), D),
        "b_mod": 0.01 * jax.random.normal(ks[4], (L, N_MOD * D), jnp.float32),
        "g_pre_ffn1": gain(ks[5], (L, D)),
        "w_gate1": nrm(ks[6], (L, D, D_FF), D),
        "w_up1": nrm(ks[7], (L, D, D_FF), D),
        "w_down1": nrm(ks[8], (L, D_FF, D), D_FF),
        "g_post_ffn1": gain(ks[9], (L, D)),
        "g_pre_mix": gain(ks[10], (L, D)),
        "w_in": nrm(ks[11], (L, D, D_IN), D),
        "g_cq": gain(ks[12], (L, Q_LORA)),
        "g_ckv": gain(ks[13], (L, KV_LORA)),
        "w_uq": nrm(ks[14], (L, Q_LORA, H_A, D_NOPE + D_ROPE_A), Q_LORA),
        "w_uk": nrm(ks[15], (L, KV_LORA, H_A, D_NOPE), KV_LORA),
        "w_uv": nrm(ks[16], (L, KV_LORA, H_A, D_V_A), KV_LORA),
        "w_iq": nrm(ks[17], (L, Q_LORA, H_IDX, D_IDX), Q_LORA),
        "w_up_a": nrm(ks[18], (L, WIDTH_A, D), WIDTH_A),
        "w_up_b": nrm(ks[19], (L, WIDTH_B, D), WIDTH_B),
        "w_o": nrm(ks[20], (L, D, D), D),
        "g_post_mix": gain(ks[21], (L, D)),
        "g_pre_ffn2": gain(ks[22], (L, D)),
        "w_gate2": nrm(ks[23], (L, D, D_FF), D),
        "w_up2": nrm(ks[24], (L, D, D_FF), D),
        "w_down2": nrm(ks[25], (L, D_FF, D), D_FF),
        "g_post_ffn2": gain(ks[26], (L, D)),
    }

def first_block(x, c, positions, w_mod, b_mod, g_pre_ffn1, w_gate1, w_up1, w_down1, g_post_ffn1,
              g_pre_mix, w_in, g_cq, g_ckv, w_uq, w_uk, w_uv, w_iq, w_up_a, w_up_b, w_o, g_post_mix,
              g_pre_ffn2, w_gate2, w_up2, w_down2, g_post_ffn2):
    B = x.shape[0]
    for l in range(DEPTH):
        mod = (jax.nn.silu(c) @ w_mod[l] + b_mod[l]).reshape(B, N_MOD, D_MODEL)
        sh1, sc1, gt1, sh2, sc2, gt2, sh3, sc3, gt3 = [mod[:, j, None, :] for j in range(N_MOD)]
        h = rms_norm(x, g_pre_ffn1[l]) * (1 + sc1) + sh1
        x = x + 0.5 * gt1 * rms_norm(swiglu(h, w_gate1[l], w_up1[l], w_down1[l]), g_post_ffn1[l])
        u = rms_norm(x, g_pre_mix[l]) * (1 + sc2) + sh2
        y = hybrid_mixer(u, positions, w_in[l], g_cq[l], g_ckv[l], w_uq[l], w_uk[l], w_uv[l], w_iq[l],
                         w_up_a[l], w_up_b[l], w_o[l])
        x = x + gt2 * rms_norm(y, g_post_mix[l])
        h = rms_norm(x, g_pre_ffn2[l]) * (1 + sc3) + sh3
        x = x + 0.5 * gt3 * rms_norm(swiglu(h, w_gate2[l], w_up2[l], w_down2[l]), g_post_ffn2[l])
    return x


D_MIX = D_MODEL
EPS = 1e-6

MLA_HEADS = 8
MLA_QK_NOPE = 64
MLA_QK_ROPE = 32
MLA_QK_DIM = MLA_QK_NOPE + MLA_QK_ROPE
MLA_V_DIM = 64
MLA_Q_RANK = 256
MLA_KV_RANK = 128
MLA_WIDTH = MLA_HEADS * MLA_V_DIM
ATTN_BLOCK = 128

RET_HEADS = 8
RET_HEAD_DIM = 64
RET_WIDTH = RET_HEADS * RET_HEAD_DIM
RET_CHUNK = 128

IN_SPLITS = (
    MLA_Q_RANK,
    MLA_KV_RANK,
    MLA_QK_ROPE,
    RET_WIDTH, RET_WIDTH, RET_WIDTH, RET_WIDTH,
)
IN_COLS = sum(IN_SPLITS)

PEER_HEADS = 8
PEER_N_KEYS = 128
PEER_N_EXPERTS = PEER_N_KEYS * PEER_N_KEYS
PEER_KEY_DIM = 256
PEER_HALF = PEER_KEY_DIM // 2
PEER_TOPK = 16
PEER_TOKEN_BLOCK = 128


def rms_norm_2(x, g):
    xf = x.astype(jnp.float32)
    y = xf * lax.rsqrt(jnp.mean(xf * xf, axis=-1, keepdims=True) + EPS)
    return (y * g.astype(jnp.float32)).astype(x.dtype)

def rope_2(x, positions):
    d = x.shape[-1]
    inv = ROPE_THETA ** (-jnp.arange(0, d, 2, dtype=jnp.float32) / d)
    ang = positions.astype(jnp.float32)[:, :, None, None] * inv
    cos, sin = jnp.cos(ang), jnp.sin(ang)
    x1, x2 = jnp.split(x.astype(jnp.float32), 2, axis=-1)
    out = jnp.concatenate([x1 * cos - x2 * sin, x1 * sin + x2 * cos], axis=-1)
    return out.astype(x.dtype)

def mla_group(q_lat, kv_lat, k_rope, positions, g_q_norm, w_uq, g_kv_norm, w_ukv):
    B, S, _ = q_lat.shape
    q = (rms_norm_2(q_lat, g_q_norm) @ w_uq).reshape(B, S, MLA_HEADS, MLA_QK_DIM)
    q_nope, q_rope = q[..., :MLA_QK_NOPE], q[..., MLA_QK_NOPE:]
    q_rope = rope_2(q_rope, positions)
    kv = (rms_norm_2(kv_lat, g_kv_norm) @ w_ukv).reshape(B, S, MLA_HEADS, MLA_QK_NOPE + MLA_V_DIM)
    k_nope, v = kv[..., :MLA_QK_NOPE], kv[..., MLA_QK_NOPE:]
    k_r = rope_2(k_rope[:, :, None, :], positions)
    k = jnp.concatenate([k_nope, jnp.broadcast_to(k_r, (B, S, MLA_HEADS, MLA_QK_ROPE))], axis=-1)
    qh = jnp.concatenate([q_nope, q_rope], axis=-1) * (MLA_QK_DIM ** -0.5)

    nb = S // ATTN_BLOCK
    q_blocks = qh.reshape(B, nb, ATTN_BLOCK, MLA_HEADS, MLA_QK_DIM).transpose(1, 0, 2, 3, 4)
    key_pos = jnp.arange(S)

    def one_block(args):
        qb, bi = args
        s = jnp.einsum('bqhd,bkhd->bhqk', qb, k).astype(jnp.float32)
        q_pos = bi * ATTN_BLOCK + jnp.arange(ATTN_BLOCK)
        mask = key_pos[None, :] <= q_pos[:, None]
        s = jnp.where(mask[None, None], s, -jnp.inf)
        p = jax.nn.softmax(s, axis=-1).astype(v.dtype)
        return jnp.einsum('bhqk,bkhd->bqhd', p, v)

    out = lax.map(one_block, (q_blocks, jnp.arange(nb)))
    return out.transpose(1, 0, 2, 3, 4).reshape(B, S, MLA_WIDTH)

def retention_group(q, k, v, gate, positions, g_ret_norm):
    B, S, _ = q.shape
    H, d, C = RET_HEADS, RET_HEAD_DIM, RET_CHUNK
    nc = S // C
    q = rope_2(q.reshape(B, S, H, d), positions)
    k = rope_2(k.reshape(B, S, H, d), positions) * (d ** -0.5)
    v = v.reshape(B, S, H, d)

    gamma = 1.0 - 2.0 ** (-5.0 - jnp.arange(H, dtype=jnp.float32))
    log_g = jnp.log(gamma)
    idx = jnp.arange(C, dtype=jnp.float32)
    diff = idx[:, None] - idx[None, :]
    dmask = jnp.where(diff >= 0, jnp.exp(log_g[:, None, None] * jnp.maximum(diff, 0.0)), 0.0)

    qc = q.reshape(B, nc, C, H, d).astype(jnp.float32)
    kc = k.reshape(B, nc, C, H, d).astype(jnp.float32)
    vc = v.reshape(B, nc, C, H, d).astype(jnp.float32)

    scores = jnp.einsum('bnihd,bnjhd->bnhij', qc, kc) * dmask
    y_inner = jnp.einsum('bnhij,bnjhd->bnihd', scores, vc)

    zeta = jnp.exp(log_g[:, None] * (C - 1.0 - idx))
    kv_chunk = jnp.einsum('bnjhk,hj,bnjhv->bnhkv', kc, zeta, vc)
    chunk_decay = jnp.exp(log_g * C)

    def step(state, kv_n):
        return state * chunk_decay[None, :, None, None] + kv_n, state

    _, prev = lax.scan(step, jnp.zeros((B, H, d, d), jnp.float32), kv_chunk.transpose(1, 0, 2, 3, 4))
    prev = prev.transpose(1, 0, 2, 3, 4)
    xi = jnp.exp(log_g[:, None] * (idx + 1.0))
    y_cross = jnp.einsum('bnihk,bnhkv,hi->bnihv', qc, prev, xi)

    y = (y_inner + y_cross).reshape(B, S, H, d)
    mu = jnp.mean(y, axis=-1, keepdims=True)
    var = jnp.mean(jnp.square(y - mu), axis=-1, keepdims=True)
    yn = ((y - mu) * lax.rsqrt(var + EPS)).reshape(B, S, RET_WIDTH) * g_ret_norm.astype(jnp.float32)
    return (jax.nn.silu(gate.astype(jnp.float32)) * yn).astype(gate.dtype)

def peer(h, w_query, sub_keys, expert_u, expert_v):
    B, S, D = h.shape
    T = B * S
    K = PEER_TOPK
    xt = h.reshape(T, D)
    q = (xt @ w_query).reshape(T, PEER_HEADS, 2, PEER_HALF)
    s = jnp.einsum('thpd,pkd->thpk', q, sub_keys).astype(jnp.float32)
    s_top, i_top = lax.top_k(s, K)
    cand = (s_top[:, :, 0, :, None] + s_top[:, :, 1, None, :]).reshape(T, PEER_HEADS, K * K)
    cand_idx = (i_top[:, :, 0, :, None] * PEER_N_KEYS + i_top[:, :, 1, None, :]).reshape(T, PEER_HEADS, K * K)
    best, pos = lax.top_k(cand, K)
    eidx = jnp.take_along_axis(cand_idx, pos, axis=-1)
    g = jax.nn.softmax(best, axis=-1)

    nb = T // PEER_TOKEN_BLOCK

    def one_block(args):
        xb, ib, gb = args
        u = expert_u[ib]
        a = jax.nn.gelu(jnp.einsum('thkd,td->thk', u, xb).astype(jnp.float32), approximate=False)
        w = (gb * a).astype(expert_v.dtype)
        return jnp.einsum('thk,thkd->td', w, expert_v[ib])

    out = lax.map(one_block, (xt.reshape(nb, PEER_TOKEN_BLOCK, D),
                              eidx.reshape(nb, PEER_TOKEN_BLOCK, PEER_HEADS, K),
                              g.reshape(nb, PEER_TOKEN_BLOCK, PEER_HEADS, K)))
    return out.reshape(B, S, D)

def second_inputs(seed: int = 0) -> dict:
    key = jax.random.key(seed)
    ks = jax.random.split(key, 20)
    L, D = DEPTH, D_MODEL
    nrm = lambda k, shape, scale: jax.random.normal(k, shape, jnp.float32) * scale
    gain = lambda k, shape: 1.0 + 0.02 * jax.random.normal(k, shape, jnp.float32)
    return {
        "x": nrm(ks[0], (BATCH, SEQ, D), 1.0),
        "c": nrm(ks[1], (BATCH, D), 1.0),
        "positions": jnp.broadcast_to(jnp.arange(SEQ, dtype=jnp.int32), (BATCH, SEQ)),
        "w_ada": nrm(ks[2], (L, D, 6 * D), D ** -0.5),
        "b_ada": nrm(ks[3], (L, 6 * D), 0.01),
        "g_norm1": gain(ks[4], (L, D)),
        "w_in": nrm(ks[5], (L, D, IN_COLS), D ** -0.5),
        "g_q_norm": gain(ks[6], (L, MLA_Q_RANK)),
        "w_uq": nrm(ks[7], (L, MLA_Q_RANK, MLA_HEADS * MLA_QK_DIM), MLA_Q_RANK ** -0.5),
        "g_kv_norm": gain(ks[8], (L, MLA_KV_RANK)),
        "w_ukv": nrm(ks[9], (L, MLA_KV_RANK, MLA_HEADS * (MLA_QK_NOPE + MLA_V_DIM)), MLA_KV_RANK ** -0.5),
        "g_ret_norm": gain(ks[10], (L, RET_WIDTH)),
        "w_out": nrm(ks[11], (L, MLA_WIDTH + RET_WIDTH, D), (MLA_WIDTH + RET_WIDTH) ** -0.5),
        "g_norm2": gain(ks[12], (L, D)),
        "w_query": nrm(ks[13], (L, D, PEER_HEADS * PEER_KEY_DIM), D ** -0.5),
        "sub_keys": nrm(ks[14], (L, 2, PEER_N_KEYS, PEER_HALF), PEER_HALF ** -0.5),
        "expert_u": nrm(ks[15], (L, PEER_N_EXPERTS, D), D ** -0.5),
        "expert_v": nrm(ks[16], (L, PEER_N_EXPERTS, D), 0.5),
        "g_final": gain(ks[17], (D,)),
    }

def second_block(x, c, positions, w_ada, b_ada, g_norm1, w_in, g_q_norm, w_uq, g_kv_norm, w_ukv,
              g_ret_norm, w_out, g_norm2, w_query, sub_keys, expert_u, expert_v, g_final):
    offs = np.cumsum(IN_SPLITS)[:-1].tolist()
    for l in range(DEPTH):
        mod = jax.nn.silu(c) @ w_ada[l] + b_ada[l]
        sh1, sc1, gt1, sh2, sc2, gt2 = [m[:, None, :] for m in jnp.split(mod, 6, axis=-1)]

        h = rms_norm_2(x, g_norm1[l]) * (1.0 + sc1) + sh1
        proj = h @ w_in[l]
        q_lat, kv_lat, k_rope, rq, rk, rv, rg = jnp.split(proj, offs, axis=-1)
        y_mla = mla_group(q_lat, kv_lat, k_rope, positions, g_q_norm[l], w_uq[l], g_kv_norm[l], w_ukv[l])
        y_ret = retention_group(rq, rk, rv, rg, positions, g_ret_norm[l])
        mixed = jnp.concatenate([y_mla.astype(x.dtype), y_ret.astype(x.dtype)], axis=-1) @ w_out[l]
        x = x + gt1 * mixed

        h2 = rms_norm_2(x, g_norm2[l]) * (1.0 + sc2) + sh2
        x = x + gt2 * peer(h2, w_query[l], sub_keys[l], expert_u[l], expert_v[l]).astype(x.dtype)
    return rms_norm_2(x, g_final)


def setup_inputs(seed=0):
    out = dict(first_inputs(seed))
    for name, value in second_inputs(seed + 1).items():
        if name != "x":
            out[name + "_2"] = value
    return out


def reference(
    x, c, positions, w_mod, b_mod, g_pre_ffn1, w_gate1, w_up1, w_down1, g_post_ffn1, g_pre_mix,
    w_in, g_cq, g_ckv, w_uq, w_uk, w_uv, w_iq, w_up_a, w_up_b, w_o, g_post_mix, g_pre_ffn2,
    w_gate2, w_up2, w_down2, g_post_ffn2, c_2, positions_2, w_ada_2, b_ada_2, g_norm1_2, w_in_2,
    g_q_norm_2, w_uq_2, g_kv_norm_2, w_ukv_2, g_ret_norm_2, w_out_2, g_norm2_2, w_query_2,
    sub_keys_2, expert_u_2, expert_v_2, g_final_2,
):
    x = first_block(
        x, c, positions, w_mod, b_mod, g_pre_ffn1, w_gate1, w_up1, w_down1, g_post_ffn1,
        g_pre_mix, w_in, g_cq, g_ckv, w_uq, w_uk, w_uv, w_iq, w_up_a, w_up_b, w_o, g_post_mix,
        g_pre_ffn2, w_gate2, w_up2, w_down2, g_post_ffn2,
    )
    return second_block(
        x, c_2, positions_2, w_ada_2, b_ada_2, g_norm1_2, w_in_2, g_q_norm_2, w_uq_2,
        g_kv_norm_2, w_ukv_2, g_ret_norm_2, w_out_2, g_norm2_2, w_query_2, sub_keys_2,
        expert_u_2, expert_v_2, g_final_2,
    )


_drawn_inputs = setup_inputs


def setup_inputs(seed=0):
    import zlib

    import numpy as np

    out = dict(_drawn_inputs(seed))
    spreads = {}
    factors = {'g_pre_ffn2': 2.712,
     'g_post_ffn2': 3.287,
     'g_q_norm_2': 8.0,
     'g_kv_norm_2': 5.061,
     'g_ret_norm_2': 18.271,
     'g_final_2': 7.821,
     'g_norm2_2': 5.245}
    for name, (base, spread) in spreads.items():
        noise = np.random.default_rng([zlib.crc32(name.encode()), seed]).standard_normal(out[name].shape)
        drawn = base * np.exp(spread * noise) if base else spread * noise
        out[name] = __import__('jax').numpy.asarray(drawn.astype(out[name].dtype))
    for name, factor in factors.items():
        out[name] = (out[name] * factor).astype(out[name].dtype)
    return out
```

```python
from contextlib import ExitStack

import numpy as np

import concourse.bass as bass
from concourse import mybir

F32 = mybir.dt.float32
I32 = mybir.dt.int32
U32 = mybir.dt.uint32
ALU = mybir.AluOpType
ACT = mybir.ActivationFunctionType
AX = mybir.AxisListType

P = 128
S = 512
D = 1024
TT = S // P
DC = D // P
F = 2816
FC = F // P
EPS = 1e-6
THETA = 10000.0
NEG = -1e30

QL, KVL, NOPE, ROPE_A, DV = 384, 256, 64, 32, 64
HEADS = 8
IDX = 32
TOPK = 128
GRP, HB, DH = 3, 4, 64
DIL = ((128, 1), (512, 4), (2048, 16))
C_CKV = QL
C_KR = QL + KVL
C_KI = C_KR + ROPE_A
C_WI = C_KI + IDX
C_QKV = C_WI + HEADS
C_GATE = C_QKV + 3 * GRP * HB * DH
DQ = NOPE + ROPE_A
QL2, KVL2 = 256, 128
RW = 512
C2_KR = QL2 + KVL2
C2_RET = C2_KR + ROPE_A
PH, NKEY, KH, PK = 8, 128, 128, 16
NEXP = NKEY * NKEY

VECS = [("g_pre_ffn1", 8), ("g_pre_mix", 8), ("g_pre_ffn2", 8), ("g_norm1_2", 8), ("g_norm2_2", 8),
        ("g_cq", 3), ("g_ckv", 2), ("g_q_norm_2", 2), ("g_kv_norm_2", 1), ("c", 8), ("c_2", 8),
        ("g_post_ffn1", 8), ("g_post_mix", 8), ("g_post_ffn2", 8), ("g_final_2", 8), ("g_ret_norm_2", 4)]
VEC_AT = {}
_n = 0
for _name, _k in VECS:
    VEC_AT[_name] = _n
    _n += _k
NVEC = _n
NMOD1, NMOD2 = 9 * DC, 6 * DC
NMOD = NMOD1 + NMOD2

CONSTS = {}


def build_constants():
    p = np.arange(P)
    parts = []

    def put(name, a):
        at = sum(x.shape[1] for x in parts)
        CONSTS[name] = (at, a.shape[1])
        parts.append(np.ascontiguousarray(a, np.float32))

    put("identity", np.eye(P))
    put("ones", np.ones((P, P)))
    put("causal_bias", np.where(p[None, :] <= p[:, None], 0.0, NEG))
    put("decay_mask", np.concatenate([(p[None, :] >= p[:, None]) * 1.0, np.ones((P, S - P))], 1))
    f32 = np.float32
    inv = [f32(THETA) ** (-np.arange(h, dtype=f32) / f32(h)) for h in (ROPE_A // 2, DH // 2)]
    put("inv_freq", np.tile(np.concatenate(inv)[None], (P, 1)))
    log_g = np.log(1.0 - 2.0 ** (-5.0 - np.arange(HEADS)))
    t = (np.arange(TT)[None, :] * P + p[:, None])[:, :, None]
    put("q_decay", np.exp(log_g * t).reshape(P, -1))
    put("k_decay", (np.exp(-log_g * t) * DH ** -0.5).reshape(P, -1))
    put("iota", np.tile(np.arange(PK)[None], (P, 1)))
    put("half_pi", np.full((P, 1), np.pi / 2))
    put("eps", np.full((P, 1), EPS))
    return np.concatenate(parts, 1)


CONST_PACK = build_constants()


def build_dilated_bias():
    n = np.arange(P)
    out = np.full((P, TT, S + 2 * P), NEG, np.float32)
    for r in range(TT):
        for r2 in range(TT):
            d = (4 * n + r)[:, None] - (4 * n + r2)[None, :]
            out[:, r, r2 * P:(r2 + 1) * P][(d >= 0) & (d <= DIL[0][0])] = 0
        d = 4 * (n[:, None] - n[None, :])
        for g in (1, 2):
            at = S + (g - 1) * P
            out[:, r, at:at + P][(d >= 0) & (d <= DIL[g][0]) & (d % DIL[g][1] == 0)] = 0
    return out.reshape(P, -1)


DILATED_BIAS = build_dilated_bias()


class Chain:

    def __init__(self, eng, sem):
        self.eng, self.sem, self.n = eng, sem, 0

    def __call__(self, ins):
        self.n += 1
        ins.then_inc(self.sem, 1)
        self.eng.wait_ge(self.sem, self.n)


def root_mean(nc, b, act, stat, n, squares, count, rooted):
    act.wait_ge(squares, count)
    nc.scalar.activation(stat, stat, ACT.Sqrt, scale=1.0 / n, bias=b.const("eps")).then_inc(rooted, 1)


class Bufs:

    def __init__(self, nc):
        self.nc, self.sems = nc, []

    def sem(self, name):
        self.sems.append(self.nc.alloc_semaphore(name))
        return self.sems[-1]

    def end_of_part(self):
        self.nc.clear_and_free_semaphores(self.sems)
        self.nc.all_engine_barrier()
        self.sems = []


def mm(nc, out, lhsT, rhs, start, stop):
    return nc.tensor.matmul(out, lhsT, rhs, start=start, stop=stop, skip_group_check=True)


def stage_setup(nc, b, d):
    with ExitStack() as own:
        vec_rows = own.enter_context(nc.sbuf_tensor("vec_rows", [NVEC, P], F32))
        bias_rows = own.enter_context(nc.sbuf_tensor("bias_rows", [NMOD, P], F32))
        pos_i = own.enter_context(nc.sbuf_tensor("pos_i", [2 * TT, P], I32))
        pos_rows = own.enter_context(nc.sbuf_tensor("pos_rows", [2 * TT, P], F32))
        pos_col = own.enter_context(nc.sbuf_tensor("pos_col", [P, 2 * TT], F32))
        NA = 2 * TT * b.n_freq
        ang = own.enter_context(nc.sbuf_tensor("ang", [P, 2 * TT, b.n_freq], F32))
        turns = own.enter_context(nc.sbuf_tensor("turns", [P, NA], F32))
        c_sig = own.enter_context(nc.sbuf_tensor("c_sig", [P, 2 * DC], F32))
        const_in = b.sem("const_in")
        x_in = b.sem("x_in")
        vec_in = b.sem("vec_in")
        pos_in = b.sem("pos_in")
        pos_float = b.sem("pos_float")
        cols_up = b.sem("cols_turned")
        setup_chain = b.sem("setup_chain")
        angle_ready = b.sem("angle_ready")
        n_vec_dma = len(VECS) + 2
        with nc.Block() as block:
            @block.sync
            def _(sp):
                sp.dma_start(pos_i[0:TT, :], d["positions"].rearrange("a (i p) -> (a i) p", p=P)).then_inc(pos_in, 16)
                sp.dma_start(pos_i[TT:2 * TT, :],
                             d["positions_2"].rearrange("a (i p) -> (a i) p", p=P)).then_inc(pos_in, 16)
                sp.dma_start(b.consts[:, :], d["const_pack"]).then_inc(const_in, 16)
                sp.dma_start(b.x[:, :, :], d["x"].rearrange("a (i p) n -> p (a i) n", p=P)).then_inc(x_in, 16)
                sp.wait_ge(x_in, 16)

            @block.scalar
            def _(act):
                for name, k in VECS:
                    v = d[name]
                    v = v.rearrange("(k p) -> k p", p=P) if len(v.shape) == 1 else v.rearrange("a (k p) -> (a k) p", p=P)
                    at = VEC_AT[name]
                    act.dma_start(vec_rows[at:at + k, :], v).then_inc(vec_in, 16)
                act.dma_start(bias_rows[0:NMOD1, :], d["b_mod"].rearrange("a (k p) -> (a k) p", p=P)).then_inc(vec_in, 16)
                act.dma_start(bias_rows[NMOD1:NMOD, :],
                              d["b_ada_2"].rearrange("a (k p) -> (a k) p", p=P)).then_inc(vec_in, 16)
                act.wait_ge(cols_up, 4)
                at = VEC_AT["c"]
                nc.scalar.activation(c_sig[:, :], b.vec[:, at:at + 2 * DC], ACT.Sigmoid).then_inc(angle_ready, 1)
                act.wait_ge(angle_ready, 3)
                nc.scalar.activation(b.sin[:, :, :].rearrange("p a f -> p (a f)"),
                                     ang[:, :, :].rearrange("p a f -> p (a f)"), ACT.Sin)
                nc.scalar.activation(b.cos[:, :, :].rearrange("p a f -> p (a f)"), turns[:, :], ACT.Sin,
                                     bias=b.const("half_pi"), scale=-1.0)

            @block.tensor
            def _(pe):
                pe.wait_ge(const_in, 16)
                pe.wait_ge(pos_float, 1)
                ident = b.const("identity")
                nc.tensor.transpose(b.ps[:, 0, 0:2 * TT], pos_rows[:, :], ident[0:2 * TT, 0:2 * TT]).then_inc(cols_up, 1)
                pe.wait_ge(vec_in, 16 * n_vec_dma)
                nc.tensor.transpose(b.ps[:, 1, 0:NVEC], vec_rows[:, :], ident[0:NVEC, 0:NVEC]).then_inc(cols_up, 1)
                nc.tensor.transpose(b.ps[:, 2, 0:NMOD], bias_rows[:, :], ident[0:NMOD, 0:NMOD]).then_inc(cols_up, 1)

            @block.vector
            def _(dve):
                link = Chain(dve, setup_chain)
                dve.wait_ge(pos_in, 32)
                nc.vector.tensor_copy(pos_rows[:, :], pos_i[:, :]).then_inc(pos_float, 1)
                dve.wait_ge(cols_up, 1)
                link(nc.vector.tensor_copy(pos_col[:, :], b.ps[:, 0, 0:2 * TT]))
                dve.wait_ge(const_in, 16)
                dve.wait_ge(cols_up, 3)
                link(nc.vector.tensor_copy(b.bias_cols[:, :], b.ps[:, 2, 0:NMOD]))
                nc.vector.tensor_copy(b.vec[:, :], b.ps[:, 1, 0:NVEC]).then_inc(cols_up, 1)
                inv = b.const("inv_freq").unsqueeze(1).to_broadcast([P, 2 * TT, b.n_freq])
                link(nc.vector.tensor_tensor(ang[:, :, :], inv,
                                             pos_col[:, :].unsqueeze(2).to_broadcast([P, 2 * TT, b.n_freq]), ALU.mult))
                a = ang[:, :, :].rearrange("p a f -> p (a f)")
                magic = 1.5 * 2.0 ** 23
                two_pi = 2 * np.pi
                c1 = 6.28125
                c2 = round((two_pi - c1) * 2 ** 21) / 2 ** 21
                c3 = two_pi - c1 - c2
                link(nc.vector.tensor_scalar(turns[:, :], a, float(1 / two_pi), None, ALU.mult))
                link(nc.vector.tensor_scalar(turns[:, :], turns[:, :], magic, None, ALU.add))
                link(nc.vector.tensor_scalar(turns[:, :], turns[:, :], -magic, None, ALU.add))
                for part in (c1, c2, c3):
                    link(nc.vector.scalar_tensor_tensor(a, turns[:, :], -float(part), a, ALU.mult, ALU.add))
                link(nc.vector.tensor_scalar(a, a, 3.1415925, -3.1415925, ALU.min, ALU.max))
                nc.vector.scalar_tensor_tensor(turns[:, :], a, -1.0, a, ALU.mult, ALU.max).then_inc(angle_ready, 1)
                dve.wait_ge(angle_ready, 2)
                at = VEC_AT["c"]
                nc.vector.tensor_tensor(b.silu_c[:, :], c_sig[:, :], b.vec[:, at:at + 2 * DC],
                                        ALU.mult).then_inc(angle_ready, 1)


def stage_modulation(nc, b, d):
    W = 512
    with ExitStack() as own:
        w = own.enter_context(nc.sbuf_tensor("mod_w", [P, 2, DC, W], F32))
        acc = own.enter_context(nc.sbuf_tensor("mod_acc", [P, 2, W], F32))
        diag = own.enter_context(nc.sbuf_tensor("gate_diag", [P, 2, 4, P], F32))
        gates = own.enter_context(nc.sbuf_tensor("gate_cols", [P, 6, DC], F32))
        w_in = [b.sem(f"mod_w_in{j}") for j in range(2)]
        part = b.sem("mod_part")
        summed = b.sem("mod_summed")
        chain = b.sem("mod_chain")
        diag_ready = b.sem("diag_ready")
        row_up = b.sem("gate_row_up")
        row_out = b.sem("gate_row_out")
        parts = [(d["w_mod"], 9 * D // W, 0, 0), (d["w_ada_2"], 6 * D // W, 9 * D // W, DC)]
        with nc.Block() as block:
            @block.sync
            def _(sp):
                def load(rows, i, j, before):
                    sp.dma_start(w[:, j, :, :], rows[:, :, bass.ds((i * 2 + j) * W, W)]).then_inc(w_in[j], 16)

                for src, n, before, _c in parts:
                    rows = src.rearrange("a (k p) n -> p (a k) n", p=P)
                    if not before:
                        load(rows, 0, 0, before)
                        load(rows, 0, 1, before)
                    with sp.Fori(0 if before else 1, n // 2) as i:
                        for j in range(2):
                            sp.wait_ge(part, (i * 2 + j + before - 1) * DC)
                            load(rows, i, j, before)

            @block.vector
            def _(dve):
                def chunk(i, j, before, c_at):
                    dve.wait_ge(w_in[j], (i + before // 2 + 1) * 16)
                    for k in range(DC):
                        c = b.silu_c[:, c_at + k:c_at + k + 1]
                        if k == 0:
                            ins = nc.vector.tensor_scalar(acc[:, j, :], w[:, j, k, :], c, None, ALU.mult)
                        else:
                            dve.wait_ge(part, (i * 2 + j + before) * DC + k)
                            ins = nc.vector.scalar_tensor_tensor(acc[:, j, :], w[:, j, k, :], c, acc[:, j, :],
                                                                 ALU.mult, ALU.add)
                        ins.then_inc(part, 1)

                for _src, n, before, c_at in parts:
                    if not before:
                        chunk(0, 0, before, c_at)
                        chunk(0, 1, before, c_at)
                    with dve.Fori(0 if before else 1, n // 2) as i:
                        for j in range(2):
                            dve.wait_ge(summed, i * 2 + j + before - 1)
                            chunk(i, j, before, c_at)
                link = Chain(dve, chain)
                dve.wait_ge(summed, NMOD * P // W)
                link(nc.vector.tensor_tensor(b.mod[:, :], b.ps[:, 0, 0:NMOD], b.bias_cols[:, :], ALU.add))
                for n, (name, at) in enumerate((("g_pre_ffn1", 1), ("g_pre_mix", 4), ("g_pre_ffn2", 7),
                                                ("g_norm1_2", 10), ("g_norm2_2", 13))):
                    v = VEC_AT[name]
                    nc.vector.scalar_tensor_tensor(b.scale_cols[:, n, :], b.mod[:, at * DC:(at + 1) * DC], 1.0,
                                                   b.vec[:, v:v + DC], ALU.add, ALU.mult)
                for n, (name, at, half) in enumerate((("g_post_ffn1", 2, 0.5), ("g_post_mix", 5, 1.0),
                                                      ("g_post_ffn2", 8, 0.5))):
                    v = VEC_AT[name]
                    nc.vector.scalar_tensor_tensor(gates[:, n, :], b.mod[:, at * DC:(at + 1) * DC], half,
                                                   b.vec[:, v:v + DC], ALU.mult, ALU.mult)
                v = VEC_AT["g_final_2"]
                nc.vector.tensor_copy(gates[:, 5, :], b.vec[:, v:v + DC])
                nc.vector.tensor_copy(gates[:, 3, :], b.mod[:, 11 * DC:12 * DC])
                link(nc.vector.tensor_copy(gates[:, 4, :], b.mod[:, 14 * DC:15 * DC]))
                ident = b.const("identity").unsqueeze(1).to_broadcast([P, 4, P])
                for n in range(12):
                    if n >= 2:
                        dve.wait_ge(row_up, n - 1)
                    cols = gates[:, n // 2, 4 * (n % 2):4 * (n % 2) + 4].unsqueeze(2).to_broadcast([P, 4, P])
                    nc.vector.tensor_tensor(diag[:, n % 2, :, :], ident, cols, ALU.mult).then_inc(diag_ready, 1)

            @block.tensor
            def _(pe):
                ones = b.const("ones")
                for _src, n, before, _c in parts:
                    with pe.Fori(0, n // 2) as i:
                        for j in range(2):
                            pe.wait_ge(part, (i * 2 + j + before + 1) * DC)
                            for q in range(4):
                                col = (i * 2 + j + before) * 4 + q
                                ins = mm(nc, b.ps[:, 0, bass.ds(col, 1)], acc[:, j, q * P:(q + 1) * P], ones[:, 0:1],
                                         True, True)
                            ins.then_inc(summed, 1)
                for n in range(12):
                    pe.wait_ge(diag_ready, n + 1)
                    if n >= 2:
                        pe.wait_ge(row_out, n - 1)
                    mm(nc, b.ps[:, 1 + n % 2, :], ones, diag[:, n % 2, :, :].rearrange("p a c -> p (a c)"),
                       True, True).then_inc(row_up, 1)

            @block.scalar
            def _(act):
                for n in range(12):
                    act.wait_ge(row_up, n + 1)
                    nc.scalar.activation(b.rows[:, n // 2, (n % 2) * 512:(n % 2) * 512 + 512], b.ps[:, 1 + n % 2, :],
                                         ACT.Copy).then_inc(row_out, 1)


def stage_norm_turn(nc, b, tag, scale_at, shift_at, keep_tokens=None):
    xs = b.tok
    squares = b.sem(f"{tag}_squares")
    rooted = b.sem(f"{tag}_rooted")
    rstd = b.sem(f"{tag}_rstd")
    scaled = b.sem(f"{tag}_scaled")
    turned = b.sem(f"{tag}_turned")
    out_act = b.sem(f"{tag}_out_act")
    out_dve = b.sem(f"{tag}_out_dve")
    back = b.sem(f"{tag}_back")
    with nc.Block() as block:
        @block.scalar
        def _(act):
            for i in range(TT):
                nc.scalar.activation(b.feat[:, 2 * i:2 * i + 2, :].rearrange("p a n -> p (a n)"), b.x[:, i, :],
                                     ACT.Square, accum_out=b.stat[:, i:i + 1]).then_inc(squares, 1)
            root_mean(nc, b, act, b.stat[:, :], D, squares, TT, rooted)
            for k in range(1, DC, 2):
                act.wait_ge(turned, k + 1)
                nc.scalar.activation(b.feat[:, k, :], b.ps[:, k, :], ACT.Identity, scale=b.scale_cols[:, scale_at, k:k + 1],
                                     bias=b.mod[:, shift_at * DC + k:shift_at * DC + k + 1]).then_inc(out_act, 1)
            if keep_tokens is not None:
                for n in range(2 * TT):
                    act.wait_ge(back, n + 1)
                    nc.scalar.activation(keep_tokens[:, n // 2, (n % 2) * 512:(n % 2) * 512 + 512], b.ps[:, n, :], ACT.Copy)

        @block.vector
        def _(dve):
            dve.wait_ge(rooted, 1)
            nc.vector.reciprocal(b.stat[:, :], b.stat[:, :]).then_inc(rstd, 1)
            dve.wait_ge(rstd, 1)
            for i in range(TT):
                nc.vector.tensor_scalar(xs[:, i, :], b.x[:, i, :], b.stat[:, i:i + 1], None, ALU.mult).then_inc(scaled, 1)
            for k in range(0, DC, 2):
                dve.wait_ge(turned, k + 1)
                nc.vector.tensor_scalar(b.feat[:, k, :], b.ps[:, k, :], b.scale_cols[:, scale_at, k:k + 1],
                                        b.mod[:, shift_at * DC + k:shift_at * DC + k + 1], ALU.mult,
                                        ALU.add).then_inc(out_dve, 1)

        @block.tensor
        def _(pe):
            ident = b.const("identity")
            for i in range(TT):
                pe.wait_ge(scaled, i + 1)
                for k in range(DC):
                    ins = nc.tensor.transpose(b.ps[:, k, i * P:(i + 1) * P], xs[:, i, k * P:(k + 1) * P], ident)
                    if i == TT - 1:
                        ins.then_inc(turned, 1)
            if keep_tokens is not None:
                pe.wait_ge(out_act, DC // 2)
                pe.wait_ge(out_dve, DC // 2)
                for n in range(2 * TT):
                    for q in range(4):
                        ins = nc.tensor.transpose(b.ps[:, n, q * P:(q + 1) * P],
                                                  b.feat[:, (n % 2) * 4 + q, (n // 2) * P:(n // 2 + 1) * P], ident)
                    ins.then_inc(back, 1)


def stage_post_norm(nc, b, tag, row):
    squares = b.sem(f"{tag}_squares")
    chain = b.sem(f"{tag}_chain")
    rooted = b.sem(f"{tag}_rooted")
    rstd = b.sem(f"{tag}_rstd")
    with nc.Block() as block:
        @block.scalar
        def _(act):
            for i in range(TT):
                nc.scalar.activation(b.feat[:, 2 * i:2 * i + 2, :].rearrange("p a n -> p (a n)"), b.tok[:, i, :],
                                     ACT.Square, accum_out=b.stat[:, i:i + 1]).then_inc(squares, 1)
            root_mean(nc, b, act, b.stat[:, :], D, squares, TT, rooted)

        @block.vector
        def _(dve):
            link = Chain(dve, chain)
            dve.wait_ge(rooted, 1)
            nc.vector.reciprocal(b.stat[:, :], b.stat[:, :]).then_inc(rstd, 1)
            dve.wait_ge(rstd, 1)
            for i in range(TT):
                link(nc.vector.scalar_tensor_tensor(b.tok[:, i, :], b.tok[:, i, :], b.stat[:, i:i + 1], b.rows[:, row, :],
                                                    ALU.mult, ALU.mult))
                nc.vector.tensor_tensor(b.x[:, i, :], b.x[:, i, :], b.tok[:, i, :], ALU.add)


def stage_swiglu(nc, b, tag, w_gate, w_up, w_down):
    QW = 256
    NQ = D // QW
    wg = w_gate.rearrange("a (k p) n -> p (a k) n", p=P)
    wu = w_up.rearrange("a (k p) n -> p (a k) n", p=P)
    wd = w_down.rearrange("a (k p) n -> p (a k) n", p=P)
    with ExitStack() as own:
        gu = own.enter_context(nc.sbuf_tensor(f"{tag}_gu", [P, FC, S], F32))
        w_gu = own.enter_context(nc.sbuf_tensor(f"{tag}_w_gu", [P, 2, 2, DC, P], F32))
        w_dn = own.enter_context(nc.sbuf_tensor(f"{tag}_w_dn", [P, 2, FC, QW], F32))
        silu = b.tok[:, :, 0:S]
        gu_in = [b.sem(f"{tag}_gu_in{j}") for j in range(2)]
        dn_in = [b.sem(f"{tag}_dn_in{j}") for j in range(2)]
        both_up = b.sem(f"{tag}_both_up")
        silu_done = b.sem(f"{tag}_silu")
        gu_done = b.sem(f"{tag}_gu_done")
        y_up = b.sem(f"{tag}_y_up")
        y_out = b.sem(f"{tag}_y_out")
        with nc.Block() as block:
            @block.sync
            def _(sp):
                for j in range(2):
                    for m, src in enumerate((wg, wu)):
                        sp.dma_start(w_gu[:, j, m, :, :], src[:, :, j * P:(j + 1) * P]).then_inc(gu_in[j], 16)
                for q in range(2):
                    sp.dma_start(w_dn[:, q, :, :], wd[:, :, q * QW:(q + 1) * QW]).then_inc(dn_in[q], 16)
                with sp.Fori(1, FC // 2) as i:
                    for j in range(2):
                        sp.wait_ge(both_up, i * 2 + j - 1)
                        for m, src in enumerate((wg, wu)):
                            sp.dma_start(w_gu[:, j, m, :, :],
                                         src[:, :, bass.ds((i * 2 + j) * P, P)]).then_inc(gu_in[j], 16)
                for q in range(2, NQ):
                    sp.wait_ge(y_up, (q - 1) * TT)
                    sp.dma_start(w_dn[:, q % 2, :, :], wd[:, :, q * QW:(q + 1) * QW]).then_inc(dn_in[q % 2], 16)

            @block.tensor
            def _(pe):
                def chunk(i, j):
                    pe.wait_ge(gu_in[j], (i + 1) * 32)
                    for m in range(2):
                        for k in range(DC):
                            ins = mm(nc, b.ps[:, 2 * j + m, :], w_gu[:, j, m, k, :], b.feat[:, k, :], k == 0, k == DC - 1)
                    ins.then_inc(both_up, 1)

                chunk(0, 0)
                chunk(0, 1)
                with pe.Fori(1, FC // 2) as i:
                    for j in range(2):
                        pe.wait_ge(gu_done, i * 2 + j - 1)
                        chunk(i, j)
                for q in range(NQ):
                    pe.wait_ge(dn_in[q % 2], 16 * (q // 2 + 1))
                    if q == 0:
                        pe.wait_ge(gu_done, FC)
                    for i in range(TT):
                        if q:
                            pe.wait_ge(y_out, (q - 1) * TT + i + 1)
                        for k in range(FC):
                            ins = mm(nc, b.ps[:, 4 + i, 0:QW], gu[:, k, i * P:(i + 1) * P], w_dn[:, q % 2, k, :],
                                     k == 0, k == FC - 1)
                        ins.then_inc(y_up, 1)

            @block.scalar
            def _(act):
                def chunk(i, j):
                    act.wait_ge(both_up, i * 2 + j + 1)
                    nc.scalar.activation(silu[:, j, :], b.ps[:, 2 * j, :], ACT.Silu).then_inc(silu_done, 1)

                chunk(0, 0)
                chunk(0, 1)
                with act.Fori(1, FC // 2) as i:
                    for j in range(2):
                        act.wait_ge(gu_done, i * 2 + j - 1)
                        chunk(i, j)
                act.wait_ge(gu_done, FC)
                for q in range(NQ):
                    for i in range(TT):
                        act.wait_ge(y_up, q * TT + i + 1)
                        nc.scalar.activation(b.tok[:, i, q * QW:(q + 1) * QW], b.ps[:, 4 + i, 0:QW],
                                             ACT.Copy).then_inc(y_out, 1)

            @block.vector
            def _(dve):
                with dve.Fori(0, FC // 2) as i:
                    for j in range(2):
                        dve.wait_ge(silu_done, i * 2 + j + 1)
                        nc.vector.tensor_tensor(gu[:, i * 2 + j, :], silu[:, j, :], b.ps[:, 2 * j + 1, :],
                                                ALU.mult).then_inc(gu_done, 1)


def stage_project(nc, b, tag, jobs, slot_k, slots=2):
    with ExitStack() as own:
        w = own.enter_context(nc.sbuf_tensor(f"{tag}_w", [P, slots, slot_k, 512], F32))
        w_in = [b.sem(f"{tag}_w_in{j}") for j in range(slots)]
        up = b.sem(f"{tag}_up")
        out_act = b.sem(f"{tag}_out_act")
        out_dve = b.sem(f"{tag}_out_dve")
        acts = [i for i in range(TT) if i % 2 == 0]
        with nc.Block() as block:
            @block.sync
            def _(sp):
                for n, (src, nk, _l, _s) in enumerate(jobs):
                    if n >= slots:
                        sp.wait_ge(up, (n - slots + 1) * TT)
                    width = src.shape[-1]
                    sp.dma_start(w[:, n % slots, 0:nk, 0:width],
                                 src.rearrange("(k p) n -> p k n", p=P)).then_inc(w_in[n % slots], 16)

            @block.tensor
            def _(pe):
                for n, (src, nk, lhsT, _s) in enumerate(jobs):
                    width = src.shape[-1]
                    pe.wait_ge(w_in[n % slots], 16 * (n // slots + 1))
                    for i in range(TT):
                        bank = (n % 2) * TT + i
                        if n >= 2:
                            pe.wait_ge(out_act if i in acts else out_dve, (n - 2) * 2 + i // 2 + 1)
                        for k in range(nk):
                            ins = mm(nc, b.ps[:, bank, 0:width], lhsT(k, i), w[:, n % slots, k, 0:width],
                                     k == 0, k == nk - 1)
                        ins.then_inc(up, 1)

            @block.scalar
            def _(act):
                for n, (src, _n, _l, stores) in enumerate(jobs):
                    for i in acts:
                        act.wait_ge(up, n * TT + i + 1)
                        for dst, ps in stores(i, b.ps[:, (n % 2) * TT + i, 0:src.shape[-1]]):
                            ins = nc.scalar.activation(dst, ps, ACT.Copy)
                        ins.then_inc(out_act, 1)

            @block.vector
            def _(dve):
                for n, (src, _n, _l, stores) in enumerate(jobs):
                    for i in range(TT):
                        if i in acts:
                            continue
                        dve.wait_ge(up, n * TT + i + 1)
                        for dst, ps in stores(i, b.ps[:, (n % 2) * TT + i, 0:src.shape[-1]]):
                            ins = nc.vector.tensor_copy(dst, ps)
                        ins.then_inc(out_dve, 1)


def stage_turn(nc, b, tag, jobs):
    NB = 8
    turned = b.sem(f"{tag}_turned")
    out_act = b.sem(f"{tag}_out_act")
    out_dve = b.sem(f"{tag}_out_dve")
    with nc.Block() as block:
        @block.tensor
        def _(pe):
            ident = b.const("identity")
            for n, (src, f, _d, _s) in enumerate(jobs):
                if n >= NB:
                    pe.wait_ge(out_act if n % 2 == 0 else out_dve, (n - NB) // 2 + 1)
                for i in range(TT):
                    ins = nc.tensor.transpose(b.ps[0:f, n % NB, i * P:(i + 1) * P], src(i), ident)
                ins.then_inc(turned, 1)

        @block.scalar
        def _(act):
            for n, (_src, f, dst, scale) in enumerate(jobs):
                if n % 2 == 0:
                    act.wait_ge(turned, n + 1)
                    nc.scalar.activation(dst, b.ps[0:f, n % NB, :], ACT.Copy,
                                         scale=1.0 if scale is None else scale).then_inc(out_act, 1)

        @block.vector
        def _(dve):
            for n, (_src, f, dst, scale) in enumerate(jobs):
                if n % 2:
                    dve.wait_ge(turned, n + 1)
                    if scale is None:
                        ins = nc.vector.tensor_copy(dst, b.ps[0:f, n % NB, :])
                    else:
                        ins = nc.vector.tensor_scalar(dst, b.ps[0:f, n % NB, :], scale, None, ALU.mult)
                    ins.then_inc(out_dve, 1)


def stage_norm_rope(nc, b, tag, norms, ropes, copies=(), decays=()):
    with ExitStack() as own:
        size = 768
        tmp = own.enter_context(nc.sbuf_tensor(f"{tag}_tmp", [P, 4, size], F32))
        stat = own.enter_context(nc.sbuf_tensor(f"{tag}_stat", [P, max(1, len(norms)), TT], F32))
        squares = b.sem(f"{tag}_squares")
        chain = b.sem(f"{tag}_chain")
        first = b.sem(f"{tag}_first_half")
        second = b.sem(f"{tag}_second_half")
        done = b.sem(f"{tag}_rope_done")
        pool_chain = b.sem(f"{tag}_pool_chain")
        rooted = b.sem(f"{tag}_rooted")

        def view(t, like):
            a, c = like.shape[1], like.shape[2]
            return tmp[:, t, 0:a * c].rearrange("p (a c) -> p a c", c=c)

        with nc.Block() as block:
            @block.scalar
            def _(act):
                for n, (t, w) in enumerate(norms):
                    for i in range(TT):
                        nc.scalar.activation(b.ps[:, n * TT + i, 0:w], t(i), ACT.Square,
                                             accum_out=stat[:, n, i:i + 1]).then_inc(squares, 1)
                for n, (t, w) in enumerate(norms):
                    root_mean(nc, b, act, stat[:, n, :], w, squares, TT * len(norms), rooted)

            @block.vector
            def _(dve):
                link = Chain(dve, chain)
                for n, (x1, x2, cos, sin) in enumerate(ropes):
                    link(nc.vector.tensor_tensor(view(0, x1), x1, cos, ALU.mult))
                    nc.vector.tensor_tensor(view(1, x1), x2, sin, ALU.mult).then_inc(first, 1)
                    dve.wait_ge(first, n + 1)
                    dve.wait_ge(second, n + 1)
                    link(nc.vector.tensor_tensor(x1, view(0, x1), view(1, x1), ALU.subtract))
                for n, (t, w) in enumerate(norms):
                    dve.wait_ge(rooted, n + 1)
                    link(nc.vector.reciprocal(stat[:, n, :], stat[:, n, :]))
                    for i in range(TT):
                        nc.vector.tensor_scalar(t(i), t(i), stat[:, n, i:i + 1], None, ALU.mult)
                if copies or decays:
                    dve.wait_ge(done, len(ropes))
                for dst, src in copies:
                    nc.vector.tensor_copy(dst, src)
                for t, factors in decays:
                    nc.vector.tensor_tensor(t, t, factors, ALU.mult)

            @block.gpsimd
            def _(pool):
                link = Chain(pool, pool_chain)
                for n, (x1, x2, cos, sin) in enumerate(ropes):
                    link(nc.gpsimd.tensor_tensor(view(2, x1), x2, cos, ALU.mult))
                    nc.gpsimd.tensor_tensor(view(3, x1), x1, sin, ALU.mult).then_inc(second, 1)
                    pool.wait_ge(first, n + 1)
                    pool.wait_ge(second, n + 1)
                    nc.gpsimd.tensor_tensor(x2, view(2, x1), view(3, x1), ALU.add).then_inc(done, 1)
                    pool.wait_ge(done, n + 1)


def stage_attention(nc, b, tag, items, width, scale):
    N = len(items)
    with ExitStack() as own:
        neg = own.enter_context(nc.sbuf_tensor(f"{tag}_neg", [P, 2, width], F32))
        prob = own.enter_context(nc.sbuf_tensor(f"{tag}_prob", [P, 2, width], F32))
        prob_t = own.enter_context(nc.sbuf_tensor(f"{tag}_prob_t", [P, 2, width], F32))
        neg_max = own.enter_context(nc.sbuf_tensor(f"{tag}_neg_max", [P, N], F32))
        total = own.enter_context(nc.sbuf_tensor(f"{tag}_total", [P, N], F32))
        inverse = own.enter_context(nc.sbuf_tensor(f"{tag}_inverse", [P, N], F32))
        score_up = b.sem(f"{tag}_score_up")
        biased = b.sem(f"{tag}_biased")
        exp_done = b.sem(f"{tag}_exp_done")
        prob_up = b.sem(f"{tag}_prob_turned")
        prob_out = b.sem(f"{tag}_prob_t_out")
        inverted = b.sem(f"{tag}_inverted")
        value_up = b.sem(f"{tag}_value_up")
        value_out = b.sem(f"{tag}_value_out")
        flat = b.ps[:, :, :].rearrange("p k n -> p (k n)")

        def score_ps(n):
            return flat[:, (n % 2) * 1024:(n % 2) * 1024 + 1024]

        turn_ps = flat[:, 2048:3072]

        def value_ps(n):
            return b.ps[:, 6 + n % 2, 0:DV]

        with nc.Block() as block:
            @block.tensor
            def _(pe):
                ident = b.const("identity")

                def scores(n):
                    if n >= 2:
                        pe.wait_ge(biased, n - 1)
                    for col, lhsT, rhs in items[n][0]:
                        ins = mm(nc, score_ps(n)[:, col:col + rhs.shape[-1]], lhsT, rhs, True, True)
                    ins.then_inc(score_up, 1)

                def turn(n):
                    pe.wait_ge(exp_done, n + 1)
                    if n >= 1:
                        pe.wait_ge(prob_out, n)
                    for k in range(items[n][2] // P):
                        ins = nc.tensor.transpose(turn_ps[:, k * P:(k + 1) * P], prob[:, n % 2, k * P:(k + 1) * P], ident)
                    ins.then_inc(prob_up, 1)

                def values(n):
                    pe.wait_ge(prob_out, n + 1)
                    if n >= 2:
                        pe.wait_ge(value_out, n - 1)
                    rhs = items[n][3]
                    for k in range(len(rhs)):
                        ins = mm(nc, value_ps(n), prob_t[:, n % 2, k * P:(k + 1) * P], rhs[k], k == 0, k == len(rhs) - 1)
                    ins.then_inc(value_up, 1)

                for n in range(N + 2):
                    if n < N:
                        scores(n)
                    if 0 <= n - 1 < N:
                        turn(n - 1)
                    if 0 <= n - 2:
                        values(n - 2)

            @block.vector
            def _(dve):
                for n in range(N + 1):
                    if n < N:
                        _p, bias, w, _v, _d = items[n]
                        dve.wait_ge(score_up, n + 1)
                        if n >= 2:
                            dve.wait_ge(exp_done, n - 1)
                        nc.vector.tensor_tensor_reduce(neg[:, n % 2, 0:w], score_ps(n)[:, 0:w], bias, -scale, 3e38,
                                                       ALU.add, ALU.min, neg_max[:, n:n + 1]).then_inc(biased, 1)
                    if n >= 1:
                        m = n - 1
                        dve.wait_ge(exp_done, m + 1)
                        nc.vector.reciprocal(inverse[:, m:m + 1], total[:, m:m + 1]).then_inc(inverted, 1)
                        if m % 2 == 0:
                            w = items[m][2]
                            dve.wait_ge(prob_up, m + 1)
                            if m >= 2:
                                dve.wait_ge(value_up, m - 1)
                            nc.vector.tensor_copy(prob_t[:, m % 2, 0:w], turn_ps[:, 0:w]).then_inc(prob_out, 1)

            @block.scalar
            def _(act):
                for n in range(N + 2):
                    if n < N:
                        w = items[n][2]
                        act.wait_ge(biased, n + 1)
                        if n >= 2:
                            act.wait_ge(prob_up, n - 1)
                        nc.scalar.activation(prob[:, n % 2, 0:w], neg[:, n % 2, 0:w], ACT.Exp, bias=neg_max[:, n:n + 1],
                                             scale=-1.0, accum_out=total[:, n:n + 1]).then_inc(exp_done, 1)
                    m = n - 1
                    if 0 <= m < N and m % 2 == 1:
                        w = items[m][2]
                        act.wait_ge(prob_up, m + 1)
                        if m >= 2:
                            act.wait_ge(value_up, m - 1)
                        nc.scalar.activation(prob_t[:, m % 2, 0:w], turn_ps[:, 0:w], ACT.Copy).then_inc(prob_out, 1)
                    m = n - 2
                    if m >= 0:
                        act.wait_ge(value_up, m + 1)
                        act.wait_ge(inverted, m + 1)
                        nc.scalar.activation(items[m][4], value_ps(m), ACT.Copy,
                                             scale=inverse[:, m:m + 1]).then_inc(value_out, 1)


def stage_select(nc, b, q_idx_t, k_idx_t, w_idx, bias):
    FILL, TAKEN = -1e37, -3e38
    items = [(i, h) for i in range(1, TT) for h in range(HEADS)]
    with ExitStack() as own:
        relu = own.enter_context(nc.sbuf_tensor("idx_relu", [P, 2, S], F32))
        score = own.enter_context(nc.sbuf_tensor("idx_score", [P, TT, S], F32))
        best = own.enter_context(nc.sbuf_tensor("idx_best", [P, 2, 8], F32))
        up = b.sem("idx_up")
        relu_done = b.sem("idx_relu_done")
        added = b.sem("idx_added")
        chain = b.sem("idx_chain")
        with nc.Block() as block:
            @block.tensor
            def _(pe):
                for n, (i, h) in enumerate(items):
                    if n >= 4:
                        pe.wait_ge(relu_done, n - 3)
                    at = 32 * (h % 4)
                    mm(nc, b.ps[:, n % 4, 0:(i + 1) * P], q_idx_t[at:at + 32, h // 4, i * P:(i + 1) * P],
                       k_idx_t[at:at + 32, 0:(i + 1) * P], True, True).then_inc(up, 1)

            @block.scalar
            def _(act):
                for n, (i, h) in enumerate(items):
                    act.wait_ge(up, n + 1)
                    if n >= 2:
                        act.wait_ge(added, n - 1)
                    nc.scalar.activation(relu[:, n % 2, 0:(i + 1) * P], b.ps[:, n % 4, 0:(i + 1) * P], ACT.Relu,
                                         scale=IDX ** -0.5).then_inc(relu_done, 1)

            @block.vector
            def _(dve):
                link = Chain(dve, chain)
                causal = b.const("causal_bias")
                for n, (i, h) in enumerate(items):
                    w = (i + 1) * P
                    dve.wait_ge(relu_done, n + 1)
                    if h:
                        dve.wait_ge(added, n)
                        ins = nc.vector.scalar_tensor_tensor(score[:, i, 0:w], relu[:, n % 2, 0:w], w_idx(i, h),
                                                             score[:, i, 0:w], ALU.mult, ALU.add)
                    else:
                        ins = nc.vector.tensor_scalar(score[:, i, 0:w], relu[:, n % 2, 0:w], w_idx(i, h), None, ALU.mult)
                    ins.then_inc(added, 1)
                dve.wait_ge(added, len(items))
                nc.vector.tensor_copy(bias[:, 0, 0:P], causal)
                for i in range(1, TT):
                    link(nc.vector.scalar_tensor_tensor(score[:, i, i * P:(i + 1) * P], causal, FILL / NEG,
                                                        score[:, i, i * P:(i + 1) * P], ALU.mult, ALU.add))
                for r in range(TOPK // 8):
                    for i in range(1, TT):
                        w = (i + 1) * P
                        link(nc.vector.max(best[:, r % 2, :], score[:, i, 0:w]))
                        link(nc.vector.match_replace(score[:, i, 0:w], best[:, r % 2, :], score[:, i, 0:w], TAKEN))
                for i in range(1, TT):
                    w = (i + 1) * P
                    nc.vector.tensor_scalar(bias[:, i, 0:w], score[:, i, 0:w], -2e38, NEG, ALU.is_gt, ALU.mult)


def stage_gated_up(nc, b, d, a_t, b_t, z_t):
    w_in_v = d["w_in"].rearrange("a (k p) n -> p (a k) n", p=P)
    up_a = d["w_up_a"].rearrange("a (k p) n -> p (a k) n", p=P)
    up_b = d["w_up_b"].rearrange("a (k p) n -> p (a k) n", p=P)
    KA, KB = a_t.shape[1], b_t.shape[1]
    with ExitStack() as own:
        w_g = own.enter_context(nc.sbuf_tensor("gate_w", [P, 2, 2, DC, P], F32))
        w_u = own.enter_context(nc.sbuf_tensor("branch_w", [P, 2, KA + KB, P], F32))
        sig = own.enter_context(nc.sbuf_tensor("gate_sig", [P, 2, 2, S], F32))
        part = own.enter_context(nc.sbuf_tensor("gated_part", [P, 2, 2, S], F32))
        w_in = [b.sem(f"gated_w_in{j}") for j in range(2)]
        up = b.sem("gated_up")
        sig_done = b.sem("gated_sig")
        read = b.sem("gated_read")
        z_done = b.sem("gated_z")
        with nc.Block() as block:
            @block.sync
            def _(sp):
                for m in range(DC):
                    j = m % 2
                    if m >= 2:
                        sp.wait_ge(up, m - 1)
                    for g in range(2):
                        at = C_GATE + g * D + m * P
                        sp.dma_start(w_g[:, j, g, :, :], w_in_v[:, :, at:at + P]).then_inc(w_in[j], 16)
                    sp.dma_start(w_u[:, j, 0:KA, :], up_a[:, :, m * P:(m + 1) * P]).then_inc(w_in[j], 16)
                    sp.dma_start(w_u[:, j, KA:KA + KB, :], up_b[:, :, m * P:(m + 1) * P]).then_inc(w_in[j], 16)

            @block.tensor
            def _(pe):
                for m in range(DC):
                    j = m % 2
                    pe.wait_ge(w_in[j], 64 * (m // 2 + 1))
                    if m >= 2:
                        pe.wait_ge(read, 2 * (m - 1))
                    for g in range(2):
                        for k in range(DC):
                            mm(nc, b.ps[:, 4 * j + g, :], w_g[:, j, g, k, :], b.feat[:, k, :], k == 0, k == DC - 1)
                    for k in range(KA):
                        mm(nc, b.ps[:, 4 * j + 2, :], w_u[:, j, k, :], a_t[:, k, :], k == 0, k == KA - 1)
                    for k in range(KB):
                        ins = mm(nc, b.ps[:, 4 * j + 3, :], w_u[:, j, KA + k, :], b_t[:, k, :], k == 0, k == KB - 1)
                    ins.then_inc(up, 1)

            @block.scalar
            def _(act):
                for m in range(DC):
                    j = m % 2
                    act.wait_ge(up, m + 1)
                    if m >= 2:
                        act.wait_ge(read, 2 * (m - 1))
                    nc.scalar.activation(sig[:, j, :, :], b.ps[:, 4 * j:4 * j + 2, :], ACT.Sigmoid).then_inc(sig_done, 1)

            @block.vector
            def _(dve):
                for m in range(DC):
                    j = m % 2
                    dve.wait_ge(sig_done, m + 1)
                    if m >= 2:
                        dve.wait_ge(z_done, m - 1)
                    for g in range(2):
                        nc.vector.tensor_tensor(part[:, j, g, :], sig[:, j, g, :], b.ps[:, 4 * j + 2 + g, :],
                                                ALU.mult).then_inc(read, 1)

            @block.gpsimd
            def _(pool):
                for m in range(DC):
                    j = m % 2
                    pool.wait_ge(read, 2 * (m + 1))
                    nc.gpsimd.tensor_tensor(z_t[:, m, :], part[:, j, 0, :], part[:, j, 1, :], ALU.add).then_inc(z_done, 1)


def stage_retention(nc, b, q_t, k_t, v, y):
    with ExitStack() as own:
        kept = own.enter_context(nc.sbuf_tensor("ret_scores", [P, 2, TT, S], F32))
        up = b.sem("ret_up")
        out = b.sem("ret_out")
        y_up = b.sem("ret_y_up")
        y_out = b.sem("ret_y_out")
        mask = b.const("decay_mask")
        with nc.Block() as block:
            @block.tensor
            def _(pe):
                def scores(h):
                    at = DH * (h % 2)
                    for j in range(TT):
                        n = h * TT + j
                        if n >= 4:
                            pe.wait_ge(out, n - 3)
                        w = S - j * P
                        mm(nc, b.ps[:, j, 0:w], k_t[at:at + DH, h // 2, j * P:(j + 1) * P],
                           q_t[at:at + DH, h // 2, j * P:S], True, True).then_inc(up, 1)

                def sums(h):
                    pe.wait_ge(out, (h + 1) * TT)
                    if h >= 2:
                        pe.wait_ge(y_out, h - 1)
                    for i in range(TT):
                        for j in range(i + 1):
                            ins = mm(nc, b.ps[:, 4 + h % 2, i * DH:(i + 1) * DH],
                                     kept[:, h % 2, j, (i - j) * P:(i - j + 1) * P], v[:, j, h * DH:(h + 1) * DH],
                                     j == 0, j == i)
                    ins.then_inc(y_up, 1)

                for h in range(HEADS + 1):
                    if h < HEADS:
                        scores(h)
                    if h:
                        sums(h - 1)

            @block.vector
            def _(dve):
                for h in range(HEADS):
                    if h >= 2:
                        dve.wait_ge(y_up, h - 1)
                    for j in range(TT):
                        w = S - j * P
                        dve.wait_ge(up, h * TT + j + 1)
                        nc.vector.tensor_tensor(kept[:, h % 2, j, 0:w], b.ps[:, j, 0:w], mask[:, 0:w],
                                                ALU.mult).then_inc(out, 1)

            @block.scalar
            def _(act):
                for h in range(HEADS):
                    act.wait_ge(y_up, h + 1)
                    nc.scalar.activation(y[:, :, h * DH:(h + 1) * DH],
                                         b.ps[:, 4 + h % 2, 0:TT * DH].rearrange("p (i c) -> p i c", c=DH),
                                         ACT.Copy).then_inc(y_out, 1)


def stage_retention_norm(nc, b, y, gate):
    with ExitStack() as own:
        sq = b.tok
        mean = own.enter_context(nc.sbuf_tensor("ret_mean", [P, TT * HEADS], F32))
        var = own.enter_context(nc.sbuf_tensor("ret_var", [P, TT * HEADS], F32))
        chain = b.sem("ret_norm_chain")
        silu_done = b.sem("ret_silu")
        squares = b.sem("ret_squares")
        rooted = b.sem("ret_rooted")
        y3 = y[:, :, :].rearrange("p i (h c) -> p (i h) c", c=DH)
        s3 = sq[:, :, 0:RW].rearrange("p i (h c) -> p i h c", c=DH)
        y4 = y[:, :, :].rearrange("p i (h c) -> p i h c", c=DH)
        full = [P, TT * HEADS, DH]
        with nc.Block() as block:
            @block.scalar
            def _(act):
                nc.scalar.activation(gate, gate, ACT.Silu).then_inc(silu_done, 1)
                root_mean(nc, b, act, mean[:, :], DH, squares, 1, rooted)

            @block.vector
            def _(dve):
                link = Chain(dve, chain)
                link(nc.vector.tensor_reduce(mean[:, :], y3, AX.X, ALU.add))
                link(nc.vector.tensor_scalar(mean[:, :], mean[:, :], 1.0 / DH, None, ALU.mult))
                link(nc.vector.tensor_tensor(y3, y3, mean[:, :].unsqueeze(2).to_broadcast(full), ALU.subtract))
                link(nc.vector.tensor_tensor(s3, y4, y4, ALU.mult))
                link(nc.vector.tensor_reduce(var[:, :].rearrange("p (i h) -> p i h", h=HEADS), s3, AX.X, ALU.add))
                nc.vector.tensor_copy(mean[:, :], var[:, :]).then_inc(squares, 1)
                dve.wait_ge(rooted, 1)
                link(nc.vector.reciprocal(mean[:, :], mean[:, :]))
                link(nc.vector.tensor_tensor(y3, y3, mean[:, :].unsqueeze(2).to_broadcast(full), ALU.mult))
                dve.wait_ge(silu_done, 1)
                link(nc.vector.tensor_tensor(gate, gate, y[:, :, :], ALU.mult))


def stage_key_scores(nc, b, d, q_t, s):
    G = 2 * PH
    with ExitStack() as own:
        keys = own.enter_context(nc.sbuf_tensor("peer_keys", [NKEY, 2, KH], F32))
        keys_t = own.enter_context(nc.sbuf_tensor("peer_keys_t", [KH, 2, NKEY], F32))
        keys_in = b.sem("peer_keys_in")
        keys_up = b.sem("peer_keys_up")
        keys_out = b.sem("peer_keys_out")
        s_up = b.sem("peer_s_up")
        s_out = b.sem("peer_s_out")
        with nc.Block() as block:
            @block.sync
            def _(sp):
                sp.dma_start(keys[:, :, :], d["sub_keys_2"].rearrange("a g k c -> k (a g) c")).then_inc(keys_in, 16)

            @block.tensor
            def _(pe):
                pe.wait_ge(keys_in, 16)
                for g in range(2):
                    ins = nc.tensor.transpose(b.ps[:, 0, g * P:(g + 1) * P], keys[:, g, :], b.const("identity"))
                ins.then_inc(keys_up, 1)
                pe.wait_ge(keys_out, 1)
                for n in range(4 * TT):
                    if n >= 4:
                        pe.wait_ge(s_out, n - 3)
                    i, q = n // 4, n % 4
                    for g in range(4 * q, 4 * q + 4):
                        ins = mm(nc, b.ps[:, 4 + q, (g % 4) * P:(g % 4 + 1) * P], q_t[:, g, i * P:(i + 1) * P],
                                 keys_t[:, g % 2, :], True, True)
                    ins.then_inc(s_up, 1)

            @block.scalar
            def _(act):
                act.wait_ge(keys_up, 1)
                nc.scalar.activation(keys_t[:, :, :].rearrange("p g k -> p (g k)"), b.ps[:, 0, 0:2 * P],
                                     ACT.Copy).then_inc(keys_out, 1)
                for n in range(4 * TT):
                    i, q = n // 4, n % 4
                    act.wait_ge(s_up, n + 1)
                    nc.scalar.activation(s[:, i, 4 * q:4 * q + 4, :].rearrange("p g k -> p (g k)"),
                                         b.ps[:, 4 + q, :], ACT.Copy).then_inc(s_out, 1)


def stage_experts(nc, b, d, s):
    G = 2 * PH
    R = 8
    NE = PH * PK
    STEPS = NE // R
    u_rows = d["expert_u_2"].rearrange("a e n -> (a e) n")
    v_rows = d["expert_v_2"].rearrange("a e n -> (a e) n")
    h2 = b.tok
    with ExitStack() as own:
        def sb(name, shape, dt=F32):
            return own.enter_context(nc.sbuf_tensor(name, shape, dt))

        expert = sb("expert", [P, TT, NE], U32)
        weight = sb("expert_weight", [P, TT, NE])
        top = sb("peer_top", [P, G, PK])
        top_i = sb("peer_top_i", [P, G, PK], U32)
        top_f = sb("peer_top_f", [P, G, PK])
        cand = sb("peer_cand", [P, PH, PK, PK])
        hot = cand
        best = sb("peer_best", [P, PH, PK])
        pos = sb("peer_pos", [P, PH, PK], U32)
        part_i = sb("peer_part_i", [P, 2, PH, PK], U32)
        part_f = sb("peer_part_f", [P, 2, PH, PK])
        chosen = sb("peer_chosen", [P, 2, PH, PK])
        sums = sb("peer_sums", [P, 2 * PH])
        u = sb("u_rows", [P, R, D])
        v = sb("v_rows", [P, R, D])
        dots = sb("peer_dots", [P, NE])
        dot_cells = sb("peer_dot_cells", [P, R])
        act_w = sb("peer_act_w", [P, 2, NE])
        diag = sb("peer_diag", [P, 4, P])
        u_in = [b.sem(f"u_in{r}") for r in range(R)]
        v_in = [b.sem(f"v_in{r}") for r in range(R)]
        chain = b.sem("peer_route_chain")
        routed = b.sem("peer_routed")
        dot_done = b.sem("dot_done")
        dots_kept = b.sem("dots_kept")
        gelu_done = b.sem("gelu_done")
        act_w_done = b.sem("act_w_done")
        diag_done = b.sem("diag_done")
        v_used = b.sem("v_used")
        y_out = b.sem("peer_y_out")
        with nc.Block() as block:
            @block.gpsimd
            def _(pool):
                def gather(i, k, rows, table, arrived, used):
                    r = k % R
                    if i * NE + k >= R:
                        pool.wait_ge(used, i * NE + k - R + 1)
                    nc.gpsimd.indirect_dma_start(
                        out=rows[:, r, :], out_offset=None, in_=table,
                        in_offset=bass.IndirectOffsetOnAxis(ap=expert[:, i, k:k + 1], axis=0),
                    ).then_inc(arrived[r], 16)

                for i in range(-1, TT):
                    if i + 1 < TT:
                        pool.wait_ge(routed, i + 2)
                    for k in range(NE):
                        if i + 1 < TT:
                            gather(i + 1, k, u, u_rows, u_in, dot_done)
                        if i >= 0:
                            gather(i, k, v, v_rows, v_in, v_used)

            @block.vector
            def _(dve):
                link = Chain(dve, chain)

                def best_keys(i):
                    for half in range(2):
                        at = slice(8 * half, 8 * half + 8)
                        for g in range(G):
                            ins = nc.vector.max(top[:, g, at], s[:, i, g, :])
                        link(ins)
                        for g in range(G):
                            ins = nc.vector.max_index(top_i[:, g, at], top[:, g, at], s[:, i, g, :])
                        link(ins)
                        if half == 0:
                            for g in range(G):
                                ins = nc.vector.match_replace(s[:, i, g, :], top[:, g, at], s[:, i, g, :], -3e38)
                            link(ins)
                    link(nc.vector.tensor_copy(top_f[:, :, :], top_i[:, :, :]))

                def best_pairs(i):
                    for h in range(PH):
                        a = top[:, 2 * h, :].unsqueeze(2).to_broadcast([P, PK, PK])
                        c = top[:, 2 * h + 1, :].unsqueeze(1).to_broadcast([P, PK, PK])
                        ins = nc.vector.tensor_tensor(cand[:, h, :, :], a, c, ALU.add)
                    link(ins)
                    rows = [cand[:, h, :, :].rearrange("p a c -> p (a c)") for h in range(PH)]
                    for half in range(2):
                        at = slice(8 * half, 8 * half + 8)
                        for h in range(PH):
                            ins = nc.vector.max(best[:, h, at], rows[h])
                        link(ins)
                        for h in range(PH):
                            ins = nc.vector.max_index(pos[:, h, at], best[:, h, at], rows[h])
                        link(ins)
                        if half == 0:
                            for h in range(PH):
                                ins = nc.vector.match_replace(rows[h], best[:, h, at], rows[h], -3e38)
                            link(ins)
                    nc.vector.tensor_scalar(part_i[:, 0, :, :], pos[:, :, :], 4, None, ALU.logical_shift_right)
                    link(nc.vector.tensor_scalar(part_i[:, 1, :, :], pos[:, :, :], PK - 1, None, ALU.bitwise_and))
                    link(nc.vector.tensor_copy(part_f[:, :, :, :], part_i[:, :, :, :]))
                    iota = b.const("iota").unsqueeze(1).to_broadcast([P, PH * PK, PK])
                    hot3 = hot[:, :, :, :].rearrange("p h k c -> p (h k) c")
                    for g in range(2):
                        rank = part_f[:, g, :, :].rearrange("p h k -> p (h k)").unsqueeze(2).to_broadcast([P, PH * PK, PK])
                        link(nc.vector.tensor_tensor(hot3, rank, iota, ALU.is_equal))
                        key = top_f[:, g:G:2, :].unsqueeze(2).to_broadcast([P, PH, PK, PK])
                        link(nc.vector.tensor_tensor(hot[:, :, :, :], hot[:, :, :, :], key, ALU.mult))
                        link(nc.vector.tensor_reduce(chosen[:, g, :, :].rearrange("p h k -> p (h k)"), hot3, AX.X, ALU.add))
                    c0 = chosen[:, 0, :, :].rearrange("p h k -> p (h k)")
                    c1 = chosen[:, 1, :, :].rearrange("p h k -> p (h k)")
                    nc.vector.scalar_tensor_tensor(expert[:, i, :], c0, float(NKEY), c1, ALU.mult, ALU.add)
                    w3 = weight[:, i, :].rearrange("p (h k) -> p h k", k=PK)
                    nc.vector.tensor_tensor(w3, best[:, :, :], best[:, :, 0:1].to_broadcast([P, PH, PK]),
                                            ALU.subtract).then_inc(routed, 1)
                    dve.wait_ge(routed, i + 1)

                def dot_steps(i, first, last):
                    with dve.Fori(first, last) as t:
                        for r in range(R):
                            dve.wait_ge(u_in[r], (t + i * STEPS + 1) * 16)
                            nc.vector.tensor_tensor_reduce(u[:, r, :], u[:, r, :], h2[:, i, :], 1.0, 0.0, ALU.mult,
                                                           ALU.add, dot_cells[:, r:r + 1]).then_inc(dot_done, 1)
                        dve.wait_ge(dot_done, (t + i * STEPS + 1) * R)
                        nc.vector.tensor_copy(dots[:, bass.ds(t * R, R)], dot_cells[:, :]).then_inc(dots_kept, 1)
                        dve.wait_ge(dots_kept, t + i * STEPS + 1)

                def row_weights(i):
                    w3 = weight[:, i, :].rearrange("p (h k) -> p h k", k=PK)
                    dve.wait_ge(gelu_done, 2 * (i + 1))
                    link(nc.vector.tensor_reduce(sums[:, 0:PH], w3, AX.X, ALU.add))
                    link(nc.vector.reciprocal(sums[:, PH:2 * PH], sums[:, 0:PH]))
                    link(nc.vector.tensor_tensor(w3, w3, sums[:, PH:2 * PH].unsqueeze(2).to_broadcast([P, PH, PK]),
                                                 ALU.mult))
                    nc.vector.tensor_tensor(act_w[:, i % 2, :], act_w[:, i % 2, :], weight[:, i, :],
                                            ALU.mult).then_inc(act_w_done, 1)

                for i in range(2):
                    best_keys(i)
                    best_pairs(i)
                for i in range(TT):
                    dot_steps(i, 0, STEPS // 3)
                    if i + 2 < TT:
                        best_keys(i + 2)
                    dot_steps(i, STEPS // 3, 2 * STEPS // 3)
                    if i + 2 < TT:
                        best_pairs(i + 2)
                    dot_steps(i, 2 * STEPS // 3, STEPS)
                    row_weights(i)

            @block.scalar
            def _(act):
                def diagonals(i, t, g):
                    for r in range(2 * g, 2 * g + 2):
                        nc.scalar.activation(diag[:, r, :], b.const("identity"), ACT.Copy,
                                             scale=act_w[:, i % 2, bass.ds(t * 4 + r, 1)]).then_inc(diag_done, 1)

                for i in range(TT):
                    act.wait_ge(dots_kept, (i + 1) * STEPS)
                    nc.scalar.activation(act_w[:, i % 2, :], dots[:, :], ACT.Gelu).then_inc(gelu_done, 1)
                    nc.scalar.activation(weight[:, i, :], weight[:, i, :], ACT.Exp).then_inc(gelu_done, 1)
                    act.wait_ge(act_w_done, i + 1)
                    if i == 0:
                        diagonals(0, 0, 0)
                        diagonals(0, 0, 1)
                    with act.Fori(0 if i else 1, NE // 4) as t:
                        for g in range(2):
                            act.wait_ge(v_used, t * 4 + 2 * g + i * NE - 2)
                            diagonals(i, t, g)
                    act.wait_ge(v_used, (i + 1) * NE)
                    for half in range(2):
                        ins = nc.scalar.activation(b.tok[:, i, half * 512:half * 512 + 512],
                                                   b.ps[:, 2 * (i % 2) + half, :], ACT.Copy)
                    ins.then_inc(y_out, 1)

            @block.tensor
            def _(pe):
                def rows(t, r, i, start, stop):
                    pe.wait_ge(v_in[r], (t + i * STEPS + 1) * 16)
                    pe.wait_ge(diag_done, t * R + r + i * NE + 1)
                    for half in range(2):
                        ins = mm(nc, b.ps[:, 2 * (i % 2) + half, :], diag[:, r % 4, :],
                                 v[:, r, half * 512:half * 512 + 512], start, stop)
                    ins.then_inc(v_used, 1)

                for i in range(TT):
                    if i >= 2:
                        pe.wait_ge(y_out, i - 1)
                    for r in range(R):
                        rows(0, r, i, r == 0, False)
                    with pe.Fori(1, STEPS - 1) as t:
                        for r in range(R):
                            rows(t, r, i, False, False)
                    for r in range(R):
                        rows(STEPS - 1, r, i, False, r == R - 1)


def stage_output(nc, b, tag, w_src, nk, lhsT, row=None):
    with ExitStack() as own:
        w = own.enter_context(nc.sbuf_tensor(f"{tag}_w", [P, nk, D], F32))
        w_in = [b.sem(f"{tag}_w_in{j}") for j in range(2)]
        up = b.sem(f"{tag}_up")
        out = b.sem(f"{tag}_out")
        src = w_src.rearrange("(k p) n -> p k n", p=P)
        with nc.Block() as block:
            @block.sync
            def _(sp):
                for j in range(2):
                    at = slice(j * 512, j * 512 + 512)
                    sp.dma_start(w[:, :, at], src[:, :, at]).then_inc(w_in[j], 16)

            @block.tensor
            def _(pe):
                for j in range(2):
                    pe.wait_ge(w_in[j], 16)
                    for i in range(TT):
                        for k in range(nk):
                            ins = mm(nc, b.ps[:, j * TT + i, :], lhsT(k, i), w[:, k, j * 512:j * 512 + 512],
                                     k == 0, k == nk - 1)
                        ins.then_inc(up, 1)

            @block.vector
            def _(dve):
                for j in range(2):
                    for i in range(TT):
                        at = slice(j * 512, j * 512 + 512)
                        dve.wait_ge(up, j * TT + i + 1)
                        if row is None:
                            nc.vector.tensor_copy(b.tok[:, i, at], b.ps[:, j * TT + i, :])
                            continue
                        nc.vector.tensor_tensor(b.tok[:, i, at], b.ps[:, j * TT + i, :], b.rows[:, row, at],
                                                ALU.mult).then_inc(out, 1)
                        dve.wait_ge(out, j * TT + i + 1)
                        nc.vector.tensor_tensor(b.x[:, i, at], b.x[:, i, at], b.tok[:, i, at], ALU.add)


def stage_final(nc, b, out):
    added = b.sem("final_added")
    squares = b.sem("final_squares")
    chain = b.sem("final_chain")
    ready = b.sem("final_ready")
    rooted = b.sem("final_rooted")
    rstd = b.sem("final_rstd")
    stored = b.sem("final_stored")
    dst = out.rearrange("a (i p) n -> p (a i) n", p=P)
    with nc.Block() as block:
        @block.vector
        def _(dve):
            link = Chain(dve, chain)
            for i in range(TT):
                link(nc.vector.tensor_tensor(b.tok[:, i, :], b.tok[:, i, :], b.rows[:, 4, :], ALU.mult))
                nc.vector.tensor_tensor(b.x[:, i, :], b.x[:, i, :], b.tok[:, i, :], ALU.add).then_inc(added, 1)
            dve.wait_ge(rooted, 1)
            nc.vector.reciprocal(b.stat[:, :], b.stat[:, :]).then_inc(rstd, 1)
            dve.wait_ge(rstd, 1)
            for i in range(TT):
                nc.vector.scalar_tensor_tensor(b.tok[:, i, :], b.x[:, i, :], b.stat[:, i:i + 1], b.rows[:, 5, :],
                                               ALU.mult, ALU.mult).then_inc(ready, 1)

        @block.scalar
        def _(act):
            for i in range(TT):
                act.wait_ge(added, i + 1)
                nc.scalar.activation(b.feat[:, 2 * i:2 * i + 2, :].rearrange("p a n -> p (a n)"), b.x[:, i, :],
                                     ACT.Square, accum_out=b.stat[:, i:i + 1]).then_inc(squares, 1)
            root_mean(nc, b, act, b.stat[:, :], D, squares, TT, rooted)

        @block.sync
        def _(sp):
            for i in range(TT):
                sp.wait_ge(ready, i + 1)
                sp.dma_start(dst[:, i, :], b.tok[:, i, :]).then_inc(stored, 16)
            sp.wait_ge(stored, 16 * TT)


def cols3(t, i, c0, heads, width):
    return t[:, i, c0:c0 + heads * width].rearrange("p (h c) -> p h c", c=width)


def rope_items(b, t, heads, width, at, half, table, pos):
    out = []
    for i in range(TT):
        v = t[:, i, :].rearrange("p (h c) -> p h c", c=width)
        cos = b.cos[:, pos * TT + i, table:table + half].unsqueeze(1).to_broadcast([P, heads, half])
        sin = b.sin[:, pos * TT + i, table:table + half].unsqueeze(1).to_broadcast([P, heads, half])
        out.append((v[:, :, at:at + half], v[:, :, at + half:at + 2 * half], cos, sin))
    return out


def mixer_one(nc, b, d):
    w_in = d["w_in"].rearrange("a k n -> (a k) n")
    HQ = GRP * HB
    with ExitStack() as mix:
        lat = mix.enter_context(nc.sbuf_tensor("latents", [P, TT, C_QKV], F32))
        ob_t = mix.enter_context(nc.sbuf_tensor("ob_t", [P, 2, S], F32))
        oa_t = mix.enter_context(nc.sbuf_tensor("oa_t", [P, 4, S], F32))
        with ExitStack() as dil:
            qk = dil.enter_context(nc.sbuf_tensor("dil_qk", [P, TT, 2 * HQ * DH], F32))
            v = dil.enter_context(nc.sbuf_tensor("dil_v", [P, TT, HQ * DH], F32))

            def plain(k, i):
                return b.feat[:, k, i * P:(i + 1) * P]

            def strided(k, r):
                return b.feat[:, k, r:S:TT]

            jobs = []
            for at, w in ((0, 512), (512, C_QKV - 512)):
                jobs.append((w_in[:, at:at + w], DC, plain, lambda i, ps, at=at, w=w: [(lat[:, i, at:at + w], ps)]))
            for n in range(3):
                at = C_QKV + 512 * n
                jobs.append((w_in[:, at:at + 512], DC, plain,
                             lambda i, ps, n=n: [(qk[:, i, 512 * n:512 * n + 512], ps)]))
            for n in range(2):
                at = C_QKV + 2 * HQ * DH + 384 * n
                jobs.append((w_in[:, at:at + 384], DC, strided,
                             lambda i, ps, n=n: [(v[:, i, 384 * n:384 * n + 384], ps)]))
            stage_project(nc, b, "in1", jobs, DC)

            ropes = []
            ropes += rope_items(b, qk, 2 * HQ, DH, 0, DH // 2, ROPE_A // 2, 0)
            ropes += rope_items(b, lat[:, :, C_KR:C_KR + ROPE_A], 1, ROPE_A, 0, ROPE_A // 2, 0, 0)
            ropes += rope_items(b, lat[:, :, C_KI:C_KI + IDX], 1, IDX, 0, IDX // 2, 0, 0)
            norms = [(lambda i: lat[:, i, 0:QL], QL), (lambda i: lat[:, i, C_CKV:C_CKV + KVL], KVL)]
            stage_norm_rope(nc, b, "nr1", norms, ropes)

            with ExitStack() as att:
                qk_t = att.enter_context(nc.sbuf_tensor("dil_qk_t", [P, HQ, S], F32))
                bias = att.enter_context(nc.sbuf_tensor("dil_bias", [P, TT, S + 2 * P], F32))
                o = att.enter_context(nc.sbuf_tensor("dil_o", [P, TT, HB * DH], F32))
                bias_in = b.sem("dil_bias_in")
                with nc.Block() as block:
                    @block.sync
                    def _(sp):
                        sp.dma_start(bias[:, :, :], d["dilated_bias"].rearrange("p (r n) -> p r n", r=TT)).then_inc(bias_in, 16)
                        sp.wait_ge(bias_in, 16)
                stage_turn(nc, b, "dqk", [(lambda i, n=n: qk[:, i, n * P:(n + 1) * P], P, qk_t[:, n, :], None)
                                          for n in range(HQ)])
                items = []
                for r in range(TT):
                    for h in range(HB):
                        prods, vals = [], []
                        for g in range(GRP):
                            hq = g * HB + h
                            at = DH * (hq % 2)
                            q = qk_t[at:at + DH, hq // 2, r:S:TT]
                            kc = (HQ + hq) // 2
                            if g == 0:
                                for r2 in range(TT):
                                    prods.append((r2 * P, q, qk_t[at:at + DH, kc, r2:S:TT]))
                                    vals.append(v[:, r2, hq * DH:(hq + 1) * DH])
                            else:
                                prods.append((S + (g - 1) * P, q, qk_t[at:at + DH, kc, r:S:TT]))
                                vals.append(v[:, r, hq * DH:(hq + 1) * DH])
                        items.append((prods, bias[:, r, :], S + 2 * P, vals, o[:, r, h * DH:(h + 1) * DH]))
                stage_attention(nc, b, "dil", items, S + 2 * P, DH ** -0.5)
                with nc.Block() as block:
                    o_up = b.sem("dil_o_up")

                    @block.tensor
                    def _(pe):
                        for k in range(2):
                            for r in range(TT):
                                ins = nc.tensor.transpose(b.ps[:, k, r * P:(r + 1) * P], o[:, r, k * P:(k + 1) * P],
                                                          b.const("identity"))
                            ins.then_inc(o_up, 1)

                    @block.vector
                    def _(dve):
                        for k in range(2):
                            dve.wait_ge(o_up, k + 1)
                            nc.vector.tensor_copy(ob_t[:, k, :].rearrange("p (n r) -> p r n", r=TT),
                                                  b.ps[:, k, :].rearrange("p (r n) -> p r n", r=TT))

        with ExitStack() as dsa:
            q_t = dsa.enter_context(nc.sbuf_tensor("dsa_q_t", [DQ, HEADS, S], F32))
            k_t = dsa.enter_context(nc.sbuf_tensor("dsa_k_t", [DQ, HEADS, S], F32))
            v = dsa.enter_context(nc.sbuf_tensor("dsa_v", [P, TT, HEADS * DV], F32))
            qi_t = dsa.enter_context(nc.sbuf_tensor("idx_q_t", [P, 2, S], F32))
            ki_t = dsa.enter_context(nc.sbuf_tensor("idx_k_t", [P, S], F32))
            with ExitStack() as prep:
                lat_t = prep.enter_context(nc.sbuf_tensor("lat_t", [P, 5, S], F32))
                q = prep.enter_context(nc.sbuf_tensor("dsa_q", [P, TT, HEADS * DQ], F32))
                kk = prep.enter_context(nc.sbuf_tensor("dsa_k", [P, TT, HEADS * DQ], F32))
                qi = prep.enter_context(nc.sbuf_tensor("idx_q", [P, TT, HEADS * IDX], F32))
                ki = prep.enter_context(nc.sbuf_tensor("idx_k", [P, TT, P], F32))
                gq, gkv = VEC_AT["g_cq"], VEC_AT["g_ckv"]
                jobs = [(lambda i, n=n: lat[:, i, n * P:(n + 1) * P], P, lat_t[:, n, :],
                         b.vec[:, gq + n:gq + n + 1] if n < 3 else b.vec[:, gkv + n - 3:gkv + n - 2]) for n in range(5)]
                stage_turn(nc, b, "lat1", jobs)
                w_uq = d["w_uq"].rearrange("a k h c -> (a k) (h c)")
                w_uk = d["w_uk"].rearrange("a k h c -> (a k) (h c)")
                w_uv = d["w_uv"].rearrange("a k h c -> (a k) (h c)")
                w_iq = d["w_iq"].rearrange("a k h c -> (a k) (h c)")

                def from_q(k, i):
                    return lat_t[:, k, i * P:(i + 1) * P]

                def from_kv(k, i):
                    return lat_t[:, 3 + k, i * P:(i + 1) * P]

                jobs = [(w_uq[:, n * 384:n * 384 + 384], 3, from_q,
                         lambda i, ps, n=n: [(q[:, i, n * 384:n * 384 + 384], ps)]) for n in range(2)]
                jobs.append((w_iq, 3, from_q, lambda i, ps: [(qi[:, i, :], ps)]))
                jobs.append((w_uk, 2, from_kv,
                             lambda i, ps: [(cols3(kk, i, 0, HEADS, DQ)[:, :, 0:NOPE],
                                             ps.rearrange("p (h c) -> p h c", c=NOPE))]))
                jobs.append((w_uv, 2, from_kv, lambda i, ps: [(v[:, i, :], ps)]))
                stage_project(nc, b, "uq1", jobs, 3)
                ropes = rope_items(b, q, HEADS, DQ, NOPE, ROPE_A // 2, 0, 0)
                ropes += rope_items(b, qi, HEADS, IDX, 0, IDX // 2, 0, 0)
                copies = []
                for i in range(TT):
                    copies.append((cols3(kk, i, 0, HEADS, DQ)[:, :, NOPE:DQ],
                                   lat[:, i, C_KR:C_KR + ROPE_A].unsqueeze(1).to_broadcast([P, HEADS, ROPE_A])))
                    copies.append((ki[:, i, :].rearrange("p (a c) -> p a c", c=IDX),
                                   lat[:, i, C_KI:C_KI + IDX].unsqueeze(1).to_broadcast([P, 4, IDX])))
                stage_norm_rope(nc, b, "nr2", [], ropes, copies)
                jobs = [(lambda i, n=n: qi[:, i, n * P:(n + 1) * P], P, qi_t[:, n, :], None) for n in range(2)]
                jobs.append((lambda i: ki[:, i, :], P, ki_t[:, :], None))
                for src, dst in ((q, q_t), (kk, k_t)):
                    jobs += [(lambda i, h=h, src=src: src[:, i, h * DQ:(h + 1) * DQ], DQ, dst[:, h, :], None)
                             for h in range(HEADS)]
                stage_turn(nc, b, "dsaqk", jobs)
            with ExitStack() as att:
                bias = att.enter_context(nc.sbuf_tensor("dsa_bias", [P, TT, S], F32))
                wi = att.enter_context(nc.sbuf_tensor("idx_w", [P, TT, HEADS], F32))
                with nc.Block() as block:
                    @block.vector
                    def _(dve):
                        nc.vector.tensor_scalar(wi[:, :, :], lat[:, :, C_WI:C_WI + HEADS], float(HEADS ** -0.5), None, ALU.mult)
                stage_select(nc, b, qi_t, ki_t, lambda i, h: wi[:, i, h:h + 1], bias)
                latent_attention(nc, b, "dsa", q_t, k_t, v, lambda i: bias[:, i, 0:(i + 1) * P], oa_t)
        with ExitStack() as out:
            z_t = out.enter_context(nc.sbuf_tensor("z_t", [P, DC, S], F32))
            stage_gated_up(nc, b, d, oa_t, ob_t, z_t)
            stage_output(nc, b, "o1", d["w_o"].rearrange("a k n -> (a k) n"), DC,
                         lambda k, i: z_t[:, k, i * P:(i + 1) * P])


def latent_attention(nc, b, tag, q_t, k_t, v, bias, o_t):
    with ExitStack() as own:
        o = own.enter_context(nc.sbuf_tensor(f"{tag}_o", [P, TT, HEADS * DV], F32))
        items = []
        for i in range(TT):
            for h in range(HEADS):
                w = (i + 1) * P
                items.append(([(0, q_t[:, h, i * P:w], k_t[:, h, 0:w])], bias(i), w,
                              [v[:, k, h * DV:(h + 1) * DV] for k in range(i + 1)], o[:, i, h * DV:(h + 1) * DV]))
        stage_attention(nc, b, tag, items, S, DQ ** -0.5)
        stage_turn(nc, b, f"{tag}o", [(lambda i, n=n: o[:, i, n * P:(n + 1) * P], P, o_t[:, n, :], None)
                                      for n in range(4)])


def mixer_two(nc, b, d):
    w_in = d["w_in_2"].rearrange("a k n -> (a k) n")
    with ExitStack() as mix:
        y_t = mix.enter_context(nc.sbuf_tensor("y_t", [P, DC, S], F32))
        lat = mix.enter_context(nc.sbuf_tensor("latents2", [P, TT, C2_RET], F32))
        with ExitStack() as heads:
            rq = heads.enter_context(nc.sbuf_tensor("ret_q", [P, TT, RW], F32))
            rk = heads.enter_context(nc.sbuf_tensor("ret_k", [P, TT, RW], F32))
            rv = heads.enter_context(nc.sbuf_tensor("ret_v", [P, TT, RW], F32))
            rg = heads.enter_context(nc.sbuf_tensor("ret_g", [P, TT, RW], F32))

            def plain(k, i):
                return b.feat[:, k, i * P:(i + 1) * P]

            jobs = [(w_in[:, 0:C2_RET], DC, plain, lambda i, ps: [(lat[:, i, :], ps)])]
            for n, t in enumerate((rq, rk, rv, rg)):
                at = C2_RET + n * RW
                jobs.append((w_in[:, at:at + RW], DC, plain, lambda i, ps, t=t: [(t[:, i, :], ps)]))
            stage_project(nc, b, "in2", jobs, DC)
            ropes = rope_items(b, rq, HEADS, DH, 0, DH // 2, ROPE_A // 2, 1)
            ropes += rope_items(b, rk, HEADS, DH, 0, DH // 2, ROPE_A // 2, 1)
            ropes += rope_items(b, lat[:, :, C2_KR:C2_KR + ROPE_A], 1, ROPE_A, 0, ROPE_A // 2, 0, 1)
            norms = [(lambda i: lat[:, i, 0:QL2], QL2), (lambda i: lat[:, i, QL2:QL2 + KVL2], KVL2)]
            decays = []
            for t, name in ((rq, "q_decay"), (rk, "k_decay")):
                for i in range(TT):
                    f = b.const(name)[:, i * HEADS:(i + 1) * HEADS].unsqueeze(2).to_broadcast([P, HEADS, DH])
                    decays.append((cols3(t, i, 0, HEADS, DH), f))
            stage_norm_rope(nc, b, "nr3", norms, ropes, (), decays)
            with ExitStack() as ret:
                q_t = ret.enter_context(nc.sbuf_tensor("ret_q_t", [P, 4, S], F32))
                k_t = ret.enter_context(nc.sbuf_tensor("ret_k_t", [P, 4, S], F32))
                stage_turn(nc, b, "ret", [(lambda i, n=n, t=t: t[:, i, n * P:(n + 1) * P], P, dst[:, n, :], None)
                                          for t, dst in ((rq, q_t), (rk, k_t)) for n in range(4)])
                stage_retention(nc, b, q_t, k_t, rv, rq)
            stage_retention_norm(nc, b, rq, rg[:, :, :])
            g = VEC_AT["g_ret_norm_2"]
            stage_turn(nc, b, "reto", [(lambda i, n=n: rg[:, i, n * P:(n + 1) * P], P, y_t[:, 4 + n, :],
                                        b.vec[:, g + n:g + n + 1]) for n in range(4)])
        with ExitStack() as mla:
            q_t = mla.enter_context(nc.sbuf_tensor("mla_q_t", [DQ, HEADS, S], F32))
            k_t = mla.enter_context(nc.sbuf_tensor("mla_k_t", [DQ, HEADS, S], F32))
            v = mla.enter_context(nc.sbuf_tensor("mla_v", [P, TT, HEADS * DV], F32))
            with ExitStack() as prep:
                lat_t = prep.enter_context(nc.sbuf_tensor("lat2_t", [P, 3, S], F32))
                q = prep.enter_context(nc.sbuf_tensor("mla_q", [P, TT, HEADS * DQ], F32))
                kk = prep.enter_context(nc.sbuf_tensor("mla_k", [P, TT, HEADS * DQ], F32))
                gq, gkv = VEC_AT["g_q_norm_2"], VEC_AT["g_kv_norm_2"]
                jobs = [(lambda i, n=n: lat[:, i, n * P:(n + 1) * P], P, lat_t[:, n, :],
                         b.vec[:, gq + n:gq + n + 1] if n < 2 else b.vec[:, gkv:gkv + 1]) for n in range(3)]
                stage_turn(nc, b, "lat2", jobs)
                w_uq = d["w_uq_2"].rearrange("a k n -> (a k) n")
                w_ukv = d["w_ukv_2"].rearrange("a k n -> (a k) n")

                def from_q(k, i):
                    return lat_t[:, k, i * P:(i + 1) * P]

                def from_kv(k, i):
                    return lat_t[:, 2, i * P:(i + 1) * P]

                def split_kv(n):
                    def stores(i, ps):
                        ps3 = ps.rearrange("p (h c) -> p h c", c=NOPE + DV)
                        k3 = cols3(kk, i, 0, HEADS, DQ)[:, 4 * n:4 * n + 4, 0:NOPE]
                        v3 = cols3(v, i, 0, HEADS, DV)[:, 4 * n:4 * n + 4, :]
                        return [(k3, ps3[:, :, 0:NOPE]), (v3, ps3[:, :, NOPE:NOPE + DV])]
                    return stores

                jobs = [(w_uq[:, n * 384:n * 384 + 384], 2, from_q,
                         lambda i, ps, n=n: [(q[:, i, n * 384:n * 384 + 384], ps)]) for n in range(2)]
                jobs += [(w_ukv[:, n * 512:n * 512 + 512], 1, from_kv, split_kv(n)) for n in range(2)]
                stage_project(nc, b, "uq2", jobs, 2)
                ropes = rope_items(b, q, HEADS, DQ, NOPE, ROPE_A // 2, 0, 1)
                copies = [(cols3(kk, i, 0, HEADS, DQ)[:, :, NOPE:DQ],
                           lat[:, i, C2_KR:C2_KR + ROPE_A].unsqueeze(1).to_broadcast([P, HEADS, ROPE_A]))
                          for i in range(TT)]
                stage_norm_rope(nc, b, "nr4", [], ropes, copies)
                jobs = []
                for src, dst in ((q, q_t), (kk, k_t)):
                    jobs += [(lambda i, h=h, src=src: src[:, i, h * DQ:(h + 1) * DQ], DQ, dst[:, h, :], None)
                             for h in range(HEADS)]
                stage_turn(nc, b, "mlaqk", jobs)
            with ExitStack() as att:
                bias = att.enter_context(nc.sbuf_tensor("mla_bias", [P, S + P], F32))
                with nc.Block() as block:
                    @block.vector
                    def _(dve):
                        nc.vector.memset(bias[:, 0:S - P], 0.0)
                        nc.vector.tensor_copy(bias[:, S - P:S], b.const("causal_bias"))
                latent_attention(nc, b, "mla", q_t, k_t, v, lambda i: bias[:, S - (i + 1) * P:S], y_t[:, 0:4, :])
        stage_output(nc, b, "o2", d["w_out_2"].rearrange("a k n -> (a k) n"), DC,
                     lambda k, i: y_t[:, k, i * P:(i + 1) * P], row=3)


def peer(nc, b, d):
    with ExitStack() as own:
        scores = own.enter_context(nc.sbuf_tensor("peer_s", [P, TT, 2 * PH, NKEY], F32))
        stage_norm_turn(nc, b, "nt5", 4, 12, keep_tokens=b.tok)
        with ExitStack() as route:
            q_t = route.enter_context(nc.sbuf_tensor("peer_q_t", [P, 2 * PH, S], F32))
            stage_queries(nc, b, d["w_query_2"], q_t)
            stage_key_scores(nc, b, d, q_t, scores)
        stage_experts(nc, b, d, scores)


def stage_queries(nc, b, w_query, q_t):
    NG = 2 * PH
    src = w_query.rearrange("a (k p) n -> p (a k) n", p=P)
    with ExitStack() as own:
        w = own.enter_context(nc.sbuf_tensor("query_w", [P, 2, DC, P], F32))
        w_in = [b.sem(f"query_w_in{j}") for j in range(2)]
        up = b.sem("query_up")
        out = b.sem("query_out")
        with nc.Block() as block:
            @block.sync
            def _(sp):
                for g in range(NG):
                    if g >= 2:
                        sp.wait_ge(up, g - 1)
                    sp.dma_start(w[:, g % 2, :, :], src[:, :, g * P:(g + 1) * P]).then_inc(w_in[g % 2], 16)

            @block.tensor
            def _(pe):
                for g in range(NG):
                    pe.wait_ge(w_in[g % 2], 16 * (g // 2 + 1))
                    if g >= 4:
                        pe.wait_ge(out, g - 3)
                    for k in range(DC):
                        ins = mm(nc, b.ps[:, g % 4, :], w[:, g % 2, k, :], b.feat[:, k, :], k == 0, k == DC - 1)
                    ins.then_inc(up, 1)

            @block.scalar
            def _(act):
                for g in range(NG):
                    act.wait_ge(up, g + 1)
                    nc.scalar.activation(q_t[:, g, :], b.ps[:, g % 4, :], ACT.Copy).then_inc(out, 1)


def build_program(nc, d, out, upto=99):
    b = Bufs(nc)
    b.n_freq = ROPE_A // 2 + DH // 2
    with ExitStack() as ctx:
        def sb(name, shape, dt=F32):
            return ctx.enter_context(nc.sbuf_tensor(name, shape, dt))

        b.consts = sb("consts", [P, CONST_PACK.shape[1]])
        b.x = sb("residual", [P, TT, D])
        b.tok = sb("tok", [P, TT, D])
        b.feat = sb("feat", [P, DC, S])
        b.rows = sb("gate_rows", [P, 6, D])
        b.vec = sb("vec_cols", [P, NVEC])
        b.bias_cols = sb("bias_cols", [P, NMOD])
        b.mod = sb("mod_cols", [P, NMOD])
        b.scale_cols = sb("scale_cols", [P, 5, DC])
        b.silu_c = sb("silu_c", [P, 2 * DC])
        b.sin = sb("sin", [P, 2 * TT, b.n_freq])
        b.cos = sb("cos", [P, 2 * TT, b.n_freq])
        b.stat = sb("stat", [P, TT])
        b.ps = ctx.enter_context(nc.psum_tensor("ps", [P, 8, 512], F32))

        def const(name):
            at, n = CONSTS[name]
            return b.consts[:, at:at + n]

        b.const = const
        stage_setup(nc, b, d)
        stage_modulation(nc, b, d)
        if upto >= 1:
            b.end_of_part()
            stage_norm_turn(nc, b, "nt1", 0, 0)
            stage_swiglu(nc, b, "ffn1", d["w_gate1"], d["w_up1"], d["w_down1"])
            stage_post_norm(nc, b, "pn1", 0)
        if upto >= 2:
            b.end_of_part()
            stage_norm_turn(nc, b, "nt2", 1, 3)
            mixer_one(nc, b, d)
            stage_post_norm(nc, b, "pn2", 1)
        if upto >= 3:
            b.end_of_part()
            stage_norm_turn(nc, b, "nt3", 2, 6)
            stage_swiglu(nc, b, "ffn2", d["w_gate2"], d["w_up2"], d["w_down2"])
            stage_post_norm(nc, b, "pn3", 2)
        if upto >= 4:
            b.end_of_part()
            stage_norm_turn(nc, b, "nt4", 3, 9)
            mixer_two(nc, b, d)
        if upto >= 5:
            b.end_of_part()
            peer(nc, b, d)
        if upto >= 5:
            stage_final(nc, b, out)


_INS = ["x", "c", "positions", "w_mod", "b_mod", "g_pre_ffn1", "w_gate1", "w_up1", "w_down1", "g_post_ffn1",
        "g_pre_mix", "w_in", "g_cq", "g_ckv", "w_uq", "w_uk", "w_uv", "w_iq", "w_up_a", "w_up_b", "w_o",
        "g_post_mix", "g_pre_ffn2", "w_gate2", "w_up2", "w_down2", "g_post_ffn2", "c_2", "positions_2",
        "w_ada_2", "b_ada_2", "g_norm1_2", "w_in_2", "g_q_norm_2", "w_uq_2", "g_kv_norm_2", "w_ukv_2",
        "g_ret_norm_2", "w_out_2", "g_norm2_2", "w_query_2", "sub_keys_2", "expert_u_2", "expert_v_2",
        "g_final_2"]


def kernel(**inputs):
    import numpy as _np
    import concourse.bacc as _bacc
    from concourse import mybir as _mybir
    from concourse.bass_utils import run_bass_kernel_spmd as _run

    nc = _bacc.Bacc("TRN2", target_bir_lowering=False, num_devices=1)
    given = {name: _np.ascontiguousarray(inputs[name]) for name in _INS}
    given["const_pack"] = CONST_PACK
    given["dilated_bias"] = DILATED_BIAS
    arrays, d = {}, {}
    for name, a in given.items():
        arrays[f"in_{name}"] = a
        d[name] = nc.dram_tensor(f"in_{name}", a.shape, _mybir.dt.from_np(a.dtype), kind="ExternalInput").ap()
    out = nc.dram_tensor("out_0", (1, S, D), F32, kind="ExternalOutput").ap()
    build_program(nc, d, out)
    r = _run(nc, [arrays], core_ids=[0])
    return r.results[0]["out_0"]
```

```python
from contextlib import ExitStack

import numpy as np

import concourse.bass as bass
from concourse import mybir

F32 = mybir.dt.float32
F32R = mybir.dt.float32r
I32 = mybir.dt.int32
U32 = mybir.dt.uint32
ALU = mybir.AluOpType
ACT = mybir.ActivationFunctionType
AX = mybir.AxisListType

P = 128
S = 512
D = 1024
TT = S // P
DC = D // P
F = 2816
FC = F // P
EPS = 1e-6
THETA = 10000.0
NEG = -1e30

SLOT = 2048

QL, KVL, NOPE, ROPE_A, DV = 384, 256, 64, 32, 64
HEADS = 8
IDX = 32
TOPK = 128
GRP, HB, DH = 3, 4, 64
DIL = ((128, 1), (512, 4), (2048, 16))
C_CKV = QL
C_KR = QL + KVL
C_KI = C_KR + ROPE_A
C_WI = C_KI + IDX
C_QKV = C_WI + HEADS
C_GATE = C_QKV + 3 * GRP * HB * DH
DQ = NOPE + ROPE_A
QL2, KVL2 = 256, 128
RW = 512
C2_KR = QL2 + KVL2
C2_RET = C2_KR + ROPE_A
PH, NKEY, KH, PK = 8, 128, 128, 16
NEXP = NKEY * NKEY

VECS = [("g_pre_ffn1", 8), ("g_pre_mix", 8), ("g_pre_ffn2", 8), ("g_norm1_2", 8), ("g_norm2_2", 8),
        ("g_cq", 3), ("g_ckv", 2), ("g_q_norm_2", 2), ("g_kv_norm_2", 1), ("c", 8), ("c_2", 8),
        ("g_post_ffn1", 8), ("g_post_mix", 8), ("g_post_ffn2", 8), ("g_final_2", 8), ("g_ret_norm_2", 4)]
VEC_AT = {}
_n = 0
for _name, _k in VECS:
    VEC_AT[_name] = _n
    _n += _k
NVEC = _n
NMOD1, NMOD2 = 9 * DC, 6 * DC
NMOD = NMOD1 + NMOD2

CONSTS = {}


def build_constants():
    p = np.arange(P)
    parts = []

    def put(name, a):
        at = sum(x.shape[1] for x in parts)
        CONSTS[name] = (at, a.shape[1])
        parts.append(np.ascontiguousarray(a, np.float32))

    put("identity", np.eye(P))
    put("causal_bias", np.where(p[None, :] <= p[:, None], 0.0, NEG))
    put("decay_mask", np.concatenate([(p[None, :] >= p[:, None]) * 1.0, np.ones((P, S - P))], 1))
    CONSTS["ones"] = (CONSTS["decay_mask"][0] + P, P)
    f32 = np.float32
    inv = [f32(THETA) ** (-np.arange(h, dtype=f32) / f32(h)) for h in (ROPE_A // 2, DH // 2)]
    put("inv_freq", np.tile(np.concatenate(inv)[None], (P, 1)))
    log_g = np.log(1.0 - 2.0 ** (-5.0 - np.arange(HEADS)))
    t = (np.arange(TT)[None, :] * P + p[:, None])[:, :, None]
    put("q_decay", np.exp(log_g * t).reshape(P, -1))
    put("k_decay", (np.exp(-log_g * t) * DH ** -0.5).reshape(P, -1))
    put("iota", np.tile(np.arange(PK)[None], (P, 1)))
    put("half_pi", np.full((P, 1), np.pi / 2))
    put("eps", np.full((P, 1), EPS))
    return np.concatenate(parts, 1)


CONST_PACK = build_constants()


def build_dilated_bias():
    n = np.arange(P)
    out = np.full((P, TT, S + 2 * P), NEG, np.float32)
    for r in range(TT):
        for r2 in range(TT):
            d = (4 * n + r)[:, None] - (4 * n + r2)[None, :]
            out[:, r, r2 * P:(r2 + 1) * P][(d >= 0) & (d <= DIL[0][0])] = 0
        d = 4 * (n[:, None] - n[None, :])
        for g in (1, 2):
            at = S + (g - 1) * P
            out[:, r, at:at + P][(d >= 0) & (d <= DIL[g][0]) & (d % DIL[g][1] == 0)] = 0
    return out.reshape(P, -1)


DILATED_BIAS = build_dilated_bias()


class Chain:

    def __init__(self, eng, sem):
        self.eng, self.sem, self.n = eng, sem, 0

    def __call__(self, ins):
        self.n += 1
        ins.then_inc(self.sem, 1)
        self.eng.wait_ge(self.sem, self.n)


def root_mean(nc, b, act, stat, n, squares, count, rooted):
    act.wait_ge(squares, count)
    nc.scalar.activation(stat, stat, ACT.Sqrt, scale=1.0 / n, bias=b.const("eps")).then_inc(rooted, 1)


class Bufs:

    def __init__(self, nc):
        self.nc, self.sems = nc, []

    def sem(self, name):
        self.sems.append(self.nc.alloc_semaphore(name))
        return self.sems[-1]

    def split_pair(self, own, name, chunks):
        return [own.enter_context(self.nc.sbuf_tensor(f"{name}_{part}", [P, chunks, S], F32R)) for part in ("hi", "lo")]

    def end_of_part(self):
        self.nc.clear_and_free_semaphores(self.sems)
        self.nc.all_engine_barrier()
        self.sems = []


def mm(nc, out, lhsT, rhs, start, stop):
    return nc.tensor.matmul(out, lhsT, rhs, start=start, stop=stop, skip_group_check=True)


def split_products(nc, out, lhsT, rhs, start, stop):
    mm(nc, out, lhsT[0], rhs[0], start, False)
    mm(nc, out, lhsT[0], rhs[1], False, False)
    return mm(nc, out, lhsT[1], rhs[0], False, stop)


class WeightStream:

    def __init__(self, nc, b, own, tag, raw):
        self.nc, self.raw = nc, raw
        self.hi = own.enter_context(nc.sbuf_tensor(f"{tag}_w_hi", [P, 2, SLOT], F32R))
        self.lo = own.enter_context(nc.sbuf_tensor(f"{tag}_w_lo", [P, 2, SLOT], F32R))
        self.arrived = [b.sem(f"{tag}_w_arrived{j}") for j in range(2)]
        self.hi_done = b.sem(f"{tag}_w_hi_done")
        self.lo_done = b.sem(f"{tag}_w_lo_done")
        self.used = b.sem(f"{tag}_w_used")

    def load(self, sp, n, j, srcs, first=False):
        if not first:
            sp.wait_ge(self.lo_done, n - 1)
        for at, k, src in srcs:
            w = src.shape[-1]
            sp.dma_start(self.raw[:, j, at:at + k * w].rearrange("p (k n) -> p k n", k=k), src).then_inc(self.arrived[j], 16)

    def round(self, act, n, j, dmas, width=SLOT, first=False):
        act.wait_ge(self.arrived[j], dmas)
        if not first:
            act.wait_ge(self.used, n - 1)
        self.nc.scalar.activation(self.hi[:, j, 0:width], self.raw[:, j, 0:width], ACT.Copy).then_inc(self.hi_done, 1)

    def rest(self, dve, n, j, width=SLOT):
        dve.wait_ge(self.hi_done, n + 1)
        self.nc.vector.tensor_tensor(self.lo[:, j, 0:width], self.raw[:, j, 0:width], self.hi[:, j, 0:width],
                                     ALU.subtract).then_inc(self.lo_done, 1)

    def parts(self, j, at, w):
        return self.hi[:, j, at:at + w], self.lo[:, j, at:at + w]


def stage_setup(nc, b, d):
    with ExitStack() as own:
        vec_rows = own.enter_context(nc.sbuf_tensor("vec_rows", [NVEC, P], F32))
        bias_rows = own.enter_context(nc.sbuf_tensor("bias_rows", [NMOD, P], F32))
        pos_i = own.enter_context(nc.sbuf_tensor("pos_i", [2 * TT, P], I32))
        pos_rows = own.enter_context(nc.sbuf_tensor("pos_rows", [2 * TT, P], F32))
        pos_col = own.enter_context(nc.sbuf_tensor("pos_col", [P, 2 * TT], F32))
        NA = 2 * TT * b.n_freq
        ang = own.enter_context(nc.sbuf_tensor("ang", [P, 2 * TT, b.n_freq], F32))
        turns = own.enter_context(nc.sbuf_tensor("turns", [P, NA], F32))
        c_sig = own.enter_context(nc.sbuf_tensor("c_sig", [P, 2 * DC], F32))
        const_in = b.sem("const_in")
        x_in = b.sem("x_in")
        vec_in = b.sem("vec_in")
        pos_in = b.sem("pos_in")
        pos_float = b.sem("pos_float")
        cols_up = b.sem("cols_turned")
        setup_chain = b.sem("setup_chain")
        angle_ready = b.sem("angle_ready")
        n_vec_dma = len(VECS) + 2
        with nc.Block() as block:
            @block.sync
            def _(sp):
                sp.dma_start(pos_i[0:TT, :], d["positions"].rearrange("a (i p) -> (a i) p", p=P)).then_inc(pos_in, 16)
                sp.dma_start(pos_i[TT:2 * TT, :],
                             d["positions_2"].rearrange("a (i p) -> (a i) p", p=P)).then_inc(pos_in, 16)
                sp.dma_start(b.consts[:, :], d["const_pack"]).then_inc(const_in, 16)
                sp.dma_start(b.x[:, :, :], d["x"].rearrange("a (i p) n -> p (a i) n", p=P)).then_inc(x_in, 16)
                sp.wait_ge(x_in, 16)

            @block.scalar
            def _(act):
                for name, k in VECS:
                    v = d[name]
                    v = v.rearrange("(k p) -> k p", p=P) if len(v.shape) == 1 else v.rearrange("a (k p) -> (a k) p", p=P)
                    at = VEC_AT[name]
                    act.dma_start(vec_rows[at:at + k, :], v).then_inc(vec_in, 16)
                act.dma_start(bias_rows[0:NMOD1, :], d["b_mod"].rearrange("a (k p) -> (a k) p", p=P)).then_inc(vec_in, 16)
                act.dma_start(bias_rows[NMOD1:NMOD, :],
                              d["b_ada_2"].rearrange("a (k p) -> (a k) p", p=P)).then_inc(vec_in, 16)
                act.wait_ge(cols_up, 4)
                at = VEC_AT["c"]
                nc.scalar.activation(c_sig[:, :], b.vec[:, at:at + 2 * DC], ACT.Sigmoid).then_inc(angle_ready, 1)
                act.wait_ge(angle_ready, 3)
                nc.scalar.activation(b.sin[:, :, :].rearrange("p a f -> p (a f)"),
                                     ang[:, :, :].rearrange("p a f -> p (a f)"), ACT.Sin)
                nc.scalar.activation(b.cos[:, :, :].rearrange("p a f -> p (a f)"), turns[:, :], ACT.Sin,
                                     bias=b.const("half_pi"), scale=-1.0)

            @block.tensor
            def _(pe):
                pe.wait_ge(const_in, 16)
                pe.wait_ge(pos_float, 1)
                ident = b.const("identity")
                nc.tensor.transpose(b.ps[:, 0, 0:2 * TT], pos_rows[:, :], ident[0:2 * TT, 0:2 * TT]).then_inc(cols_up, 1)
                pe.wait_ge(vec_in, 16 * n_vec_dma)
                nc.tensor.transpose(b.ps[:, 1, 0:NVEC], vec_rows[:, :], ident[0:NVEC, 0:NVEC]).then_inc(cols_up, 1)
                nc.tensor.transpose(b.ps[:, 2, 0:NMOD], bias_rows[:, :], ident[0:NMOD, 0:NMOD]).then_inc(cols_up, 1)

            @block.vector
            def _(dve):
                link = Chain(dve, setup_chain)
                dve.wait_ge(pos_in, 32)
                nc.vector.tensor_copy(pos_rows[:, :], pos_i[:, :]).then_inc(pos_float, 1)
                dve.wait_ge(cols_up, 1)
                link(nc.vector.tensor_copy(pos_col[:, :], b.ps[:, 0, 0:2 * TT]))
                dve.wait_ge(const_in, 16)
                dve.wait_ge(cols_up, 3)
                link(nc.vector.tensor_copy(b.bias_cols, b.ps[:, 2, 0:NMOD]))
                nc.vector.tensor_copy(b.vec[:, :], b.ps[:, 1, 0:NVEC]).then_inc(cols_up, 1)
                inv = b.const("inv_freq").unsqueeze(1).to_broadcast([P, 2 * TT, b.n_freq])
                link(nc.vector.tensor_tensor(ang[:, :, :], inv,
                                             pos_col[:, :].unsqueeze(2).to_broadcast([P, 2 * TT, b.n_freq]), ALU.mult))
                a = ang[:, :, :].rearrange("p a f -> p (a f)")
                magic = 1.5 * 2.0 ** 23
                two_pi = 2 * np.pi
                c1 = 6.28125
                c2 = round((two_pi - c1) * 2 ** 21) / 2 ** 21
                c3 = two_pi - c1 - c2
                link(nc.vector.tensor_scalar(turns[:, :], a, float(1 / two_pi), None, ALU.mult))
                link(nc.vector.tensor_scalar(turns[:, :], turns[:, :], magic, None, ALU.add))
                link(nc.vector.tensor_scalar(turns[:, :], turns[:, :], -magic, None, ALU.add))
                for part in (c1, c2, c3):
                    link(nc.vector.scalar_tensor_tensor(a, turns[:, :], -float(part), a, ALU.mult, ALU.add))
                link(nc.vector.tensor_scalar(a, a, 3.1415925, -3.1415925, ALU.min, ALU.max))
                nc.vector.scalar_tensor_tensor(turns[:, :], a, -1.0, a, ALU.mult, ALU.max).then_inc(angle_ready, 1)
                dve.wait_ge(angle_ready, 2)
                at = VEC_AT["c"]
                nc.vector.tensor_tensor(b.silu_c[:, :], c_sig[:, :], b.vec[:, at:at + 2 * DC],
                                        ALU.mult).then_inc(angle_ready, 1)


def stage_modulation(nc, b, d):
    W = 512
    with ExitStack() as own:
        w = own.enter_context(nc.sbuf_tensor("mod_w", [P, 2, DC, W], F32))
        acc = own.enter_context(nc.sbuf_tensor("mod_acc", [P, 2, W], F32))
        diag = own.enter_context(nc.sbuf_tensor("gate_diag", [P, 2, 4, P], F32))
        gates = own.enter_context(nc.sbuf_tensor("gate_cols", [P, 6, DC], F32))
        w_in = [b.sem(f"mod_w_in{j}") for j in range(2)]
        part = b.sem("mod_part")
        summed = b.sem("mod_summed")
        chain = b.sem("mod_chain")
        diag_ready = b.sem("diag_ready")
        row_up = b.sem("gate_row_up")
        row_out = b.sem("gate_row_out")
        parts = [(d["w_mod"], 9 * D // W, 0, 0), (d["w_ada_2"], 6 * D // W, 9 * D // W, DC)]
        with nc.Block() as block:
            @block.sync
            def _(sp):
                def load(rows, i, j, before):
                    sp.dma_start(w[:, j, :, :], rows[:, :, bass.ds((i * 2 + j) * W, W)]).then_inc(w_in[j], 16)

                for src, n, before, _c in parts:
                    rows = src.rearrange("a (k p) n -> p (a k) n", p=P)
                    if not before:
                        load(rows, 0, 0, before)
                        load(rows, 0, 1, before)
                    with sp.Fori(0 if before else 1, n // 2) as i:
                        for j in range(2):
                            sp.wait_ge(part, (i * 2 + j + before - 1) * DC)
                            load(rows, i, j, before)

            @block.vector
            def _(dve):
                def chunk(i, j, before, c_at):
                    dve.wait_ge(w_in[j], (i + before // 2 + 1) * 16)
                    for k in range(DC):
                        c = b.silu_c[:, c_at + k:c_at + k + 1]
                        if k == 0:
                            ins = nc.vector.tensor_scalar(acc[:, j, :], w[:, j, k, :], c, None, ALU.mult)
                        else:
                            dve.wait_ge(part, (i * 2 + j + before) * DC + k)
                            ins = nc.vector.scalar_tensor_tensor(acc[:, j, :], w[:, j, k, :], c, acc[:, j, :],
                                                                 ALU.mult, ALU.add)
                        ins.then_inc(part, 1)

                for _src, n, before, c_at in parts:
                    if not before:
                        chunk(0, 0, before, c_at)
                        chunk(0, 1, before, c_at)
                    with dve.Fori(0 if before else 1, n // 2) as i:
                        for j in range(2):
                            dve.wait_ge(summed, i * 2 + j + before - 1)
                            chunk(i, j, before, c_at)
                link = Chain(dve, chain)
                dve.wait_ge(summed, NMOD * P // W)
                link(nc.vector.tensor_tensor(b.mod[:, :], b.ps[:, 0, 0:NMOD], b.bias_cols, ALU.add))
                for n, (name, at) in enumerate((("g_pre_ffn1", 1), ("g_pre_mix", 4), ("g_pre_ffn2", 7),
                                                ("g_norm1_2", 10), ("g_norm2_2", 13))):
                    v = VEC_AT[name]
                    nc.vector.scalar_tensor_tensor(b.scale_cols[:, n, :], b.mod[:, at * DC:(at + 1) * DC], 1.0,
                                                   b.vec[:, v:v + DC], ALU.add, ALU.mult)
                for n, (name, at, half) in enumerate((("g_post_ffn1", 2, 0.5), ("g_post_mix", 5, 1.0),
                                                      ("g_post_ffn2", 8, 0.5))):
                    v = VEC_AT[name]
                    nc.vector.scalar_tensor_tensor(gates[:, n, :], b.mod[:, at * DC:(at + 1) * DC], half,
                                                   b.vec[:, v:v + DC], ALU.mult, ALU.mult)
                v = VEC_AT["g_final_2"]
                nc.vector.tensor_copy(gates[:, 5, :], b.vec[:, v:v + DC])
                nc.vector.tensor_copy(gates[:, 3, :], b.mod[:, 11 * DC:12 * DC])
                link(nc.vector.tensor_copy(gates[:, 4, :], b.mod[:, 14 * DC:15 * DC]))
                ident = b.const("identity").unsqueeze(1).to_broadcast([P, 4, P])
                for n in range(12):
                    if n >= 2:
                        dve.wait_ge(row_up, n - 1)
                    cols = gates[:, n // 2, 4 * (n % 2):4 * (n % 2) + 4].unsqueeze(2).to_broadcast([P, 4, P])
                    nc.vector.tensor_tensor(diag[:, n % 2, :, :], ident, cols, ALU.mult).then_inc(diag_ready, 1)

            @block.tensor
            def _(pe):
                ones = b.const("ones")
                for _src, n, before, _c in parts:
                    with pe.Fori(0, n // 2) as i:
                        for j in range(2):
                            pe.wait_ge(part, (i * 2 + j + before + 1) * DC)
                            for q in range(4):
                                col = (i * 2 + j + before) * 4 + q
                                ins = mm(nc, b.ps[:, 0, bass.ds(col, 1)], acc[:, j, q * P:(q + 1) * P], ones[:, 0:1],
                                         True, True)
                            ins.then_inc(summed, 1)
                for n in range(12):
                    pe.wait_ge(diag_ready, n + 1)
                    if n >= 2:
                        pe.wait_ge(row_out, n - 1)
                    mm(nc, b.ps[:, 1 + n % 2, :], ones, diag[:, n % 2, :, :].rearrange("p a c -> p (a c)"),
                       True, True).then_inc(row_up, 1)

            @block.scalar
            def _(act):
                for n in range(12):
                    act.wait_ge(row_up, n + 1)
                    nc.scalar.activation(b.rows[:, n // 2, (n % 2) * 512:(n % 2) * 512 + 512], b.ps[:, 1 + n % 2, :],
                                         ACT.Copy).then_inc(row_out, 1)


def stage_norm_turn(nc, b, tag, scale_at, shift_at, h_hi, h_lo, keep_tokens=None):
    xs = b.tok
    squares = b.sem(f"{tag}_squares")
    rooted = b.sem(f"{tag}_rooted")
    rstd = b.sem(f"{tag}_rstd")
    scaled = b.sem(f"{tag}_scaled")
    turned = b.sem(f"{tag}_turned")
    moved = b.sem(f"{tag}_moved")
    hi_done = b.sem(f"{tag}_hi_done")
    back = b.sem(f"{tag}_back")
    with nc.Block() as block:
        @block.scalar
        def _(act):
            for i in range(TT):
                nc.scalar.activation(b.feat[:, 2 * i:2 * i + 2, :].rearrange("p a n -> p (a n)"), b.x[:, i, :],
                                     ACT.Square, accum_out=b.stat[:, i:i + 1]).then_inc(squares, 1)
            root_mean(nc, b, act, b.stat[:, :], D, squares, TT, rooted)
            for k in range(DC):
                act.wait_ge(moved, k + 1)
                nc.scalar.activation(h_hi[:, k, :], b.feat[:, k, :], ACT.Copy).then_inc(hi_done, 1)
            if keep_tokens is not None:
                for n in range(2 * TT):
                    act.wait_ge(back, n + 1)
                    nc.scalar.activation(keep_tokens[:, n // 2, (n % 2) * 512:(n % 2) * 512 + 512], b.ps[:, n, :], ACT.Copy)

        @block.vector
        def _(dve):
            dve.wait_ge(rooted, 1)
            nc.vector.reciprocal(b.stat[:, :], b.stat[:, :]).then_inc(rstd, 1)
            dve.wait_ge(rstd, 1)
            for i in range(TT):
                nc.vector.tensor_scalar(xs[:, i, :], b.x[:, i, :], b.stat[:, i:i + 1], None, ALU.mult).then_inc(scaled, 1)
            for k in range(DC):
                dve.wait_ge(turned, k + 1)
                nc.vector.tensor_scalar(b.feat[:, k, :], b.ps[:, k, :], b.scale_cols[:, scale_at, k:k + 1],
                                        b.mod[:, shift_at * DC + k:shift_at * DC + k + 1], ALU.mult,
                                        ALU.add).then_inc(moved, 1)

        @block.gpsimd
        def _(pool):
            for k in range(DC):
                pool.wait_ge(hi_done, k + 1)
                nc.gpsimd.tensor_tensor(h_lo[:, k, :], b.feat[:, k, :], h_hi[:, k, :], ALU.subtract)

        @block.tensor
        def _(pe):
            ident = b.const("identity")
            for i in range(TT):
                pe.wait_ge(scaled, i + 1)
                for k in range(DC):
                    ins = nc.tensor.transpose(b.ps[:, k, i * P:(i + 1) * P], xs[:, i, k * P:(k + 1) * P], ident)
                    if i == TT - 1:
                        ins.then_inc(turned, 1)
            if keep_tokens is not None:
                pe.wait_ge(moved, DC)
                for n in range(2 * TT):
                    for q in range(4):
                        ins = nc.tensor.transpose(b.ps[:, n, q * P:(q + 1) * P],
                                                  b.feat[:, (n % 2) * 4 + q, (n // 2) * P:(n // 2 + 1) * P], ident)
                    ins.then_inc(back, 1)


def stage_split(nc, b, tag, jobs):
    hi_done = b.sem(f"{tag}_hi_done")
    chunks = [(src[:, k, :], hi[:, k, :], lo[:, k, :]) for src, hi, lo in jobs for k in range(src.shape[1])]
    with nc.Block() as block:
        @block.scalar
        def _(act):
            for src, hi, _lo in chunks:
                nc.scalar.activation(hi, src, ACT.Copy).then_inc(hi_done, 1)

        @block.vector
        def _(dve):
            for n, (src, hi, lo) in enumerate(chunks):
                dve.wait_ge(hi_done, n + 1)
                nc.vector.tensor_tensor(lo, src, hi, ALU.subtract)


def stage_post_norm(nc, b, tag, row):
    squares = b.sem(f"{tag}_squares")
    chain = b.sem(f"{tag}_chain")
    rooted = b.sem(f"{tag}_rooted")
    rstd = b.sem(f"{tag}_rstd")
    with nc.Block() as block:
        @block.scalar
        def _(act):
            for i in range(TT):
                nc.scalar.activation(b.feat[:, 2 * i:2 * i + 2, :].rearrange("p a n -> p (a n)"), b.tok[:, i, :],
                                     ACT.Square, accum_out=b.stat[:, i:i + 1]).then_inc(squares, 1)
            root_mean(nc, b, act, b.stat[:, :], D, squares, TT, rooted)

        @block.vector
        def _(dve):
            link = Chain(dve, chain)
            dve.wait_ge(rooted, 1)
            nc.vector.reciprocal(b.stat[:, :], b.stat[:, :]).then_inc(rstd, 1)
            dve.wait_ge(rstd, 1)
            for i in range(TT):
                link(nc.vector.scalar_tensor_tensor(b.tok[:, i, :], b.tok[:, i, :], b.stat[:, i:i + 1], b.rows[:, row, :],
                                                    ALU.mult, ALU.mult))
                nc.vector.tensor_tensor(b.x[:, i, :], b.x[:, i, :], b.tok[:, i, :], ALU.add)


def stage_swiglu(nc, b, tag, w_gate, w_up, w_down, h_hi, h_lo):
    wg = w_gate.rearrange("a (k p) n -> p (a k) n", p=P)
    wu = w_up.rearrange("a (k p) n -> p (a k) n", p=P)
    wd = w_down.rearrange("a (k p) n -> p (a k) n", p=P)
    counts = (12, 10)
    firsts = (0, counts[0])
    slots = (0, counts[0] + counts[0] // 2)
    assert sum(counts) == FC
    last_slot = slots[1] + counts[1] + counts[1] // 2 - 1
    with ExitStack() as own:
        raw = own.enter_context(nc.sbuf_tensor(f"{tag}_w_raw", [P, 2, SLOT], F32))
        ws = WeightStream(nc, b, own, tag, raw)
        gu_hi = own.enter_context(nc.sbuf_tensor(f"{tag}_gu_hi", [P, counts[0], S], F32R))
        gu_lo = own.enter_context(nc.sbuf_tensor(f"{tag}_gu_lo", [P, counts[0], S], F32R))
        silu = b.feat[:, 0:2, :]
        gu = b.feat[:, 2:4, :]
        silu_done = b.sem(f"{tag}_silu")
        gu_done = b.sem(f"{tag}_gu_done")
        gu_hi_done = b.sem(f"{tag}_gu_hi_done")
        gu_lo_done = b.sem(f"{tag}_gu_lo_done")
        y_up = b.sem(f"{tag}_y_up")
        y_out = b.sem(f"{tag}_y_out")

        def arrived_before(slot):
            total = 0
            for m in range(slot % 2, slot, 2):
                part = 1 if m >= slots[1] else 0
                total += 32 if m - slots[part] < counts[part] else 16
            return total

        with nc.Block() as block:
            @block.sync
            def _(sp):
                for part in range(2):
                    base, c0, n = slots[part], firsts[part], counts[part]

                    def gate_up(i, j, first=False):
                        cols = bass.ds((i * 2 + j + c0) * P, P)
                        ws.load(sp, i * 2 + j + base, j, [(0, DC, wg[:, :, cols]), (DC * P, DC, wu[:, :, cols])], first)

                    if part == 0:
                        gate_up(0, 0, True)
                        gate_up(0, 1, True)
                    with sp.Fori(0 if part else 1, n // 2) as i:
                        gate_up(i, 0)
                        gate_up(i, 1)
                    for q in range(n // 2):
                        m = base + n + q
                        ws.load(sp, m, m % 2, [(0, 2, wd[:, c0 + 2 * q:c0 + 2 * q + 2, :])])

            @block.scalar
            def _(act):
                ws.round(act, 0, 0, 32, first=True)
                for part in range(2):
                    base, c0, n = slots[part], firsts[part], counts[part]
                    gone = arrived_before(base)
                    gone1 = arrived_before(base + 1)

                    def chunk(i, j, prepare=True, first=False):
                        c = i * 2 + j + c0
                        if prepare:
                            if j == 0:
                                ws.round(act, i * 2 + 1 + base, 1, gone1 + (i + 1) * 32, first=first)
                            else:
                                ws.round(act, i * 2 + 2 + base, 0, gone + (i + 2) * 32)
                        act.wait_ge(ws.used, i * 2 + j + base + 1)
                        if not first:
                            act.wait_ge(gu_done, c - 1)
                        nc.scalar.activation(silu[:, j, :], b.ps[:, 2 * j, :], ACT.Silu).then_inc(silu_done, 1)
                        act.wait_ge(gu_done, c + 1)
                        nc.scalar.activation(gu_hi[:, i * 2 + j, :], gu[:, j, :], ACT.Copy).then_inc(gu_hi_done, 1)

                    if part == 0:
                        chunk(0, 0, first=True)
                        chunk(0, 1, first=True)
                    with act.Fori(0 if part else 1, n // 2 - 1) as i:
                        chunk(i, 0)
                        chunk(i, 1)
                    chunk(n // 2 - 1, 0)
                    ws.round(act, base + n, 0, arrived_before(base + n) + 16)
                    chunk(n // 2 - 1, 1, prepare=False)
                    for q in range(n // 2):
                        m = base + n + q + 1
                        if m <= last_slot:
                            ws.round(act, m, m % 2, arrived_before(m) + (16 if q < n // 2 - 1 else 32))

            @block.vector
            def _(dve):
                ws.rest(dve, 0, 0)
                for part in range(2):
                    base, c0, n = slots[part], firsts[part], counts[part]

                    def chunk(i, j, first=False):
                        c = i * 2 + j + c0
                        ws.rest(dve, i * 2 + j + 1 + base, 1 - j)
                        dve.wait_ge(silu_done, c + 1)
                        if not first:
                            dve.wait_ge(gu_lo_done, c - 1)
                        nc.vector.tensor_tensor(gu[:, j, :], silu[:, j, :], b.ps[:, 2 * j + 1, :], ALU.mult).then_inc(gu_done, 1)
                        dve.wait_ge(gu_hi_done, c + 1)
                        nc.vector.tensor_tensor(gu_lo[:, i * 2 + j, :], gu[:, j, :], gu_hi[:, i * 2 + j, :],
                                                ALU.subtract).then_inc(gu_lo_done, 1)

                    if part == 0:
                        chunk(0, 0, True)
                        chunk(0, 1, True)
                    with dve.Fori(0 if part else 1, n // 2) as i:
                        chunk(i, 0)
                        chunk(i, 1)
                    for q in range(n // 2):
                        m = base + n + q + 1
                        if m <= last_slot:
                            ws.rest(dve, m, m % 2)
                    for n_bank in range(8):
                        i, half = n_bank // 2, n_bank % 2
                        at = slice(half * 512, half * 512 + 512)
                        if n_bank < 7:
                            dve.wait_ge(y_up, part * 7 + n_bank + 1)
                        else:
                            dve.wait_ge(ws.used, base + n + n // 2)
                        if part == 0:
                            ins = nc.vector.tensor_copy(b.tok[:, i, at], b.ps[:, n_bank, :])
                        else:
                            if n_bank == 0:
                                dve.wait_ge(y_out, 8)
                            ins = nc.vector.tensor_tensor(b.tok[:, i, at], b.tok[:, i, at], b.ps[:, n_bank, :], ALU.add)
                        ins.then_inc(y_out, 1)

            @block.tensor
            def _(pe):
                for part in range(2):
                    base, c0, n = slots[part], firsts[part], counts[part]

                    def chunk(i, j, first=False):
                        c = i * 2 + j + c0
                        pe.wait_ge(ws.lo_done, i * 2 + j + base + 1)
                        if not first:
                            pe.wait_ge(gu_done, c - 1)
                        for m in range(2):
                            for k in range(DC):
                                ins = split_products(nc, b.ps[:, 2 * j + m, :], ws.parts(j, (m * DC + k) * P, P),
                                                     (h_hi[:, k, :], h_lo[:, k, :]), k == 0, k == DC - 1)
                        ins.then_inc(ws.used, 1)

                    if part == 0:
                        chunk(0, 0, True)
                        chunk(0, 1, True)
                    else:
                        pe.wait_ge(y_out, 4)
                    with pe.Fori(0 if part else 1, n // 2) as i:
                        chunk(i, 0)
                        chunk(i, 1)
                    pe.wait_ge(gu_lo_done, c0 + n)
                    if part:
                        pe.wait_ge(y_out, 8)
                    for q in range(n // 2):
                        m = base + n + q
                        pe.wait_ge(ws.lo_done, m + 1)
                        for bank in range(8):
                            i, half = bank // 2, bank % 2
                            for f in range(2):
                                k = 2 * q + f
                                tok = slice(i * P, (i + 1) * P)
                                ins = split_products(nc, b.ps[:, bank, :], (gu_hi[:, k, tok], gu_lo[:, k, tok]),
                                                     ws.parts(m % 2, f * D + half * 512, 512), k == 0, k == n - 1)
                            if bank == 7:
                                ins.then_inc(ws.used, 1)
                            elif q == n // 2 - 1:
                                ins.then_inc(y_up, 1)


def ffn(nc, b, tag, scale_at, shift_at, w_gate, w_up, w_down, row):
    with ExitStack() as own:
        h_hi, h_lo = b.split_pair(own, f"{tag}_h", DC)
        stage_norm_turn(nc, b, f"{tag}_nt", scale_at, shift_at, h_hi, h_lo)
        stage_swiglu(nc, b, tag, w_gate, w_up, w_down, h_hi, h_lo)
    stage_post_norm(nc, b, f"{tag}_pn", row)


def stage_project(nc, b, tag, jobs, slot_k, slots=2):
    with ExitStack() as own:
        w = own.enter_context(nc.sbuf_tensor(f"{tag}_w", [P, slots, slot_k, 512], F32))
        w_in = [b.sem(f"{tag}_w_in{j}") for j in range(slots)]
        up = b.sem(f"{tag}_up")
        out_act = b.sem(f"{tag}_out_act")
        out_dve = b.sem(f"{tag}_out_dve")
        acts = [i for i in range(TT) if i % 2 == 0]
        with nc.Block() as block:
            @block.sync
            def _(sp):
                for n, (src, nk, _l, _s) in enumerate(jobs):
                    if n >= slots:
                        sp.wait_ge(up, (n - slots + 1) * TT)
                    width = src.shape[-1]
                    sp.dma_start(w[:, n % slots, 0:nk, 0:width],
                                 src.rearrange("(k p) n -> p k n", p=P)).then_inc(w_in[n % slots], 16)

            @block.tensor
            def _(pe):
                for n, (src, nk, lhsT, _s) in enumerate(jobs):
                    width = src.shape[-1]
                    pe.wait_ge(w_in[n % slots], 16 * (n // slots + 1))
                    for i in range(TT):
                        bank = (n % 2) * TT + i
                        if n >= 2:
                            pe.wait_ge(out_act if i in acts else out_dve, (n - 2) * 2 + i // 2 + 1)
                        for k in range(nk):
                            ins = mm(nc, b.ps[:, bank, 0:width], lhsT(k, i), w[:, n % slots, k, 0:width],
                                     k == 0, k == nk - 1)
                        ins.then_inc(up, 1)

            @block.scalar
            def _(act):
                for n, (src, _n, _l, stores) in enumerate(jobs):
                    for i in acts:
                        act.wait_ge(up, n * TT + i + 1)
                        for dst, ps in stores(i, b.ps[:, (n % 2) * TT + i, 0:src.shape[-1]]):
                            ins = nc.scalar.activation(dst, ps, ACT.Copy)
                        ins.then_inc(out_act, 1)

            @block.vector
            def _(dve):
                for n, (src, _n, _l, stores) in enumerate(jobs):
                    for i in range(TT):
                        if i in acts:
                            continue
                        dve.wait_ge(up, n * TT + i + 1)
                        for dst, ps in stores(i, b.ps[:, (n % 2) * TT + i, 0:src.shape[-1]]):
                            ins = nc.vector.tensor_copy(dst, ps)
                        ins.then_inc(out_dve, 1)


def stage_project_split(nc, b, tag, jobs, raw, add_row=None):
    HALF = DC // 2
    with ExitStack() as own:
        ws = WeightStream(nc, b, own, tag, raw)
        up = b.sem(f"{tag}_up")
        out_act = b.sem(f"{tag}_out_act")
        out_dve = b.sem(f"{tag}_out_dve")
        n_slots = 2 * len(jobs)
        width = [job[0].shape[-1] for job in jobs]

        def wait_up(eng, n, i):
            if i < TT - 1:
                eng.wait_ge(up, n * (TT - 1) + i + 1)
            else:
                eng.wait_ge(ws.used, 2 * n + 2)

        def gate(dve, n):
            at = slice(n * 512, (n + 1) * 512)
            for i in range(TT):
                wait_up(dve, n, i)
                nc.vector.tensor_tensor(b.tok[:, i, at], b.ps[:, n * TT + i, :], b.rows[:, add_row, at],
                                        ALU.mult).then_inc(out_dve, 1)

        def evacuate(eng, n, mine, copy, out):
            for i in mine:
                wait_up(eng, n, i)
                for dst, ps in jobs[n][2](i, b.ps[:, (n % 2) * TT + i, 0:width[n]]):
                    ins = copy(dst, ps)
                ins.then_inc(out, 1)

        with nc.Block() as block:
            @block.sync
            def _(sp):
                for m in range(n_slots):
                    src = jobs[m // 2][0].rearrange("(k p) n -> p k n", p=P)
                    ws.load(sp, m, m % 2, [(0, HALF, src[:, (m % 2) * HALF:(m % 2 + 1) * HALF, :])], m < 2)

            @block.scalar
            def _(act):
                for m in range(n_slots + 2):
                    if m < n_slots:
                        ws.round(act, m, m % 2, 16 * (m // 2 + 1), HALF * width[m // 2], m < 2)
                    if m >= 2 and m % 2 == 0 and add_row is None:
                        evacuate(act, m // 2 - 1, (0, 2), lambda dst, ps: nc.scalar.activation(dst, ps, ACT.Copy), out_act)

            @block.vector
            def _(dve):
                for m in range(n_slots + 2):
                    if m < n_slots:
                        ws.rest(dve, m, m % 2, HALF * width[m // 2])
                    if m >= 2 and m % 2 == 0:
                        if add_row is None:
                            evacuate(dve, m // 2 - 1, (1, 3), nc.vector.tensor_copy, out_dve)
                        else:
                            gate(dve, m // 2 - 1)

            if add_row is not None:
                @block.gpsimd
                def _(pool):
                    for n in range(len(jobs)):
                        at = slice(n * 512, (n + 1) * 512)
                        for i in range(TT):
                            pool.wait_ge(out_dve, n * TT + i + 1)
                            nc.gpsimd.tensor_tensor(b.x[:, i, at], b.x[:, i, at], b.tok[:, i, at], ALU.add)

            @block.tensor
            def _(pe):
                for m in range(n_slots):
                    n, half = m // 2, m % 2
                    w = width[n]
                    pe.wait_ge(ws.lo_done, m + 1)
                    for i in range(TT):
                        if half == 0 and n >= 2:
                            pe.wait_ge(out_act if i % 2 == 0 else out_dve, (n - 2) * 2 + i // 2 + 1)
                        for k in range(HALF):
                            ins = split_products(nc, b.ps[:, (n % 2) * TT + i, 0:w], jobs[n][1](half * HALF + k, i),
                                                 ws.parts(m % 2, k * w, w), half == 0 and k == 0,
                                                 half == 1 and k == HALF - 1)
                        if i == TT - 1:
                            ins.then_inc(ws.used, 1)
                        elif half:
                            ins.then_inc(up, 1)


def stage_turn(nc, b, tag, jobs):
    NB = 8
    turned = b.sem(f"{tag}_turned")
    out_act = b.sem(f"{tag}_out_act")
    out_dve = b.sem(f"{tag}_out_dve")
    with nc.Block() as block:
        @block.tensor
        def _(pe):
            ident = b.const("identity")
            for n, (src, f, _d, _s) in enumerate(jobs):
                if n >= NB:
                    pe.wait_ge(out_act if n % 2 == 0 else out_dve, (n - NB) // 2 + 1)
                for i in range(TT):
                    ins = nc.tensor.transpose(b.ps[0:f, n % NB, i * P:(i + 1) * P], src(i), ident)
                ins.then_inc(turned, 1)

        @block.scalar
        def _(act):
            for n, (_src, f, dst, scale) in enumerate(jobs):
                if n % 2 == 0:
                    act.wait_ge(turned, n + 1)
                    nc.scalar.activation(dst, b.ps[0:f, n % NB, :], ACT.Copy,
                                         scale=1.0 if scale is None else scale).then_inc(out_act, 1)

        @block.vector
        def _(dve):
            for n, (_src, f, dst, scale) in enumerate(jobs):
                if n % 2:
                    dve.wait_ge(turned, n + 1)
                    if scale is None:
                        ins = nc.vector.tensor_copy(dst, b.ps[0:f, n % NB, :])
                    else:
                        ins = nc.vector.tensor_scalar(dst, b.ps[0:f, n % NB, :], scale, None, ALU.mult)
                    ins.then_inc(out_dve, 1)


def stage_norm_rope(nc, b, tag, norms, ropes, copies=(), decays=()):
    with ExitStack() as own:
        size = 768
        tmp = own.enter_context(nc.sbuf_tensor(f"{tag}_tmp", [P, 4, size], F32))
        stat = own.enter_context(nc.sbuf_tensor(f"{tag}_stat", [P, max(1, len(norms)), TT], F32))
        squares = b.sem(f"{tag}_squares")
        chain = b.sem(f"{tag}_chain")
        first = b.sem(f"{tag}_first_half")
        second = b.sem(f"{tag}_second_half")
        done = b.sem(f"{tag}_rope_done")
        pool_chain = b.sem(f"{tag}_pool_chain")
        rooted = b.sem(f"{tag}_rooted")

        def view(t, like):
            a, c = like.shape[1], like.shape[2]
            return tmp[:, t, 0:a * c].rearrange("p (a c) -> p a c", c=c)

        with nc.Block() as block:
            @block.scalar
            def _(act):
                for n, (t, w) in enumerate(norms):
                    for i in range(TT):
                        nc.scalar.activation(b.ps[:, n * TT + i, 0:w], t(i), ACT.Square,
                                             accum_out=stat[:, n, i:i + 1]).then_inc(squares, 1)
                for n, (t, w) in enumerate(norms):
                    root_mean(nc, b, act, stat[:, n, :], w, squares, TT * len(norms), rooted)

            @block.vector
            def _(dve):
                link = Chain(dve, chain)
                for n, (x1, x2, cos, sin) in enumerate(ropes):
                    link(nc.vector.tensor_tensor(view(0, x1), x1, cos, ALU.mult))
                    nc.vector.tensor_tensor(view(1, x1), x2, sin, ALU.mult).then_inc(first, 1)
                    dve.wait_ge(first, n + 1)
                    dve.wait_ge(second, n + 1)
                    link(nc.vector.tensor_tensor(x1, view(0, x1), view(1, x1), ALU.subtract))
                for n, (t, w) in enumerate(norms):
                    dve.wait_ge(rooted, n + 1)
                    link(nc.vector.reciprocal(stat[:, n, :], stat[:, n, :]))
                    for i in range(TT):
                        nc.vector.tensor_scalar(t(i), t(i), stat[:, n, i:i + 1], None, ALU.mult)
                if copies or decays:
                    dve.wait_ge(done, len(ropes))
                for dst, src in copies:
                    nc.vector.tensor_copy(dst, src)
                for t, factors in decays:
                    nc.vector.tensor_tensor(t, t, factors, ALU.mult)

            @block.gpsimd
            def _(pool):
                link = Chain(pool, pool_chain)
                for n, (x1, x2, cos, sin) in enumerate(ropes):
                    link(nc.gpsimd.tensor_tensor(view(2, x1), x2, cos, ALU.mult))
                    nc.gpsimd.tensor_tensor(view(3, x1), x1, sin, ALU.mult).then_inc(second, 1)
                    pool.wait_ge(first, n + 1)
                    pool.wait_ge(second, n + 1)
                    nc.gpsimd.tensor_tensor(x2, view(2, x1), view(3, x1), ALU.add).then_inc(done, 1)
                    pool.wait_ge(done, n + 1)


def stage_attention(nc, b, tag, items, width, scale):
    N = len(items)
    with ExitStack() as own:
        neg = own.enter_context(nc.sbuf_tensor(f"{tag}_neg", [P, 2, width], F32))
        prob = own.enter_context(nc.sbuf_tensor(f"{tag}_prob", [P, 2, width], F32))
        prob_t = own.enter_context(nc.sbuf_tensor(f"{tag}_prob_t", [P, 2, width], F32))
        neg_max = own.enter_context(nc.sbuf_tensor(f"{tag}_neg_max", [P, N], F32))
        total = own.enter_context(nc.sbuf_tensor(f"{tag}_total", [P, N], F32))
        inverse = own.enter_context(nc.sbuf_tensor(f"{tag}_inverse", [P, N], F32))
        score_up = b.sem(f"{tag}_score_up")
        biased = b.sem(f"{tag}_biased")
        exp_done = b.sem(f"{tag}_exp_done")
        prob_up = b.sem(f"{tag}_prob_turned")
        prob_out = b.sem(f"{tag}_prob_t_out")
        inverted = b.sem(f"{tag}_inverted")
        value_up = b.sem(f"{tag}_value_up")
        value_out = b.sem(f"{tag}_value_out")
        flat = b.ps[:, :, :].rearrange("p k n -> p (k n)")

        def score_ps(n):
            return flat[:, (n % 2) * 1024:(n % 2) * 1024 + 1024]

        turn_ps = flat[:, 2048:3072]

        def value_ps(n):
            return b.ps[:, 6 + n % 2, 0:DV]

        with nc.Block() as block:
            @block.tensor
            def _(pe):
                ident = b.const("identity")

                def scores(n):
                    if n >= 2:
                        pe.wait_ge(biased, n - 1)
                    for col, lhsT, rhs in items[n][0]:
                        ins = mm(nc, score_ps(n)[:, col:col + rhs.shape[-1]], lhsT, rhs, True, True)
                    ins.then_inc(score_up, 1)

                def turn(n):
                    pe.wait_ge(exp_done, n + 1)
                    if n >= 1:
                        pe.wait_ge(prob_out, n)
                    for k in range(items[n][2] // P):
                        ins = nc.tensor.transpose(turn_ps[:, k * P:(k + 1) * P], prob[:, n % 2, k * P:(k + 1) * P], ident)
                    ins.then_inc(prob_up, 1)

                def values(n):
                    pe.wait_ge(prob_out, n + 1)
                    if n >= 2:
                        pe.wait_ge(value_out, n - 1)
                    rhs = items[n][3]
                    for k in range(len(rhs)):
                        ins = mm(nc, value_ps(n), prob_t[:, n % 2, k * P:(k + 1) * P], rhs[k], k == 0, k == len(rhs) - 1)
                    ins.then_inc(value_up, 1)

                for n in range(N + 2):
                    if n < N:
                        scores(n)
                    if 0 <= n - 1 < N:
                        turn(n - 1)
                    if 0 <= n - 2:
                        values(n - 2)

            @block.vector
            def _(dve):
                for n in range(N + 1):
                    if n < N:
                        _p, bias, w, _v, _d = items[n]
                        dve.wait_ge(score_up, n + 1)
                        if n >= 2:
                            dve.wait_ge(exp_done, n - 1)
                        nc.vector.tensor_tensor_reduce(neg[:, n % 2, 0:w], score_ps(n)[:, 0:w], bias, -scale, 3e38,
                                                       ALU.add, ALU.min, neg_max[:, n:n + 1]).then_inc(biased, 1)
                    if n >= 1:
                        m = n - 1
                        dve.wait_ge(exp_done, m + 1)
                        nc.vector.reciprocal(inverse[:, m:m + 1], total[:, m:m + 1]).then_inc(inverted, 1)
                        if m % 2 == 0:
                            w = items[m][2]
                            dve.wait_ge(prob_up, m + 1)
                            if m >= 2:
                                dve.wait_ge(value_up, m - 1)
                            nc.vector.tensor_copy(prob_t[:, m % 2, 0:w], turn_ps[:, 0:w]).then_inc(prob_out, 1)

            @block.scalar
            def _(act):
                for n in range(N + 2):
                    if n < N:
                        w = items[n][2]
                        act.wait_ge(biased, n + 1)
                        if n >= 2:
                            act.wait_ge(prob_up, n - 1)
                        nc.scalar.activation(prob[:, n % 2, 0:w], neg[:, n % 2, 0:w], ACT.Exp, bias=neg_max[:, n:n + 1],
                                             scale=-1.0, accum_out=total[:, n:n + 1]).then_inc(exp_done, 1)
                    m = n - 1
                    if 0 <= m < N and m % 2 == 1:
                        w = items[m][2]
                        act.wait_ge(prob_up, m + 1)
                        if m >= 2:
                            act.wait_ge(value_up, m - 1)
                        nc.scalar.activation(prob_t[:, m % 2, 0:w], turn_ps[:, 0:w], ACT.Copy).then_inc(prob_out, 1)
                    m = n - 2
                    if m >= 0:
                        act.wait_ge(value_up, m + 1)
                        act.wait_ge(inverted, m + 1)
                        nc.scalar.activation(items[m][4], value_ps(m), ACT.Copy,
                                             scale=inverse[:, m:m + 1]).then_inc(value_out, 1)


def stage_select(nc, b, q_idx_t, k_idx_t, w_idx, bias):
    FILL, TAKEN = -1e37, -3e38
    items = [(i, h) for i in range(1, TT) for h in range(HEADS)]
    with ExitStack() as own:
        relu = own.enter_context(nc.sbuf_tensor("idx_relu", [P, 2, S], F32))
        score = own.enter_context(nc.sbuf_tensor("idx_score", [P, TT, S], F32))
        best = own.enter_context(nc.sbuf_tensor("idx_best", [P, 2, 8], F32))
        up = b.sem("idx_up")
        relu_done = b.sem("idx_relu_done")
        added = b.sem("idx_added")
        chain = b.sem("idx_chain")
        with nc.Block() as block:
            @block.tensor
            def _(pe):
                for n, (i, h) in enumerate(items):
                    if n >= 4:
                        pe.wait_ge(relu_done, n - 3)
                    at = 32 * (h % 4)
                    mm(nc, b.ps[:, n % 4, 0:(i + 1) * P], q_idx_t[at:at + 32, h // 4, i * P:(i + 1) * P],
                       k_idx_t[at:at + 32, 0:(i + 1) * P], True, True).then_inc(up, 1)

            @block.scalar
            def _(act):
                for n, (i, h) in enumerate(items):
                    act.wait_ge(up, n + 1)
                    if n >= 2:
                        act.wait_ge(added, n - 1)
                    nc.scalar.activation(relu[:, n % 2, 0:(i + 1) * P], b.ps[:, n % 4, 0:(i + 1) * P], ACT.Relu,
                                         scale=IDX ** -0.5).then_inc(relu_done, 1)

            @block.vector
            def _(dve):
                link = Chain(dve, chain)
                causal = b.const("causal_bias")
                for n, (i, h) in enumerate(items):
                    w = (i + 1) * P
                    dve.wait_ge(relu_done, n + 1)
                    if h:
                        dve.wait_ge(added, n)
                        ins = nc.vector.scalar_tensor_tensor(score[:, i, 0:w], relu[:, n % 2, 0:w], w_idx(i, h),
                                                             score[:, i, 0:w], ALU.mult, ALU.add)
                    else:
                        ins = nc.vector.tensor_scalar(score[:, i, 0:w], relu[:, n % 2, 0:w], w_idx(i, h), None, ALU.mult)
                    ins.then_inc(added, 1)
                dve.wait_ge(added, len(items))
                nc.vector.tensor_copy(bias[:, 0, 0:P], causal)
                for i in range(1, TT):
                    link(nc.vector.scalar_tensor_tensor(score[:, i, i * P:(i + 1) * P], causal, FILL / NEG,
                                                        score[:, i, i * P:(i + 1) * P], ALU.mult, ALU.add))
                for r in range(TOPK // 8):
                    for i in range(1, TT):
                        w = (i + 1) * P
                        link(nc.vector.max(best[:, r % 2, :], score[:, i, 0:w]))
                        link(nc.vector.match_replace(score[:, i, 0:w], best[:, r % 2, :], score[:, i, 0:w], TAKEN))
                for i in range(1, TT):
                    w = (i + 1) * P
                    nc.vector.tensor_scalar(bias[:, i, 0:w], score[:, i, 0:w], -2e38, NEG, ALU.is_gt, ALU.mult)


def stage_gated_up(nc, b, d, h, o_a, o_b, z):
    w_in_v = d["w_in"].rearrange("a (k p) n -> p (a k) n", p=P)
    up_a = d["w_up_a"].rearrange("a (k p) n -> p (a k) n", p=P)
    up_b = d["w_up_b"].rearrange("a (k p) n -> p (a k) n", p=P)
    KA, KB = o_a[0].shape[1], o_b[0].shape[1]
    with ExitStack() as own:
        ws = WeightStream(nc, b, own, "gated", b.feat_slots)
        sig = b.tok[:, 0:2, :].rearrange("p j (g n) -> p j g n", g=2)
        part = b.tok[:, 2:4, :].rearrange("p j (g n) -> p j g n", g=2)
        sig_done = b.sem("gated_sig")
        read = b.sem("gated_read")
        z_sum = b.sem("gated_z_sum")
        z_hi_done = b.sem("gated_z_hi")
        z_done = b.sem("gated_z")
        with nc.Block() as block:
            @block.sync
            def _(sp):
                for m in range(DC):
                    ws.load(sp, 2 * m, 0, [(g * DC * P, DC, w_in_v[:, :, C_GATE + g * D + m * P:C_GATE + g * D + (m + 1) * P])
                                           for g in range(2)], m == 0)
                    ws.load(sp, 2 * m + 1, 1, [(0, KA, up_a[:, :, m * P:(m + 1) * P]),
                                               (KA * P, KB, up_b[:, :, m * P:(m + 1) * P])], m == 0)

            @block.tensor
            def _(pe):
                for m in range(DC):
                    bank = 4 * (m % 2)
                    pe.wait_ge(ws.lo_done, 2 * m + 1)
                    if m >= 2:
                        pe.wait_ge(read, 2 * (m - 1))
                    for g in range(2):
                        for k in range(DC):
                            ins = split_products(nc, b.ps[:, bank + g, :], ws.parts(0, (g * DC + k) * P, P),
                                                 (h[0][:, k, :], h[1][:, k, :]), k == 0, k == DC - 1)
                    ins.then_inc(ws.used, 1)
                    pe.wait_ge(ws.lo_done, 2 * m + 2)
                    for g, (o, k0, kn) in enumerate(((o_a, 0, KA), (o_b, KA, KB))):
                        for k in range(kn):
                            ins = split_products(nc, b.ps[:, bank + 2 + g, :], ws.parts(1, (k0 + k) * P, P),
                                                 (o[0][:, k, :], o[1][:, k, :]), k == 0, k == kn - 1)
                    ins.then_inc(ws.used, 1)

            @block.scalar
            def _(act):
                ws.round(act, 0, 0, 32, first=True)
                ws.round(act, 1, 1, 32, (KA + KB) * P, first=True)
                for m in range(DC):
                    j = m % 2
                    if m + 1 < DC:
                        ws.round(act, 2 * m + 2, 0, 32 * (m + 2))
                    act.wait_ge(ws.used, 2 * m + 1)
                    if m >= 2:
                        act.wait_ge(read, 2 * (m - 1))
                    nc.scalar.activation(sig[:, j, :, :], b.ps[:, 4 * j:4 * j + 2, :], ACT.Sigmoid).then_inc(sig_done, 1)
                    if m + 1 < DC:
                        ws.round(act, 2 * m + 3, 1, 32 * (m + 2), (KA + KB) * P)
                    act.wait_ge(z_sum, m + 1)
                    nc.scalar.activation(z[0][:, m, :], part[:, j, 0, :], ACT.Copy).then_inc(z_hi_done, 1)

            @block.vector
            def _(dve):
                ws.rest(dve, 0, 0)
                ws.rest(dve, 1, 1, (KA + KB) * P)
                for m in range(DC):
                    j = m % 2
                    if m + 1 < DC:
                        ws.rest(dve, 2 * m + 2, 0)
                        ws.rest(dve, 2 * m + 3, 1, (KA + KB) * P)
                    dve.wait_ge(sig_done, m + 1)
                    dve.wait_ge(ws.used, 2 * m + 2)
                    if m >= 2:
                        dve.wait_ge(z_done, m - 1)
                    for g in range(2):
                        nc.vector.tensor_tensor(part[:, j, g, :], sig[:, j, g, :], b.ps[:, 4 * j + 2 + g, :],
                                                ALU.mult).then_inc(read, 1)

            @block.gpsimd
            def _(pool):
                for m in range(DC):
                    z_m = part[:, m % 2, 0, :]
                    pool.wait_ge(read, 2 * (m + 1))
                    nc.gpsimd.tensor_tensor(z_m, z_m, part[:, m % 2, 1, :], ALU.add).then_inc(z_sum, 1)
                    pool.wait_ge(z_sum, m + 1)
                    pool.wait_ge(z_hi_done, m + 1)
                    nc.gpsimd.tensor_tensor(z[1][:, m, :], z_m, z[0][:, m, :], ALU.subtract).then_inc(z_done, 1)


def stage_retention(nc, b, q_t, k_t, v, y):
    with ExitStack() as own:
        kept = own.enter_context(nc.sbuf_tensor("ret_scores", [P, 2, TT, S], F32))
        up = b.sem("ret_up")
        out = b.sem("ret_out")
        y_up = b.sem("ret_y_up")
        y_out = b.sem("ret_y_out")
        mask = b.const("decay_mask")
        with nc.Block() as block:
            @block.tensor
            def _(pe):
                def scores(h):
                    at = DH * (h % 2)
                    for j in range(TT):
                        n = h * TT + j
                        if n >= 4:
                            pe.wait_ge(out, n - 3)
                        w = S - j * P
                        mm(nc, b.ps[:, j, 0:w], k_t[at:at + DH, h // 2, j * P:(j + 1) * P],
                           q_t[at:at + DH, h // 2, j * P:S], True, True).then_inc(up, 1)

                def sums(h):
                    pe.wait_ge(out, (h + 1) * TT)
                    if h >= 2:
                        pe.wait_ge(y_out, h - 1)
                    for i in range(TT):
                        for j in range(i + 1):
                            ins = mm(nc, b.ps[:, 4 + h % 2, i * DH:(i + 1) * DH],
                                     kept[:, h % 2, j, (i - j) * P:(i - j + 1) * P], v[:, j, h * DH:(h + 1) * DH],
                                     j == 0, j == i)
                    ins.then_inc(y_up, 1)

                for h in range(HEADS + 1):
                    if h < HEADS:
                        scores(h)
                    if h:
                        sums(h - 1)

            @block.vector
            def _(dve):
                for h in range(HEADS):
                    if h >= 2:
                        dve.wait_ge(y_up, h - 1)
                    for j in range(TT):
                        w = S - j * P
                        dve.wait_ge(up, h * TT + j + 1)
                        nc.vector.tensor_tensor(kept[:, h % 2, j, 0:w], b.ps[:, j, 0:w], mask[:, 0:w],
                                                ALU.mult).then_inc(out, 1)

            @block.scalar
            def _(act):
                for h in range(HEADS):
                    act.wait_ge(y_up, h + 1)
                    nc.scalar.activation(y[:, :, h * DH:(h + 1) * DH],
                                         b.ps[:, 4 + h % 2, 0:TT * DH].rearrange("p (i c) -> p i c", c=DH),
                                         ACT.Copy).then_inc(y_out, 1)


def stage_retention_norm(nc, b, y, gate):
    with ExitStack() as own:
        sq = b.tok
        mean = own.enter_context(nc.sbuf_tensor("ret_mean", [P, TT * HEADS], F32))
        var = own.enter_context(nc.sbuf_tensor("ret_var", [P, TT * HEADS], F32))
        chain = b.sem("ret_norm_chain")
        silu_done = b.sem("ret_silu")
        squares = b.sem("ret_squares")
        rooted = b.sem("ret_rooted")
        y3 = y[:, :, :].rearrange("p i (h c) -> p (i h) c", c=DH)
        s3 = sq[:, :, 0:RW].rearrange("p i (h c) -> p i h c", c=DH)
        y4 = y[:, :, :].rearrange("p i (h c) -> p i h c", c=DH)
        full = [P, TT * HEADS, DH]
        with nc.Block() as block:
            @block.scalar
            def _(act):
                nc.scalar.activation(gate, gate, ACT.Silu).then_inc(silu_done, 1)
                root_mean(nc, b, act, mean[:, :], DH, squares, 1, rooted)

            @block.vector
            def _(dve):
                link = Chain(dve, chain)
                link(nc.vector.tensor_reduce(mean[:, :], y3, AX.X, ALU.add))
                link(nc.vector.tensor_scalar(mean[:, :], mean[:, :], 1.0 / DH, None, ALU.mult))
                link(nc.vector.tensor_tensor(y3, y3, mean[:, :].unsqueeze(2).to_broadcast(full), ALU.subtract))
                link(nc.vector.tensor_tensor(s3, y4, y4, ALU.mult))
                link(nc.vector.tensor_reduce(var[:, :].rearrange("p (i h) -> p i h", h=HEADS), s3, AX.X, ALU.add))
                nc.vector.tensor_copy(mean[:, :], var[:, :]).then_inc(squares, 1)
                dve.wait_ge(rooted, 1)
                link(nc.vector.reciprocal(mean[:, :], mean[:, :]))
                link(nc.vector.tensor_tensor(y3, y3, mean[:, :].unsqueeze(2).to_broadcast(full), ALU.mult))
                dve.wait_ge(silu_done, 1)
                link(nc.vector.tensor_tensor(gate, gate, y[:, :, :], ALU.mult))


def stage_key_scores(nc, b, d, q_t, s):
    G = 2 * PH
    with ExitStack() as own:
        keys = own.enter_context(nc.sbuf_tensor("peer_keys", [NKEY, 2, KH], F32))
        keys_t = own.enter_context(nc.sbuf_tensor("peer_keys_t", [KH, 2, NKEY], F32))
        keys_in = b.sem("peer_keys_in")
        keys_up = b.sem("peer_keys_up")
        keys_out = b.sem("peer_keys_out")
        s_up = b.sem("peer_s_up")
        s_out = b.sem("peer_s_out")
        with nc.Block() as block:
            @block.sync
            def _(sp):
                sp.dma_start(keys[:, :, :], d["sub_keys_2"].rearrange("a g k c -> k (a g) c")).then_inc(keys_in, 16)

            @block.tensor
            def _(pe):
                pe.wait_ge(keys_in, 16)
                for g in range(2):
                    ins = nc.tensor.transpose(b.ps[:, 0, g * P:(g + 1) * P], keys[:, g, :], b.const("identity"))
                ins.then_inc(keys_up, 1)
                pe.wait_ge(keys_out, 1)
                for n in range(4 * TT):
                    if n >= 4:
                        pe.wait_ge(s_out, n - 3)
                    i, q = n // 4, n % 4
                    for g in range(4 * q, 4 * q + 4):
                        ins = mm(nc, b.ps[:, 4 + q, (g % 4) * P:(g % 4 + 1) * P], q_t[:, g, i * P:(i + 1) * P],
                                 keys_t[:, g % 2, :], True, True)
                    ins.then_inc(s_up, 1)

            @block.scalar
            def _(act):
                act.wait_ge(keys_up, 1)
                nc.scalar.activation(keys_t[:, :, :].rearrange("p g k -> p (g k)"), b.ps[:, 0, 0:2 * P],
                                     ACT.Copy).then_inc(keys_out, 1)
                for n in range(4 * TT):
                    i, q = n // 4, n % 4
                    act.wait_ge(s_up, n + 1)
                    nc.scalar.activation(s[:, i, 4 * q:4 * q + 4, :].rearrange("p g k -> p (g k)"),
                                         b.ps[:, 4 + q, :], ACT.Copy).then_inc(s_out, 1)


def stage_experts(nc, b, d, s):
    G = 2 * PH
    R = 8
    NE = PH * PK
    STEPS = NE // R
    u_rows = d["expert_u_2"].rearrange("a e n -> (a e) n")
    v_rows = d["expert_v_2"].rearrange("a e n -> (a e) n")
    h2 = b.tok
    with ExitStack() as own:
        def sb(name, shape, dt=F32):
            return own.enter_context(nc.sbuf_tensor(name, shape, dt))

        expert = sb("expert", [P, TT, NE], U32)
        weight = sb("expert_weight", [P, TT, NE])
        top = sb("peer_top", [P, G, PK])
        top_i = sb("peer_top_i", [P, G, PK], U32)
        top_f = sb("peer_top_f", [P, G, PK])
        cand = sb("peer_cand", [P, PH, PK, PK])
        hot = cand
        best = sb("peer_best", [P, PH, PK])
        pos = sb("peer_pos", [P, PH, PK], U32)
        part_i = sb("peer_part_i", [P, 2, PH, PK], U32)
        part_f = sb("peer_part_f", [P, 2, PH, PK])
        chosen = sb("peer_chosen", [P, 2, PH, PK])
        sums = sb("peer_sums", [P, 2 * PH])
        u = sb("u_rows", [P, R, D])
        v = sb("v_rows", [P, R, D])
        dots = sb("peer_dots", [P, NE])
        dot_cells = sb("peer_dot_cells", [P, R])
        act_w = sb("peer_act_w", [P, 2, NE])
        diag = sb("peer_diag", [P, 4, P])
        u_in = [b.sem(f"u_in{r}") for r in range(R)]
        v_in = [b.sem(f"v_in{r}") for r in range(R)]
        chain = b.sem("peer_route_chain")
        routed = b.sem("peer_routed")
        dot_done = b.sem("dot_done")
        dots_kept = b.sem("dots_kept")
        gelu_done = b.sem("gelu_done")
        act_w_done = b.sem("act_w_done")
        diag_done = b.sem("diag_done")
        v_used = b.sem("v_used")
        y_out = b.sem("peer_y_out")
        with nc.Block() as block:
            @block.gpsimd
            def _(pool):
                def gather(i, k, rows, table, arrived, used):
                    r = k % R
                    if i * NE + k >= R:
                        pool.wait_ge(used, i * NE + k - R + 1)
                    nc.gpsimd.indirect_dma_start(
                        out=rows[:, r, :], out_offset=None, in_=table,
                        in_offset=bass.IndirectOffsetOnAxis(ap=expert[:, i, k:k + 1], axis=0),
                    ).then_inc(arrived[r], 16)

                for i in range(-1, TT):
                    if i + 1 < TT:
                        pool.wait_ge(routed, i + 2)
                    for k in range(NE):
                        if i + 1 < TT:
                            gather(i + 1, k, u, u_rows, u_in, dot_done)
                        if i >= 0:
                            gather(i, k, v, v_rows, v_in, v_used)

            @block.vector
            def _(dve):
                link = Chain(dve, chain)

                def best_keys(i):
                    for half in range(2):
                        at = slice(8 * half, 8 * half + 8)
                        for g in range(G):
                            ins = nc.vector.max(top[:, g, at], s[:, i, g, :])
                        link(ins)
                        for g in range(G):
                            ins = nc.vector.max_index(top_i[:, g, at], top[:, g, at], s[:, i, g, :])
                        link(ins)
                        if half == 0:
                            for g in range(G):
                                ins = nc.vector.match_replace(s[:, i, g, :], top[:, g, at], s[:, i, g, :], -3e38)
                            link(ins)
                    link(nc.vector.tensor_copy(top_f[:, :, :], top_i[:, :, :]))

                def best_pairs(i):
                    for h in range(PH):
                        a = top[:, 2 * h, :].unsqueeze(2).to_broadcast([P, PK, PK])
                        c = top[:, 2 * h + 1, :].unsqueeze(1).to_broadcast([P, PK, PK])
                        ins = nc.vector.tensor_tensor(cand[:, h, :, :], a, c, ALU.add)
                    link(ins)
                    rows = [cand[:, h, :, :].rearrange("p a c -> p (a c)") for h in range(PH)]
                    for half in range(2):
                        at = slice(8 * half, 8 * half + 8)
                        for h in range(PH):
                            ins = nc.vector.max(best[:, h, at], rows[h])
                        link(ins)
                        for h in range(PH):
                            ins = nc.vector.max_index(pos[:, h, at], best[:, h, at], rows[h])
                        link(ins)
                        if half == 0:
                            for h in range(PH):
                                ins = nc.vector.match_replace(rows[h], best[:, h, at], rows[h], -3e38)
                            link(ins)
                    nc.vector.tensor_scalar(part_i[:, 0, :, :], pos[:, :, :], 4, None, ALU.logical_shift_right)
                    link(nc.vector.tensor_scalar(part_i[:, 1, :, :], pos[:, :, :], PK - 1, None, ALU.bitwise_and))
                    link(nc.vector.tensor_copy(part_f[:, :, :, :], part_i[:, :, :, :]))
                    iota = b.const("iota").unsqueeze(1).to_broadcast([P, PH * PK, PK])
                    hot3 = hot[:, :, :, :].rearrange("p h k c -> p (h k) c")
                    for g in range(2):
                        rank = part_f[:, g, :, :].rearrange("p h k -> p (h k)").unsqueeze(2).to_broadcast([P, PH * PK, PK])
                        link(nc.vector.tensor_tensor(hot3, rank, iota, ALU.is_equal))
                        key = top_f[:, g:G:2, :].unsqueeze(2).to_broadcast([P, PH, PK, PK])
                        link(nc.vector.tensor_tensor(hot[:, :, :, :], hot[:, :, :, :], key, ALU.mult))
                        link(nc.vector.tensor_reduce(chosen[:, g, :, :].rearrange("p h k -> p (h k)"), hot3, AX.X, ALU.add))
                    c0 = chosen[:, 0, :, :].rearrange("p h k -> p (h k)")
                    c1 = chosen[:, 1, :, :].rearrange("p h k -> p (h k)")
                    nc.vector.scalar_tensor_tensor(expert[:, i, :], c0, float(NKEY), c1, ALU.mult, ALU.add)
                    w3 = weight[:, i, :].rearrange("p (h k) -> p h k", k=PK)
                    nc.vector.tensor_tensor(w3, best[:, :, :], best[:, :, 0:1].to_broadcast([P, PH, PK]),
                                            ALU.subtract).then_inc(routed, 1)
                    dve.wait_ge(routed, i + 1)

                def dot_steps(i, first, last):
                    with dve.Fori(first, last) as t:
                        for r in range(R):
                            dve.wait_ge(u_in[r], (t + i * STEPS + 1) * 16)
                            nc.vector.tensor_tensor_reduce(u[:, r, :], u[:, r, :], h2[:, i, :], 1.0, 0.0, ALU.mult,
                                                           ALU.add, dot_cells[:, r:r + 1]).then_inc(dot_done, 1)
                        dve.wait_ge(dot_done, (t + i * STEPS + 1) * R)
                        nc.vector.tensor_copy(dots[:, bass.ds(t * R, R)], dot_cells[:, :]).then_inc(dots_kept, 1)
                        dve.wait_ge(dots_kept, t + i * STEPS + 1)

                def row_weights(i):
                    w3 = weight[:, i, :].rearrange("p (h k) -> p h k", k=PK)
                    dve.wait_ge(gelu_done, 2 * (i + 1))
                    link(nc.vector.tensor_reduce(sums[:, 0:PH], w3, AX.X, ALU.add))
                    link(nc.vector.reciprocal(sums[:, PH:2 * PH], sums[:, 0:PH]))
                    link(nc.vector.tensor_tensor(w3, w3, sums[:, PH:2 * PH].unsqueeze(2).to_broadcast([P, PH, PK]),
                                                 ALU.mult))
                    nc.vector.tensor_tensor(act_w[:, i % 2, :], act_w[:, i % 2, :], weight[:, i, :],
                                            ALU.mult).then_inc(act_w_done, 1)

                for i in range(2):
                    best_keys(i)
                    best_pairs(i)
                for i in range(TT):
                    dot_steps(i, 0, STEPS // 3)
                    if i + 2 < TT:
                        best_keys(i + 2)
                    dot_steps(i, STEPS // 3, 2 * STEPS // 3)
                    if i + 2 < TT:
                        best_pairs(i + 2)
                    dot_steps(i, 2 * STEPS // 3, STEPS)
                    row_weights(i)

            @block.scalar
            def _(act):
                def diagonals(i, t, g):
                    for r in range(2 * g, 2 * g + 2):
                        nc.scalar.activation(diag[:, r, :], b.const("identity"), ACT.Copy,
                                             scale=act_w[:, i % 2, bass.ds(t * 4 + r, 1)]).then_inc(diag_done, 1)

                for i in range(TT):
                    act.wait_ge(dots_kept, (i + 1) * STEPS)
                    nc.scalar.activation(act_w[:, i % 2, :], dots[:, :], ACT.Gelu).then_inc(gelu_done, 1)
                    nc.scalar.activation(weight[:, i, :], weight[:, i, :], ACT.Exp).then_inc(gelu_done, 1)
                    act.wait_ge(act_w_done, i + 1)
                    if i == 0:
                        diagonals(0, 0, 0)
                        diagonals(0, 0, 1)
                    with act.Fori(0 if i else 1, NE // 4) as t:
                        for g in range(2):
                            act.wait_ge(v_used, t * 4 + 2 * g + i * NE - 2)
                            diagonals(i, t, g)
                    act.wait_ge(v_used, (i + 1) * NE)
                    for half in range(2):
                        ins = nc.scalar.activation(b.tok[:, i, half * 512:half * 512 + 512],
                                                   b.ps[:, 2 * (i % 2) + half, :], ACT.Copy)
                    ins.then_inc(y_out, 1)

            @block.tensor
            def _(pe):
                def rows(t, r, i, start, stop):
                    pe.wait_ge(v_in[r], (t + i * STEPS + 1) * 16)
                    pe.wait_ge(diag_done, t * R + r + i * NE + 1)
                    for half in range(2):
                        ins = mm(nc, b.ps[:, 2 * (i % 2) + half, :], diag[:, r % 4, :],
                                 v[:, r, half * 512:half * 512 + 512], start, stop)
                    ins.then_inc(v_used, 1)

                for i in range(TT):
                    if i >= 2:
                        pe.wait_ge(y_out, i - 1)
                    for r in range(R):
                        rows(0, r, i, r == 0, False)
                    with pe.Fori(1, STEPS - 1) as t:
                        for r in range(R):
                            rows(t, r, i, False, False)
                    for r in range(R):
                        rows(STEPS - 1, r, i, False, r == R - 1)


def stage_output(nc, b, tag, w_src, o, add_row=None):
    def lhsT(k, i):
        return o[0][:, k, i * P:(i + 1) * P], o[1][:, k, i * P:(i + 1) * P]

    jobs = []
    for at in (slice(0, 512), slice(512, D)):
        jobs.append((w_src[:, at], lhsT, lambda i, ps, at=at: [(b.tok[:, i, at], ps)]))
    stage_project_split(nc, b, tag, jobs, b.feat_slots, add_row)


def stage_final(nc, b, out):
    added = b.sem("final_added")
    squares = b.sem("final_squares")
    chain = b.sem("final_chain")
    ready = b.sem("final_ready")
    rooted = b.sem("final_rooted")
    rstd = b.sem("final_rstd")
    stored = b.sem("final_stored")
    dst = out.rearrange("a (i p) n -> p (a i) n", p=P)
    with nc.Block() as block:
        @block.vector
        def _(dve):
            link = Chain(dve, chain)
            for i in range(TT):
                link(nc.vector.tensor_tensor(b.tok[:, i, :], b.tok[:, i, :], b.rows[:, 4, :], ALU.mult))
                nc.vector.tensor_tensor(b.x[:, i, :], b.x[:, i, :], b.tok[:, i, :], ALU.add).then_inc(added, 1)
            dve.wait_ge(rooted, 1)
            nc.vector.reciprocal(b.stat[:, :], b.stat[:, :]).then_inc(rstd, 1)
            dve.wait_ge(rstd, 1)
            for i in range(TT):
                nc.vector.scalar_tensor_tensor(b.tok[:, i, :], b.x[:, i, :], b.stat[:, i:i + 1], b.rows[:, 5, :],
                                               ALU.mult, ALU.mult).then_inc(ready, 1)

        @block.scalar
        def _(act):
            for i in range(TT):
                act.wait_ge(added, i + 1)
                nc.scalar.activation(b.feat[:, 2 * i:2 * i + 2, :].rearrange("p a n -> p (a n)"), b.x[:, i, :],
                                     ACT.Square, accum_out=b.stat[:, i:i + 1]).then_inc(squares, 1)
            root_mean(nc, b, act, b.stat[:, :], D, squares, TT, rooted)

        @block.sync
        def _(sp):
            for i in range(TT):
                sp.wait_ge(ready, i + 1)
                sp.dma_start(dst[:, i, :], b.tok[:, i, :]).then_inc(stored, 16)
            sp.wait_ge(stored, 16 * TT)


def cols3(t, i, c0, heads, width):
    return t[:, i, c0:c0 + heads * width].rearrange("p (h c) -> p h c", c=width)


def rope_items(b, t, heads, width, at, half, table, pos):
    out = []
    for i in range(TT):
        v = t[:, i, :].rearrange("p (h c) -> p h c", c=width)
        cos = b.cos[:, pos * TT + i, table:table + half].unsqueeze(1).to_broadcast([P, heads, half])
        sin = b.sin[:, pos * TT + i, table:table + half].unsqueeze(1).to_broadcast([P, heads, half])
        out.append((v[:, :, at:at + half], v[:, :, at + half:at + 2 * half], cos, sin))
    return out


def mixer_one(nc, b, d):
    w_in = d["w_in"].rearrange("a k n -> (a k) n")
    HQ = GRP * HB
    with ExitStack() as mix:
        latents = mix.enter_context(ExitStack())
        lat = latents.enter_context(nc.sbuf_tensor("latents", [P, TT, C_QKV], F32))
        oa_t = b.tok[:, 0:2, :].rearrange("p a (c n) -> p (a c) n", n=S)
        ob_t = b.tok[:, 2, :].rearrange("p (c n) -> p c n", n=S)
        with ExitStack() as dil:
            qk = dil.enter_context(nc.sbuf_tensor("dil_qk", [P, TT, 2 * HQ * DH], F32))
            v = dil.enter_context(nc.sbuf_tensor("dil_v", [P, TT, HQ * DH], F32))

            inner = dil.enter_context(ExitStack())
            h_hi, h_lo = b.split_pair(inner, "mix_h", DC)
            stage_norm_turn(nc, b, "nt2", 1, 3, h_hi, h_lo)

            def plain(k, i):
                return h_hi[:, k, i * P:(i + 1) * P], h_lo[:, k, i * P:(i + 1) * P]

            def strided(k, r):
                return h_hi[:, k, r:S:TT], h_lo[:, k, r:S:TT]

            jobs = []
            for at, w in ((0, 512), (512, C_QKV - 512)):
                jobs.append((w_in[:, at:at + w], plain, lambda i, ps, at=at, w=w: [(lat[:, i, at:at + w], ps)]))
            for n in range(3):
                at = C_QKV + 512 * n
                jobs.append((w_in[:, at:at + 512], plain,
                             lambda i, ps, n=n: [(qk[:, i, 512 * n:512 * n + 512], ps)]))
            for n in range(2):
                at = C_QKV + 2 * HQ * DH + 384 * n
                jobs.append((w_in[:, at:at + 384], strided,
                             lambda i, ps, n=n: [(v[:, i, 384 * n:384 * n + 384], ps)]))
            stage_project_split(nc, b, "in1", jobs, b.tok_slots)
            inner.close()

            ropes = []
            ropes += rope_items(b, qk, 2 * HQ, DH, 0, DH // 2, ROPE_A // 2, 0)
            ropes += rope_items(b, lat[:, :, C_KR:C_KR + ROPE_A], 1, ROPE_A, 0, ROPE_A // 2, 0, 0)
            ropes += rope_items(b, lat[:, :, C_KI:C_KI + IDX], 1, IDX, 0, IDX // 2, 0, 0)
            norms = [(lambda i: lat[:, i, 0:QL], QL), (lambda i: lat[:, i, C_CKV:C_CKV + KVL], KVL)]
            stage_norm_rope(nc, b, "nr1", norms, ropes)

            with ExitStack() as att:
                qk_t = att.enter_context(nc.sbuf_tensor("dil_qk_t", [P, HQ, S], F32))
                bias = att.enter_context(nc.sbuf_tensor("dil_bias", [P, TT, S + 2 * P], F32))
                o = att.enter_context(nc.sbuf_tensor("dil_o", [P, TT, HB * DH], F32))
                bias_in = b.sem("dil_bias_in")
                with nc.Block() as block:
                    @block.sync
                    def _(sp):
                        sp.dma_start(bias[:, :, :], d["dilated_bias"].rearrange("p (r n) -> p r n", r=TT)).then_inc(bias_in, 16)
                        sp.wait_ge(bias_in, 16)
                stage_turn(nc, b, "dqk", [(lambda i, n=n: qk[:, i, n * P:(n + 1) * P], P, qk_t[:, n, :], None)
                                          for n in range(HQ)])
                items = []
                for r in range(TT):
                    for h in range(HB):
                        prods, vals = [], []
                        for g in range(GRP):
                            hq = g * HB + h
                            at = DH * (hq % 2)
                            q = qk_t[at:at + DH, hq // 2, r:S:TT]
                            kc = (HQ + hq) // 2
                            if g == 0:
                                for r2 in range(TT):
                                    prods.append((r2 * P, q, qk_t[at:at + DH, kc, r2:S:TT]))
                                    vals.append(v[:, r2, hq * DH:(hq + 1) * DH])
                            else:
                                prods.append((S + (g - 1) * P, q, qk_t[at:at + DH, kc, r:S:TT]))
                                vals.append(v[:, r, hq * DH:(hq + 1) * DH])
                        items.append((prods, bias[:, r, :], S + 2 * P, vals, o[:, r, h * DH:(h + 1) * DH]))
                stage_attention(nc, b, "dil", items, S + 2 * P, DH ** -0.5)
                with nc.Block() as block:
                    o_up = b.sem("dil_o_up")

                    @block.tensor
                    def _(pe):
                        for k in range(2):
                            for r in range(TT):
                                ins = nc.tensor.transpose(b.ps[:, k, r * P:(r + 1) * P], o[:, r, k * P:(k + 1) * P],
                                                          b.const("identity"))
                            ins.then_inc(o_up, 1)

                    @block.vector
                    def _(dve):
                        for k in range(2):
                            dve.wait_ge(o_up, k + 1)
                            nc.vector.tensor_copy(ob_t[:, k, :].rearrange("p (n r) -> p r n", r=TT),
                                                  b.ps[:, k, :].rearrange("p (r n) -> p r n", r=TT))

        with ExitStack() as dsa:
            q_t = dsa.enter_context(nc.sbuf_tensor("dsa_q_t", [DQ, HEADS, S], F32))
            k_t = dsa.enter_context(nc.sbuf_tensor("dsa_k_t", [DQ, HEADS, S], F32))
            v = dsa.enter_context(nc.sbuf_tensor("dsa_v", [P, TT, HEADS * DV], F32))
            qi_t = dsa.enter_context(nc.sbuf_tensor("idx_q_t", [P, 2, S], F32))
            ki_t = dsa.enter_context(nc.sbuf_tensor("idx_k_t", [P, S], F32))
            with ExitStack() as prep:
                lat_t = prep.enter_context(nc.sbuf_tensor("lat_t", [P, 5, S], F32))
                q = prep.enter_context(nc.sbuf_tensor("dsa_q", [P, TT, HEADS * DQ], F32))
                kk = prep.enter_context(nc.sbuf_tensor("dsa_k", [P, TT, HEADS * DQ], F32))
                qi = prep.enter_context(nc.sbuf_tensor("idx_q", [P, TT, HEADS * IDX], F32))
                ki = prep.enter_context(nc.sbuf_tensor("idx_k", [P, TT, P], F32))
                gq, gkv = VEC_AT["g_cq"], VEC_AT["g_ckv"]
                jobs = [(lambda i, n=n: lat[:, i, n * P:(n + 1) * P], P, lat_t[:, n, :],
                         b.vec[:, gq + n:gq + n + 1] if n < 3 else b.vec[:, gkv + n - 3:gkv + n - 2]) for n in range(5)]
                stage_turn(nc, b, "lat1", jobs)
                w_uq = d["w_uq"].rearrange("a k h c -> (a k) (h c)")
                w_uk = d["w_uk"].rearrange("a k h c -> (a k) (h c)")
                w_uv = d["w_uv"].rearrange("a k h c -> (a k) (h c)")
                w_iq = d["w_iq"].rearrange("a k h c -> (a k) (h c)")

                def from_q(k, i):
                    return lat_t[:, k, i * P:(i + 1) * P]

                def from_kv(k, i):
                    return lat_t[:, 3 + k, i * P:(i + 1) * P]

                jobs = [(w_uq[:, n * 384:n * 384 + 384], 3, from_q,
                         lambda i, ps, n=n: [(q[:, i, n * 384:n * 384 + 384], ps)]) for n in range(2)]
                jobs.append((w_iq, 3, from_q, lambda i, ps: [(qi[:, i, :], ps)]))
                jobs.append((w_uk, 2, from_kv,
                             lambda i, ps: [(cols3(kk, i, 0, HEADS, DQ)[:, :, 0:NOPE],
                                             ps.rearrange("p (h c) -> p h c", c=NOPE))]))
                jobs.append((w_uv, 2, from_kv, lambda i, ps: [(v[:, i, :], ps)]))
                stage_project(nc, b, "uq1", jobs, 3)
                ropes = rope_items(b, q, HEADS, DQ, NOPE, ROPE_A // 2, 0, 0)
                ropes += rope_items(b, qi, HEADS, IDX, 0, IDX // 2, 0, 0)
                copies = []
                for i in range(TT):
                    copies.append((cols3(kk, i, 0, HEADS, DQ)[:, :, NOPE:DQ],
                                   lat[:, i, C_KR:C_KR + ROPE_A].unsqueeze(1).to_broadcast([P, HEADS, ROPE_A])))
                    copies.append((ki[:, i, :].rearrange("p (a c) -> p a c", c=IDX),
                                   lat[:, i, C_KI:C_KI + IDX].unsqueeze(1).to_broadcast([P, 4, IDX])))
                stage_norm_rope(nc, b, "nr2", [], ropes, copies)
                jobs = [(lambda i, n=n: qi[:, i, n * P:(n + 1) * P], P, qi_t[:, n, :], None) for n in range(2)]
                jobs.append((lambda i: ki[:, i, :], P, ki_t[:, :], None))
                for src, dst in ((q, q_t), (kk, k_t)):
                    jobs += [(lambda i, h=h, src=src: src[:, i, h * DQ:(h + 1) * DQ], DQ, dst[:, h, :], None)
                             for h in range(HEADS)]
                stage_turn(nc, b, "dsaqk", jobs)
            with ExitStack() as att:
                bias = att.enter_context(nc.sbuf_tensor("dsa_bias", [P, TT, S], F32))
                wi = att.enter_context(nc.sbuf_tensor("idx_w", [P, TT, HEADS], F32))
                with nc.Block() as block:
                    @block.vector
                    def _(dve):
                        nc.vector.tensor_scalar(wi[:, :, :], lat[:, :, C_WI:C_WI + HEADS], float(HEADS ** -0.5), None, ALU.mult)
                stage_select(nc, b, qi_t, ki_t, lambda i, h: wi[:, i, h:h + 1], bias)
                latent_attention(nc, b, "dsa", q_t, k_t, v, lambda i: bias[:, i, 0:(i + 1) * P], oa_t)
        latents.close()
        z = b.split_pair(mix, "z", DC)
        with ExitStack() as gated:
            h = b.split_pair(gated, "gated_h", DC)
            o_a = b.split_pair(gated, "branch_a", 4)
            o_b = b.split_pair(gated, "branch_b", 2)
            stage_split(nc, b, "gated_split", [(b.feat, *h), (oa_t, *o_a), (ob_t, *o_b)])
            stage_gated_up(nc, b, d, h, o_a, o_b, z)
        stage_output(nc, b, "o1", d["w_o"].rearrange("a k n -> (a k) n"), z)


def latent_attention(nc, b, tag, q_t, k_t, v, bias, o_t):
    with ExitStack() as own:
        o = own.enter_context(nc.sbuf_tensor(f"{tag}_o", [P, TT, HEADS * DV], F32))
        items = []
        for i in range(TT):
            for h in range(HEADS):
                w = (i + 1) * P
                items.append(([(0, q_t[:, h, i * P:w], k_t[:, h, 0:w])], bias(i), w,
                              [v[:, k, h * DV:(h + 1) * DV] for k in range(i + 1)], o[:, i, h * DV:(h + 1) * DV]))
        stage_attention(nc, b, tag, items, S, DQ ** -0.5)
        stage_turn(nc, b, f"{tag}o", [(lambda i, n=n: o[:, i, n * P:(n + 1) * P], P, o_t[:, n, :], None)
                                      for n in range(4)])


def mixer_two(nc, b, d):
    w_in = d["w_in_2"].rearrange("a k n -> (a k) n")
    with ExitStack() as mix:
        y_t = mix.enter_context(nc.sbuf_tensor("y_t", [P, DC, S], F32))
        lat = mix.enter_context(nc.sbuf_tensor("latents2", [P, TT, C2_RET], F32))
        with ExitStack() as heads:
            rq = heads.enter_context(nc.sbuf_tensor("ret_q", [P, TT, RW], F32))
            rk = heads.enter_context(nc.sbuf_tensor("ret_k", [P, TT, RW], F32))
            rv = heads.enter_context(nc.sbuf_tensor("ret_v", [P, TT, RW], F32))
            rg = heads.enter_context(nc.sbuf_tensor("ret_g", [P, TT, RW], F32))

            inner = heads.enter_context(ExitStack())
            h_hi, h_lo = b.split_pair(inner, "mix2_h", DC)
            stage_norm_turn(nc, b, "nt4", 3, 9, h_hi, h_lo)

            def plain(k, i):
                return h_hi[:, k, i * P:(i + 1) * P], h_lo[:, k, i * P:(i + 1) * P]

            jobs = [(w_in[:, 0:C2_RET], plain, lambda i, ps: [(lat[:, i, :], ps)])]
            for n, t in enumerate((rq, rk, rv, rg)):
                at = C2_RET + n * RW
                jobs.append((w_in[:, at:at + RW], plain, lambda i, ps, t=t: [(t[:, i, :], ps)]))
            stage_project_split(nc, b, "in2", jobs, b.tok_slots)
            inner.close()
            ropes = rope_items(b, rq, HEADS, DH, 0, DH // 2, ROPE_A // 2, 1)
            ropes += rope_items(b, rk, HEADS, DH, 0, DH // 2, ROPE_A // 2, 1)
            ropes += rope_items(b, lat[:, :, C2_KR:C2_KR + ROPE_A], 1, ROPE_A, 0, ROPE_A // 2, 0, 1)
            norms = [(lambda i: lat[:, i, 0:QL2], QL2), (lambda i: lat[:, i, QL2:QL2 + KVL2], KVL2)]
            decays = []
            for t, name in ((rq, "q_decay"), (rk, "k_decay")):
                for i in range(TT):
                    f = b.const(name)[:, i * HEADS:(i + 1) * HEADS].unsqueeze(2).to_broadcast([P, HEADS, DH])
                    decays.append((cols3(t, i, 0, HEADS, DH), f))
            stage_norm_rope(nc, b, "nr3", norms, ropes, (), decays)
            with ExitStack() as ret:
                q_t = ret.enter_context(nc.sbuf_tensor("ret_q_t", [P, 4, S], F32))
                k_t = ret.enter_context(nc.sbuf_tensor("ret_k_t", [P, 4, S], F32))
                stage_turn(nc, b, "ret", [(lambda i, n=n, t=t: t[:, i, n * P:(n + 1) * P], P, dst[:, n, :], None)
                                          for t, dst in ((rq, q_t), (rk, k_t)) for n in range(4)])
                stage_retention(nc, b, q_t, k_t, rv, rq)
            stage_retention_norm(nc, b, rq, rg[:, :, :])
            g = VEC_AT["g_ret_norm_2"]
            stage_turn(nc, b, "reto", [(lambda i, n=n: rg[:, i, n * P:(n + 1) * P], P, y_t[:, 4 + n, :],
                                        b.vec[:, g + n:g + n + 1]) for n in range(4)])
        with ExitStack() as mla:
            q_t = mla.enter_context(nc.sbuf_tensor("mla_q_t", [DQ, HEADS, S], F32))
            k_t = mla.enter_context(nc.sbuf_tensor("mla_k_t", [DQ, HEADS, S], F32))
            v = mla.enter_context(nc.sbuf_tensor("mla_v", [P, TT, HEADS * DV], F32))
            with ExitStack() as prep:
                lat_t = prep.enter_context(nc.sbuf_tensor("lat2_t", [P, 3, S], F32))
                q = prep.enter_context(nc.sbuf_tensor("mla_q", [P, TT, HEADS * DQ], F32))
                kk = prep.enter_context(nc.sbuf_tensor("mla_k", [P, TT, HEADS * DQ], F32))
                gq, gkv = VEC_AT["g_q_norm_2"], VEC_AT["g_kv_norm_2"]
                jobs = [(lambda i, n=n: lat[:, i, n * P:(n + 1) * P], P, lat_t[:, n, :],
                         b.vec[:, gq + n:gq + n + 1] if n < 2 else b.vec[:, gkv:gkv + 1]) for n in range(3)]
                stage_turn(nc, b, "lat2", jobs)
                w_uq = d["w_uq_2"].rearrange("a k n -> (a k) n")
                w_ukv = d["w_ukv_2"].rearrange("a k n -> (a k) n")

                def from_q(k, i):
                    return lat_t[:, k, i * P:(i + 1) * P]

                def from_kv(k, i):
                    return lat_t[:, 2, i * P:(i + 1) * P]

                def split_kv(n):
                    def stores(i, ps):
                        ps3 = ps.rearrange("p (h c) -> p h c", c=NOPE + DV)
                        k3 = cols3(kk, i, 0, HEADS, DQ)[:, 4 * n:4 * n + 4, 0:NOPE]
                        v3 = cols3(v, i, 0, HEADS, DV)[:, 4 * n:4 * n + 4, :]
                        return [(k3, ps3[:, :, 0:NOPE]), (v3, ps3[:, :, NOPE:NOPE + DV])]
                    return stores

                jobs = [(w_uq[:, n * 384:n * 384 + 384], 2, from_q,
                         lambda i, ps, n=n: [(q[:, i, n * 384:n * 384 + 384], ps)]) for n in range(2)]
                jobs += [(w_ukv[:, n * 512:n * 512 + 512], 1, from_kv, split_kv(n)) for n in range(2)]
                stage_project(nc, b, "uq2", jobs, 2)
                ropes = rope_items(b, q, HEADS, DQ, NOPE, ROPE_A // 2, 0, 1)
                copies = [(cols3(kk, i, 0, HEADS, DQ)[:, :, NOPE:DQ],
                           lat[:, i, C2_KR:C2_KR + ROPE_A].unsqueeze(1).to_broadcast([P, HEADS, ROPE_A]))
                          for i in range(TT)]
                stage_norm_rope(nc, b, "nr4", [], ropes, copies)
                jobs = []
                for src, dst in ((q, q_t), (kk, k_t)):
                    jobs += [(lambda i, h=h, src=src: src[:, i, h * DQ:(h + 1) * DQ], DQ, dst[:, h, :], None)
                             for h in range(HEADS)]
                stage_turn(nc, b, "mlaqk", jobs)
            with ExitStack() as att:
                bias = att.enter_context(nc.sbuf_tensor("mla_bias", [P, S + P], F32))
                with nc.Block() as block:
                    @block.vector
                    def _(dve):
                        nc.vector.memset(bias[:, 0:S - P], 0.0)
                        nc.vector.tensor_copy(bias[:, S - P:S], b.const("causal_bias"))
                latent_attention(nc, b, "mla", q_t, k_t, v, lambda i: bias[:, S - (i + 1) * P:S], y_t[:, 0:4, :])
        y = b.split_pair(mix, "y", DC)
        stage_split(nc, b, "y_split", [(y_t, *y)])
        stage_output(nc, b, "o2", d["w_out_2"].rearrange("a k n -> (a k) n"), y, add_row=3)


def peer(nc, b, d):
    with ExitStack() as own:
        scores = own.enter_context(nc.sbuf_tensor("peer_s", [P, TT, 2 * PH, NKEY], F32))
        with ExitStack() as route:
            q_t = route.enter_context(nc.sbuf_tensor("peer_q_t", [P, 2 * PH, S], F32))
            with ExitStack() as query:
                h_hi, h_lo = b.split_pair(query, "query_h", DC)
                stage_norm_turn(nc, b, "nt5", 4, 12, h_hi, h_lo, keep_tokens=b.tok)
                stage_queries(nc, b, d["w_query_2"], q_t, h_hi, h_lo)
            stage_key_scores(nc, b, d, q_t, scores)
        stage_experts(nc, b, d, scores)


def stage_queries(nc, b, w_query, q_t, h_hi, h_lo):
    NS = PH
    src = w_query.rearrange("a (k p) n -> p (a k) n", p=P)
    with ExitStack() as own:
        ws = WeightStream(nc, b, own, "query", b.feat_slots)
        first_up = b.sem("query_first_up")
        out = b.sem("query_out")
        with nc.Block() as block:
            @block.sync
            def _(sp):
                for m in range(NS):
                    ws.load(sp, m, m % 2, [(g * DC * P, DC, src[:, :, (2 * m + g) * P:(2 * m + g + 1) * P])
                                           for g in range(2)], m < 2)

            @block.tensor
            def _(pe):
                for m in range(NS):
                    pe.wait_ge(ws.lo_done, m + 1)
                    for g in range(2):
                        if m >= 2:
                            pe.wait_ge(out, 2 * m + g - 3)
                        for k in range(DC):
                            ins = split_products(nc, b.ps[:, (2 * m + g) % 4, :], ws.parts(m % 2, (g * DC + k) * P, P),
                                                 (h_hi[:, k, :], h_lo[:, k, :]), k == 0, k == DC - 1)
                        ins.then_inc(ws.used if g else first_up, 1)

            @block.scalar
            def _(act):
                for m in range(NS + 1):
                    if m < NS:
                        ws.round(act, m, m % 2, 32 * (m // 2 + 1), first=m < 2)
                    if m >= 1:
                        for g in range(2):
                            act.wait_ge(ws.used if g else first_up, m)
                            nc.scalar.activation(q_t[:, 2 * m - 2 + g, :], b.ps[:, (2 * m - 2 + g) % 4, :],
                                                 ACT.Copy).then_inc(out, 1)

            @block.vector
            def _(dve):
                for m in range(NS):
                    ws.rest(dve, m, m % 2)


def build_program(nc, d, out, upto=99):
    b = Bufs(nc)
    b.n_freq = ROPE_A // 2 + DH // 2
    with ExitStack() as ctx:
        def sb(name, shape, dt=F32):
            return ctx.enter_context(nc.sbuf_tensor(name, shape, dt))

        b.consts = sb("consts", [P, CONST_PACK.shape[1]])
        b.x = sb("residual", [P, TT, D])
        b.tok = sb("tok", [P, TT, D])
        b.tok_slots = b.tok[:, :, :].rearrange("p (j a) n -> p j (a n)", j=2)
        b.feat = sb("feat", [P, DC, S])
        b.feat_slots = b.feat[:, :, :].rearrange("p (j a) n -> p j (a n)", j=2)
        b.rows = sb("gate_rows", [P, 6, D])
        b.vec = sb("vec_cols", [P, NVEC])
        b.bias_cols = b.feat[:, 0, 0:NMOD]
        b.mod = sb("mod_cols", [P, NMOD])
        b.scale_cols = sb("scale_cols", [P, 5, DC])
        b.silu_c = sb("silu_c", [P, 2 * DC])
        b.sin = sb("sin", [P, 2 * TT, b.n_freq])
        b.cos = sb("cos", [P, 2 * TT, b.n_freq])
        b.stat = sb("stat", [P, TT])
        b.ps = ctx.enter_context(nc.psum_tensor("ps", [P, 8, 512], F32))

        def const(name):
            at, n = CONSTS[name]
            return b.consts[:, at:at + n]

        b.const = const
        stage_setup(nc, b, d)
        stage_modulation(nc, b, d)
        if upto >= 1:
            b.end_of_part()
            ffn(nc, b, "ffn1", 0, 0, d["w_gate1"], d["w_up1"], d["w_down1"], 0)
        if upto >= 2:
            b.end_of_part()
            mixer_one(nc, b, d)
            stage_post_norm(nc, b, "pn2", 1)
        if upto >= 3:
            b.end_of_part()
            ffn(nc, b, "ffn2", 2, 6, d["w_gate2"], d["w_up2"], d["w_down2"], 2)
        if upto >= 4:
            b.end_of_part()
            mixer_two(nc, b, d)
        if upto >= 5:
            b.end_of_part()
            peer(nc, b, d)
        if upto >= 5:
            stage_final(nc, b, out)


_INS = ["x", "c", "positions", "w_mod", "b_mod", "g_pre_ffn1", "w_gate1", "w_up1", "w_down1", "g_post_ffn1",
        "g_pre_mix", "w_in", "g_cq", "g_ckv", "w_uq", "w_uk", "w_uv", "w_iq", "w_up_a", "w_up_b", "w_o",
        "g_post_mix", "g_pre_ffn2", "w_gate2", "w_up2", "w_down2", "g_post_ffn2", "c_2", "positions_2",
        "w_ada_2", "b_ada_2", "g_norm1_2", "w_in_2", "g_q_norm_2", "w_uq_2", "g_kv_norm_2", "w_ukv_2",
        "g_ret_norm_2", "w_out_2", "g_norm2_2", "w_query_2", "sub_keys_2", "expert_u_2", "expert_v_2",
        "g_final_2"]


def kernel(**inputs):
    import numpy as _np
    import concourse.bacc as _bacc
    from concourse import mybir as _mybir
    from concourse.bass_utils import run_bass_kernel_spmd as _run

    nc = _bacc.Bacc("TRN2", target_bir_lowering=False, num_devices=1)
    given = {name: _np.ascontiguousarray(inputs[name]) for name in _INS}
    given["const_pack"] = CONST_PACK
    given["dilated_bias"] = DILATED_BIAS
    arrays, d = {}, {}
    for name, a in given.items():
        arrays[f"in_{name}"] = a
        d[name] = nc.dram_tensor(f"in_{name}", a.shape, _mybir.dt.from_np(a.dtype), kind="ExternalInput").ap()
    out = nc.dram_tensor("out_0", (1, S, D), F32, kind="ExternalOutput").ap()
    build_program(nc, d, out)
    r = _run(nc, [arrays], core_ids=[0])
    return r.results[0]["out_0"]
```

```python
from contextlib import ExitStack

import numpy as np

import concourse.bass as bass
from concourse import mybir

F32 = mybir.dt.float32
F32R = mybir.dt.float32r
I32 = mybir.dt.int32
U32 = mybir.dt.uint32
ALU = mybir.AluOpType
ACT = mybir.ActivationFunctionType
AX = mybir.AxisListType

P = 128
S = 512
D = 1024
TT = S // P
DC = D // P
F = 2816
FC = F // P
EPS = 1e-6
THETA = 10000.0
NEG = -1e30

SLOT = 2048

QL, KVL, NOPE, ROPE_A, DV = 384, 256, 64, 32, 64
HEADS = 8
IDX = 32
TOPK = 128
GRP, HB, DH = 3, 4, 64
DIL = ((128, 1), (512, 4), (2048, 16))
C_CKV = QL
C_KR = QL + KVL
C_KI = C_KR + ROPE_A
C_WI = C_KI + IDX
C_QKV = C_WI + HEADS
C_GATE = C_QKV + 3 * GRP * HB * DH
DQ = NOPE + ROPE_A
QL2, KVL2 = 256, 128
RW = 512
C2_KR = QL2 + KVL2
C2_RET = C2_KR + ROPE_A
PH, NKEY, KH, PK = 8, 128, 128, 16
NEXP = NKEY * NKEY

VECS = [("g_pre_ffn1", 8), ("g_pre_mix", 8), ("g_pre_ffn2", 8), ("g_norm1_2", 8), ("g_norm2_2", 8),
        ("g_cq", 3), ("g_ckv", 2), ("g_q_norm_2", 2), ("g_kv_norm_2", 1), ("c", 8), ("c_2", 8),
        ("g_post_ffn1", 8), ("g_post_mix", 8), ("g_post_ffn2", 8), ("g_final_2", 8), ("g_ret_norm_2", 4)]
VEC_AT = {}
_n = 0
for _name, _k in VECS:
    VEC_AT[_name] = _n
    _n += _k
NVEC = _n
NMOD1, NMOD2 = 9 * DC, 6 * DC
NMOD = NMOD1 + NMOD2

CONSTS = {}


def build_constants():
    p = np.arange(P)
    parts = []

    def put(name, a):
        at = sum(x.shape[1] for x in parts)
        CONSTS[name] = (at, a.shape[1])
        parts.append(np.ascontiguousarray(a, np.float32))

    put("identity", np.eye(P))
    put("causal_bias", np.where(p[None, :] <= p[:, None], 0.0, NEG))
    put("decay_mask", np.concatenate([(p[None, :] >= p[:, None]) * 1.0, np.ones((P, S - P))], 1))
    CONSTS["ones"] = (CONSTS["decay_mask"][0] + P, P)
    f32 = np.float32
    inv = [f32(THETA) ** (-np.arange(h, dtype=f32) / f32(h)) for h in (ROPE_A // 2, DH // 2)]
    put("inv_freq", np.tile(np.concatenate(inv)[None], (P, 1)))
    log_g = np.log(1.0 - 2.0 ** (-5.0 - np.arange(HEADS)))
    t = (np.arange(TT)[None, :] * P + p[:, None])[:, :, None]
    put("q_decay", np.exp(log_g * t).reshape(P, -1))
    put("k_decay", (np.exp(-log_g * t) * DH ** -0.5).reshape(P, -1))
    put("iota", np.tile(np.arange(PK)[None], (P, 1)))
    put("half_pi", np.full((P, 1), np.pi / 2))
    put("eps", np.full((P, 1), EPS))
    return np.concatenate(parts, 1)


CONST_PACK = build_constants()


def build_dilated_bias():
    n = np.arange(P)
    out = np.full((P, TT, S + 2 * P), NEG, np.float32)
    for r in range(TT):
        for r2 in range(TT):
            d = (4 * n + r)[:, None] - (4 * n + r2)[None, :]
            out[:, r, r2 * P:(r2 + 1) * P][(d >= 0) & (d <= DIL[0][0])] = 0
        d = 4 * (n[:, None] - n[None, :])
        for g in (1, 2):
            at = S + (g - 1) * P
            out[:, r, at:at + P][(d >= 0) & (d <= DIL[g][0]) & (d % DIL[g][1] == 0)] = 0
    return out.reshape(P, -1)


DILATED_BIAS = build_dilated_bias()


class Chain:

    def __init__(self, eng, sem):
        self.eng, self.sem, self.n = eng, sem, 0

    def __call__(self, ins):
        self.n += 1
        ins.then_inc(self.sem, 1)
        self.eng.wait_ge(self.sem, self.n)


def root_mean(nc, b, act, stat, n, squares, count, rooted):
    act.wait_ge(squares, count)
    nc.scalar.activation(stat, stat, ACT.Sqrt, scale=1.0 / n, bias=b.const("eps")).then_inc(rooted, 1)


class Bufs:

    def __init__(self, nc):
        self.nc, self.sems = nc, []

    def sem(self, name):
        self.sems.append(self.nc.alloc_semaphore(name))
        return self.sems[-1]

    def split_pair(self, own, name, chunks):
        return [own.enter_context(self.nc.sbuf_tensor(f"{name}_{part}", [P, chunks, S], F32R)) for part in ("hi", "lo")]

    def end_of_part(self):
        self.nc.clear_and_free_semaphores(self.sems)
        self.nc.all_engine_barrier()
        self.sems = []


def mm(nc, out, lhsT, rhs, start, stop):
    return nc.tensor.matmul(out, lhsT, rhs, start=start, stop=stop, skip_group_check=True)


def warm_up(nc, b, n):
    for _ in range(n):
        mm(nc, b.ps[:, 7, :], b.const("identity"), b.const("decay_mask"), True, True)


def split_products(nc, out, lhsT, rhs, start, stop):
    mm(nc, out, lhsT[0], rhs[0], start, False)
    mm(nc, out, lhsT[0], rhs[1], False, False)
    return mm(nc, out, lhsT[1], rhs[0], False, stop)


class WeightStream:

    def __init__(self, nc, b, own, tag, raw):
        self.nc, self.raw = nc, raw
        self.first = None
        self.hi = own.enter_context(nc.sbuf_tensor(f"{tag}_w_hi", [P, 2, SLOT], F32R))
        self.lo = own.enter_context(nc.sbuf_tensor(f"{tag}_w_lo", [P, 2, SLOT], F32R))
        self.arrived = [b.sem(f"{tag}_w_arrived{j}") for j in range(2)]
        self.hi_done = b.sem(f"{tag}_w_hi_done")
        self.lo_done = b.sem(f"{tag}_w_lo_done")
        self.used = b.sem(f"{tag}_w_used")

    def load(self, sp, n, j, srcs, first=False):
        if not first:
            sp.wait_ge(self.lo_done, n - 1)
        for at, k, src in srcs:
            w = src.shape[-1]
            sp.dma_start(self.raw[:, j, at:at + k * w].rearrange("p (k n) -> p k n", k=k), src).then_inc(self.arrived[j], 16)

    def round(self, act, n, j, dmas, width=SLOT, first=False):
        act.wait_ge(self.arrived[j], dmas)
        if not first:
            act.wait_ge(self.used, n - 1)
        self.nc.scalar.activation(self.hi[:, j, 0:width], self.raw[:, j, 0:width], ACT.Copy).then_inc(self.hi_done, 1)

    def rest(self, dve, n, j, width=SLOT):
        dve.wait_ge(self.hi_done, n + 1)
        self.nc.vector.tensor_tensor(self.lo[:, j, 0:width], self.raw[:, j, 0:width], self.hi[:, j, 0:width],
                                     ALU.subtract).then_inc(self.lo_done, 1)

    def parts(self, j, at, w):
        return self.hi[:, j, at:at + w], self.lo[:, j, at:at + w]


def stage_setup(nc, b, d, prefetch):
    with ExitStack() as own:
        vec_rows = own.enter_context(nc.sbuf_tensor("vec_rows", [NVEC, P], F32))
        bias_rows = own.enter_context(nc.sbuf_tensor("bias_rows", [NMOD, P], F32))
        pos_i = own.enter_context(nc.sbuf_tensor("pos_i", [2 * TT, P], I32))
        pos_rows = own.enter_context(nc.sbuf_tensor("pos_rows", [2 * TT, P], F32))
        pos_col = own.enter_context(nc.sbuf_tensor("pos_col", [P, 2 * TT], F32))
        NA = 2 * TT * b.n_freq
        ang = own.enter_context(nc.sbuf_tensor("ang", [P, 2 * TT, b.n_freq], F32))
        turns = own.enter_context(nc.sbuf_tensor("turns", [P, NA], F32))
        c_sig = own.enter_context(nc.sbuf_tensor("c_sig", [P, 2 * DC], F32))
        const_in = b.sem("const_in")
        vec_in = b.sem("vec_in")
        pos_in = b.sem("pos_in")
        pos_float = b.sem("pos_float")
        cols_up = b.sem("cols_turned")
        setup_chain = b.sem("setup_chain")
        angle_ready = b.sem("angle_ready")
        n_vec_dma = len(VECS) + 2
        with nc.Block() as block:
            @block.sync
            def _(sp):
                sp.dma_start(pos_i[0:TT, :], d["positions"].rearrange("a (i p) -> (a i) p", p=P)).then_inc(pos_in, 16)
                sp.dma_start(pos_i[TT:2 * TT, :],
                             d["positions_2"].rearrange("a (i p) -> (a i) p", p=P)).then_inc(pos_in, 16)
                sp.dma_start(b.consts[:, :], d["const_pack"]).then_inc(const_in, 16)
                prefetch(sp, range(0, 1))
                sp.wait_ge(vec_in, 16 * n_vec_dma)
                prefetch(sp, range(1, EARLY_SLOTS))

            @block.scalar
            def _(act):
                for name, k in VECS:
                    v = d[name]
                    v = v.rearrange("(k p) -> k p", p=P) if len(v.shape) == 1 else v.rearrange("a (k p) -> (a k) p", p=P)
                    at = VEC_AT[name]
                    act.dma_start(vec_rows[at:at + k, :], v).then_inc(vec_in, 16)
                act.dma_start(bias_rows[0:NMOD1, :], d["b_mod"].rearrange("a (k p) -> (a k) p", p=P)).then_inc(vec_in, 16)
                act.dma_start(bias_rows[NMOD1:NMOD, :],
                              d["b_ada_2"].rearrange("a (k p) -> (a k) p", p=P)).then_inc(vec_in, 16)
                act.wait_ge(cols_up, 4)
                at = VEC_AT["c"]
                nc.scalar.activation(c_sig[:, :], b.vec[:, at:at + 2 * DC], ACT.Sigmoid).then_inc(angle_ready, 1)
                act.wait_ge(angle_ready, 3)
                nc.scalar.activation(b.sin[:, :, :].rearrange("p a f -> p (a f)"),
                                     ang[:, :, :].rearrange("p a f -> p (a f)"), ACT.Sin)
                nc.scalar.activation(b.cos[:, :, :].rearrange("p a f -> p (a f)"), turns[:, :], ACT.Sin,
                                     bias=b.const("half_pi"), scale=-1.0)

            @block.tensor
            def _(pe):
                pe.wait_ge(const_in, 16)
                pe.wait_ge(pos_float, 1)
                ident = b.const("identity")
                nc.tensor.transpose(b.ps[:, 0, 0:2 * TT], pos_rows[:, :], ident[0:2 * TT, 0:2 * TT]).then_inc(cols_up, 1)
                pe.wait_ge(vec_in, 16 * n_vec_dma)
                nc.tensor.transpose(b.ps[:, 1, 0:NVEC], vec_rows[:, :], ident[0:NVEC, 0:NVEC]).then_inc(cols_up, 1)
                nc.tensor.transpose(b.ps[:, 2, 0:NMOD], bias_rows[:, :], ident[0:NMOD, 0:NMOD]).then_inc(cols_up, 1)

            @block.vector
            def _(dve):
                link = Chain(dve, setup_chain)
                dve.wait_ge(pos_in, 32)
                nc.vector.tensor_copy(pos_rows[:, :], pos_i[:, :]).then_inc(pos_float, 1)
                dve.wait_ge(cols_up, 1)
                link(nc.vector.tensor_copy(pos_col[:, :], b.ps[:, 0, 0:2 * TT]))
                dve.wait_ge(const_in, 16)
                dve.wait_ge(cols_up, 3)
                nc.vector.tensor_copy(b.mod[:, :], b.ps[:, 2, 0:NMOD])
                nc.vector.tensor_copy(b.vec[:, :], b.ps[:, 1, 0:NVEC]).then_inc(cols_up, 1)
                inv = b.const("inv_freq").unsqueeze(1).to_broadcast([P, 2 * TT, b.n_freq])
                link(nc.vector.tensor_tensor(ang[:, :, :], inv,
                                             pos_col[:, :].unsqueeze(2).to_broadcast([P, 2 * TT, b.n_freq]), ALU.mult))
                a = ang[:, :, :].rearrange("p a f -> p (a f)")
                magic = 1.5 * 2.0 ** 23
                two_pi = 2 * np.pi
                c1 = 6.28125
                c2 = round((two_pi - c1) * 2 ** 21) / 2 ** 21
                c3 = two_pi - c1 - c2
                link(nc.vector.tensor_scalar(turns[:, :], a, float(1 / two_pi), None, ALU.mult))
                link(nc.vector.tensor_scalar(turns[:, :], turns[:, :], magic, None, ALU.add))
                link(nc.vector.tensor_scalar(turns[:, :], turns[:, :], -magic, None, ALU.add))
                for part in (c1, c2, c3):
                    link(nc.vector.scalar_tensor_tensor(a, turns[:, :], -float(part), a, ALU.mult, ALU.add))
                link(nc.vector.tensor_scalar(a, a, 3.1415925, -3.1415925, ALU.min, ALU.max))
                nc.vector.scalar_tensor_tensor(turns[:, :], a, -1.0, a, ALU.mult, ALU.max).then_inc(angle_ready, 1)
                dve.wait_ge(angle_ready, 2)
                at = VEC_AT["c"]
                nc.vector.tensor_tensor(b.silu_c[:, :], c_sig[:, :], b.vec[:, at:at + 2 * DC],
                                        ALU.mult).then_inc(angle_ready, 1)


MOD_W = 512
MOD_COLS = MOD_W // P
EARLY_1, EARLY_2 = 6, 2
LATE_1 = NMOD1 // MOD_COLS - EARLY_1
LATE_2 = NMOD2 // MOD_COLS - EARLY_2


def add_chunk(nc, b, dve, w, acc, c_at, part, before, terms=DC):
    for k in range(terms):
        c = b.silu_c[:, c_at + k:c_at + k + 1]
        if k == 0:
            ins = nc.vector.tensor_scalar(acc, w(k), c, None, ALU.mult)
        else:
            dve.wait_ge(part, before + k)
            ins = nc.vector.scalar_tensor_tensor(acc, w(k), c, acc, ALU.mult, ALU.add)
        ins.then_inc(part, 1)


def sum_columns(nc, b, acc, ps, col):
    for q in range(MOD_COLS):
        ins = mm(nc, ps[:, bass.ds(col + q, 1)], acc[:, q * P:(q + 1) * P], b.const("ones")[:, 0:1], True, True)
    return ins


def scale_of(nc, b, n, name, at):
    v = VEC_AT[name]
    nc.vector.scalar_tensor_tensor(b.scale_cols[:, n, :], b.mod[:, at * DC:(at + 1) * DC], 1.0, b.vec[:, v:v + DC],
                                   ALU.add, ALU.mult)


EARLY_SLOTS = 4


def load_early(sp, d, w, w_in, n):
    src, at = (d["w_mod"], n) if n < EARLY_1 else (d["w_ada_2"], n - EARLY_1)
    rows = src.rearrange("a (k p) n -> p (a k) n", p=P)
    j = n % EARLY_SLOTS
    sp.dma_start(w[:, j, :, :], rows[:, :, at * MOD_W:(at + 1) * MOD_W]).then_inc(w_in[j], 16)


def stage_modulation_early(nc, b, d, w, w_in):
    ON_DVE = 7
    NSLOT = EARLY_SLOTS
    N = EARLY_1 + EARLY_2
    with ExitStack() as own:
        acc = own.enter_context(nc.sbuf_tensor("mod_acc", [P, 2, MOD_W], F32))
        part = b.sem("mod_part")
        summed = b.sem("mod_summed")
        x_in = b.sem("x_in")
        chain = b.sem("mod_chain")
        with nc.Block() as block:
            @block.sync
            def _(sp):
                sp.dma_start(b.x[:, :, :], d["x"].rearrange("a (i p) n -> p (a i) n", p=P)).then_inc(x_in, 16)
                for n in range(NSLOT, N):
                    sp.wait_ge(summed, n - NSLOT + 1)
                    load_early(sp, d, w, w_in, n)
                sp.wait_ge(x_in, 16)

            @block.vector
            def _(dve):
                for n in range(N):
                    dve.wait_ge(w_in[n % NSLOT], 16 * (n // NSLOT + 1))
                    if n >= 2:
                        dve.wait_ge(summed, n - 1)
                    add_chunk(nc, b, dve, lambda k, n=n: w[:, n % NSLOT, k, :], acc[:, n % 2, :],
                              0 if n < EARLY_1 else DC, part, n * ON_DVE, ON_DVE)
                link = Chain(dve, chain)
                dve.wait_ge(summed, N)
                for n, at, k in ((0, 0, EARLY_1), (EARLY_1, NMOD1, EARLY_2)):
                    cols = b.mod[:, at:at + k * MOD_COLS]
                    for share in range(2):
                        link(nc.vector.tensor_tensor(cols, cols, b.ps[:, share, n * MOD_COLS:(n + k) * MOD_COLS], ALU.add))
                scale_of(nc, b, 0, "g_pre_ffn1", 1)

            @block.tensor
            def _(pe):
                for n in range(N):
                    pe.wait_ge(w_in[n % NSLOT], 16 * (n // NSLOT + 1))
                    for q in range(MOD_COLS):
                        for k in range(ON_DVE, DC):
                            c = (0 if n < EARLY_1 else DC) + k
                            mm(nc, b.ps[:, 1, n * MOD_COLS + q:n * MOD_COLS + q + 1],
                               w[:, n % NSLOT, k, q * P:(q + 1) * P], b.silu_c[:, c:c + 1], k == ON_DVE, k == DC - 1)
                    pe.wait_ge(part, (n + 1) * ON_DVE)
                    sum_columns(nc, b, acc[:, n % 2, :], b.ps[:, 0, :], n * MOD_COLS).then_inc(summed, 1)


class LateModulation:

    def __init__(self, nc, b, d):
        self.nc, self.b = nc, b
        self.rows = [d[name].rearrange("a (k p) n -> p (a k) n", p=P) for name in ("w_mod", "w_ada_2")]
        flat = b.rows[:, :, :].rearrange("p a n -> p (a n)").rearrange("p (k n) -> p k n", n=MOD_W)
        self.w = [[flat[:, 0:4, :], flat[:, 4:8, :]], [flat[:, 8:12, :], b.feat[:, 4:8, :]]]
        self.acc = b.feat[:, 0:2, :]
        self.w_in = [b.sem(f"late_w_in{j}") for j in range(2)]
        self.part = b.sem("late_part")
        self.summed = b.sem("late_summed")
        self.out = b.sem("late_out")

    def load(self, sp, block, c, j, at, first=False):
        if not first:
            sp.wait_ge(self.part, (c - 1) * DC)
        for half in range(2):
            sp.dma_start(self.w[j][half], self.rows[block][:, 4 * half:4 * half + 4, bass.ds(at, MOD_W)]).then_inc(self.w_in[j], 16)

    def add(self, dve, block, c, j, pair, first=False):
        dve.wait_ge(self.w_in[j], (pair + 1) * 32)
        if not first:
            dve.wait_ge(self.summed, c - 1)
        add_chunk(self.nc, self.b, dve, lambda k: self.w[j][k // 4][:, k % 4, :], self.acc[:, j, :], block * DC,
                  self.part, c * DC)

    def sums(self, pe, c, j):
        pe.wait_ge(self.part, (c + 1) * DC)
        sum_columns(self.nc, self.b, self.acc[:, j, :], self.b.ps[:, 6, :], c * MOD_COLS).then_inc(self.summed, 1)

    def keep(self, dve, first, last):
        b = self.b
        dve.wait_ge(self.summed, last)
        for block, lo, hi, at in ((0, 0, LATE_1, EARLY_1 * MOD_COLS),
                                  (1, LATE_1, LATE_1 + LATE_2, NMOD1 + EARLY_2 * MOD_COLS)):
            c0, c1 = max(first, lo), min(last, hi)
            if c0 < c1:
                cols = b.mod[:, at + (c0 - lo) * MOD_COLS:at + (c1 - lo) * MOD_COLS]
                ins = self.nc.vector.tensor_tensor(cols, cols, b.ps[:, 6, c0 * MOD_COLS:c1 * MOD_COLS], ALU.add)
        ins.then_inc(self.out, 1)


def stage_modulation_end(nc, b, late):
    N = LATE_1 + LATE_2
    with ExitStack() as own:
        diag = own.enter_context(nc.sbuf_tensor("gate_diag", [P, 2, 4, P], F32))
        gates = own.enter_context(nc.sbuf_tensor("gate_cols", [P, 6, DC], F32))
        chain = b.sem("gates_chain")
        diag_ready = b.sem("diag_ready")
        row_up = b.sem("gate_row_up")
        row_out = b.sem("gate_row_out")
        with nc.Block() as block:
            @block.vector
            def _(dve):
                link = Chain(dve, chain)
                late.keep(dve, N - 2, N)
                dve.wait_ge(late.out, 3)
                for n, (name, at) in enumerate((("g_pre_mix", 4), ("g_pre_ffn2", 7), ("g_norm1_2", 10),
                                                ("g_norm2_2", 13))):
                    scale_of(nc, b, n + 1, name, at)
                for n, (name, at, half) in enumerate((("g_post_ffn1", 2, 0.5), ("g_post_mix", 5, 1.0),
                                                      ("g_post_ffn2", 8, 0.5))):
                    v = VEC_AT[name]
                    nc.vector.scalar_tensor_tensor(gates[:, n, :], b.mod[:, at * DC:(at + 1) * DC], half,
                                                   b.vec[:, v:v + DC], ALU.mult, ALU.mult)
                v = VEC_AT["g_final_2"]
                nc.vector.tensor_copy(gates[:, 5, :], b.vec[:, v:v + DC])
                nc.vector.tensor_copy(gates[:, 3, :], b.mod[:, 11 * DC:12 * DC])
                link(nc.vector.tensor_copy(gates[:, 4, :], b.mod[:, 14 * DC:15 * DC]))
                ident = b.const("identity").unsqueeze(1).to_broadcast([P, 4, P])
                for n in range(12):
                    if n >= 2:
                        dve.wait_ge(row_up, n - 1)
                    cols = gates[:, n // 2, 4 * (n % 2):4 * (n % 2) + 4].unsqueeze(2).to_broadcast([P, 4, P])
                    nc.vector.tensor_tensor(diag[:, n % 2, :, :], ident, cols, ALU.mult).then_inc(diag_ready, 1)

            @block.tensor
            def _(pe):
                for c in (N - 2, N - 1):
                    late.sums(pe, c, c % 2)
                for n in range(12):
                    pe.wait_ge(diag_ready, n + 1)
                    if n >= 2:
                        pe.wait_ge(row_out, n - 1)
                    mm(nc, b.ps[:, 1 + n % 2, :], b.const("ones"), diag[:, n % 2, :, :].rearrange("p a c -> p (a c)"),
                       True, True).then_inc(row_up, 1)

            @block.scalar
            def _(act):
                for n in range(12):
                    act.wait_ge(row_up, n + 1)
                    nc.scalar.activation(b.rows[:, n // 2, (n % 2) * 512:(n % 2) * 512 + 512], b.ps[:, 1 + n % 2, :],
                                         ACT.Copy).then_inc(row_out, 1)


def stage_norm_turn(nc, b, tag, scale_at, shift_at, h_hi, h_lo, keep_tokens=None, prefetch=None, squared=False):
    xs = b.tok
    squares = b.sem(f"{tag}_squares")
    rooted = b.sem(f"{tag}_rooted")
    rstd = b.sem(f"{tag}_rstd")
    scaled = b.sem(f"{tag}_scaled")
    turned = b.sem(f"{tag}_turned")
    moved = b.sem(f"{tag}_moved")
    hi_done = b.sem(f"{tag}_hi_done")
    back = b.sem(f"{tag}_back")
    with nc.Block() as block:
        if prefetch:
            ws, load = prefetch

            @block.sync
            def _(sp):
                for n in range(2):
                    load(sp, n)

        @block.scalar
        def _(act):
            if squared:
                nc.scalar.activation(b.stat[:, :], b.stat[:, :], ACT.Sqrt, scale=1.0 / D,
                                     bias=b.const("eps")).then_inc(rooted, 1)
            else:
                for i in range(TT):
                    nc.scalar.activation(b.feat[:, 2 * i:2 * i + 2, :].rearrange("p a n -> p (a n)"), b.x[:, i, :],
                                         ACT.Square, accum_out=b.stat[:, i:i + 1]).then_inc(squares, 1)
                root_mean(nc, b, act, b.stat[:, :], D, squares, TT, rooted)
            if prefetch:
                for n in range(2):
                    ws.round(act, n, n, ws.first[n][0], ws.first[n][1], first=True)
            for k in range(DC):
                act.wait_ge(moved, k + 1)
                nc.scalar.activation(h_hi[:, k, :], b.feat[:, k, :], ACT.Copy).then_inc(hi_done, 1)
            if keep_tokens is not None:
                for n in range(2 * TT):
                    act.wait_ge(back, n + 1)
                    nc.scalar.activation(keep_tokens[:, n // 2, (n % 2) * 512:(n % 2) * 512 + 512], b.ps[:, n, :], ACT.Copy)

        @block.vector
        def _(dve):
            dve.wait_ge(rooted, 1)
            nc.vector.reciprocal(b.stat[:, :], b.stat[:, :]).then_inc(rstd, 1)
            dve.wait_ge(rstd, 1)
            for i in range(TT):
                nc.vector.tensor_scalar(xs[:, i, :], b.x[:, i, :], b.stat[:, i:i + 1], None, ALU.mult).then_inc(scaled, 1)
            for k in range(DC):
                dve.wait_ge(turned, k + 1)
                nc.vector.tensor_scalar(b.feat[:, k, :], b.ps[:, k, :], b.scale_cols[:, scale_at, k:k + 1],
                                        b.mod[:, shift_at * DC + k:shift_at * DC + k + 1], ALU.mult,
                                        ALU.add).then_inc(moved, 1)
            if prefetch:
                for n in range(2):
                    ws.rest(dve, n, n, ws.first[n][1])
            for k in range(1, DC, 2):
                dve.wait_ge(hi_done, k + 1)
                nc.vector.tensor_tensor(h_lo[:, k, :], b.feat[:, k, :], h_hi[:, k, :], ALU.subtract)

        @block.gpsimd
        def _(pool):
            for k in range(0, DC, 2):
                pool.wait_ge(hi_done, k + 1)
                nc.gpsimd.tensor_tensor(h_lo[:, k, :], b.feat[:, k, :], h_hi[:, k, :], ALU.subtract)

        @block.tensor
        def _(pe):
            ident = b.const("identity")
            for i in range(TT):
                pe.wait_ge(scaled, i + 1)
                for k in range(DC):
                    ins = nc.tensor.transpose(b.ps[:, k, i * P:(i + 1) * P], xs[:, i, k * P:(k + 1) * P], ident)
                    if i == TT - 1:
                        ins.then_inc(turned, 1)
            if keep_tokens is not None:
                pe.wait_ge(moved, DC)
                for n in range(2 * TT):
                    for q in range(4):
                        ins = nc.tensor.transpose(b.ps[:, n, q * P:(q + 1) * P],
                                                  b.feat[:, (n % 2) * 4 + q, (n // 2) * P:(n // 2 + 1) * P], ident)
                    ins.then_inc(back, 1)


def stage_split(nc, b, tag, jobs):
    hi_done = b.sem(f"{tag}_hi_done")
    chunks = [(src[:, k, :], hi[:, k, :], lo[:, k, :]) for src, hi, lo in jobs for k in range(src.shape[1])]
    with nc.Block() as block:
        @block.scalar
        def _(act):
            for src, hi, _lo in chunks:
                nc.scalar.activation(hi, src, ACT.Copy).then_inc(hi_done, 1)

        @block.vector
        def _(dve):
            for n, (src, hi, lo) in enumerate(chunks):
                dve.wait_ge(hi_done, n + 1)
                nc.vector.tensor_tensor(lo, src, hi, ALU.subtract)


def stage_post_norm(nc, b, tag, row):
    squares = b.sem(f"{tag}_squares")
    rooted = b.sem(f"{tag}_rooted")
    rstd = b.sem(f"{tag}_rstd")
    gated = b.sem(f"{tag}_gated")
    added = [b.sem(f"{tag}_added_by_{name}") for name in ("gpsimd", "vector")]
    ON_POOL = 2
    stat = b.post_stat[:, :]

    def scratch(i):
        return b.feat[:, 2 * i:2 * i + 2, :].rearrange("p a n -> p (a n)")

    with nc.Block() as block:
        @block.scalar
        def _(act):
            for i in range(TT):
                nc.scalar.activation(scratch(i), b.tok[:, i, :], ACT.Square,
                                     accum_out=b.post_stat[:, i:i + 1]).then_inc(squares, 1)
            root_mean(nc, b, act, stat, D, squares, TT, rooted)
            for i in range(TT):
                act.wait_ge(added[i >= ON_POOL], i % ON_POOL + 1)
                nc.scalar.activation(scratch(i), b.x[:, i, :], ACT.Square, accum_out=b.stat[:, i:i + 1])

        @block.vector
        def _(dve):
            dve.wait_ge(rooted, 1)
            nc.vector.reciprocal(stat, stat).then_inc(rstd, 1)
            dve.wait_ge(rstd, 1)
            for i in range(TT):
                nc.vector.scalar_tensor_tensor(b.tok[:, i, :], b.tok[:, i, :], b.post_stat[:, i:i + 1],
                                               b.rows[:, row, :], ALU.mult, ALU.mult).then_inc(gated, 1)
            for i in range(ON_POOL, TT):
                dve.wait_ge(gated, i + 1)
                nc.vector.tensor_tensor(b.x[:, i, :], b.x[:, i, :], b.tok[:, i, :], ALU.add).then_inc(added[1], 1)

        @block.gpsimd
        def _(pool):
            for i in range(ON_POOL):
                pool.wait_ge(gated, i + 1)
                nc.gpsimd.tensor_tensor(b.x[:, i, :], b.x[:, i, :], b.tok[:, i, :], ALU.add).then_inc(added[0], 1)


def gate_up_slot(ws, sp, n, j, wg, wu, at, first=False):
    cols = bass.ds(at, P)
    ws.load(sp, n, j, [(0, DC, wg[:, :, cols]), (DC * P, DC, wu[:, :, cols])], first)


def stage_swiglu(nc, b, tag, wg, wu, w_down, h_hi, h_lo, ws, late=None):
    wd = w_down.rearrange("a (k p) n -> p (a k) n", p=P)
    counts = (12, 10)
    firsts = (0, counts[0])
    slots = (0, counts[0] + counts[0] // 2)
    assert sum(counts) == FC
    assert late is None or counts == (LATE_1, LATE_2)
    last_slot = slots[1] + counts[1] + counts[1] // 2 - 1
    with ExitStack() as own:
        gu_hi = own.enter_context(nc.sbuf_tensor(f"{tag}_gu_hi", [P, counts[0], S], F32R))
        gu_lo = own.enter_context(nc.sbuf_tensor(f"{tag}_gu_lo", [P, counts[0], S], F32R))
        silu = b.feat[:, 2:4, :]
        gu = b.ps[:, 4:6, :]
        silu_done = b.sem(f"{tag}_silu")
        gu_done = b.sem(f"{tag}_gu_done")
        gu_hi_done = b.sem(f"{tag}_gu_hi_done")
        gu_lo_done = b.sem(f"{tag}_gu_lo_done")
        y_up = b.sem(f"{tag}_y_up")
        y_out = b.sem(f"{tag}_y_out")

        def arrived_before(slot):
            total = 0
            for m in range(slot % 2, slot, 2):
                part = 1 if m >= slots[1] else 0
                total += 32 if m - slots[part] < counts[part] else 16
            return total

        with nc.Block() as block:
            @block.sync
            def _(sp):
                for part in range(2):
                    base, c0, n = slots[part], firsts[part], counts[part]

                    def gate_up(i, j):
                        gate_up_slot(ws, sp, i * 2 + j + base, j, wg, wu, (i * 2 + j + c0) * P)

                    def beside(at, j, first=False):
                        if late:
                            late.load(sp, part, at + c0, j, (at + (EARLY_2 if part else EARLY_1)) * MOD_W, first)

                    if part:
                        gate_up(0, 0)
                        gate_up(0, 1)
                    beside(0, 0, part == 0)
                    gate_up(1, 0)
                    beside(1, 1, part == 0)
                    gate_up(1, 1)
                    beside(2, 0)
                    with sp.Fori(2, n // 2) as i:
                        gate_up(i, 0)
                        beside(i * 2 - 1, 1)
                        gate_up(i, 1)
                        beside(i * 2, 0)
                    beside(n - 1, 1)
                    for q in range(n // 2):
                        m = base + n + q
                        ws.load(sp, m, m % 2, [(0, 2, wd[:, c0 + 2 * q:c0 + 2 * q + 2, :])])

            @block.scalar
            def _(act):
                for part in range(2):
                    base, c0, n = slots[part], firsts[part], counts[part]
                    gone = arrived_before(base)
                    gone1 = arrived_before(base + 1)

                    def chunk(i, j, prepare=True, first=False):
                        c = i * 2 + j + c0
                        if prepare:
                            if j == 0:
                                ws.round(act, i * 2 + 1 + base, 1, gone1 + (i + 1) * 32)
                            else:
                                ws.round(act, i * 2 + 2 + base, 0, gone + (i + 2) * 32)
                        act.wait_ge(ws.used, i * 2 + j + base + 1)
                        if not first:
                            act.wait_ge(gu_done, c - 1)
                        nc.scalar.activation(silu[:, j, :], b.ps[:, 2 * j, :], ACT.Silu).then_inc(silu_done, 1)
                        act.wait_ge(gu_done, c + 1)
                        nc.scalar.activation(gu_hi[:, i * 2 + j, :], gu[:, j, :], ACT.Copy).then_inc(gu_hi_done, 1)

                    if part == 0:
                        chunk(0, 0, prepare=False, first=True)
                        chunk(0, 1, first=True)
                    with act.Fori(0 if part else 1, n // 2 - 1) as i:
                        chunk(i, 0)
                        chunk(i, 1)
                    chunk(n // 2 - 1, 0)
                    ws.round(act, base + n, 0, arrived_before(base + n) + 16)
                    chunk(n // 2 - 1, 1, prepare=False)
                    for q in range(n // 2):
                        m = base + n + q + 1
                        if m <= last_slot:
                            ws.round(act, m, m % 2, arrived_before(m) + (16 if q < n // 2 - 1 else 32))

            @block.vector
            def _(dve):
                for part in range(2):
                    base, c0, n = slots[part], firsts[part], counts[part]

                    def chunk(i, j, first=False, last=False):
                        c = i * 2 + j + c0
                        if not (first and j == 0):
                            ws.rest(dve, i * 2 + j + 1 + base, 1 - j)
                        dve.wait_ge(silu_done, c + 1)
                        if not first:
                            dve.wait_ge(gu_lo_done, c - 1)
                        nc.vector.tensor_tensor(gu[:, j, :], silu[:, j, :], b.ps[:, 2 * j + 1, :], ALU.mult).then_inc(gu_done, 1)
                        dve.wait_ge(gu_hi_done, c + 1)
                        nc.vector.tensor_tensor(gu_lo[:, i * 2 + j, :], gu[:, j, :], gu_hi[:, i * 2 + j, :],
                                                ALU.subtract).then_inc(gu_lo_done, 1)
                        if late:
                            if last:
                                late.keep(dve, (0, counts[0] - 2)[part], c0 + n - 2)
                            late.add(dve, part, c, j, i + c0 // 2, first)

                    if part == 0:
                        chunk(0, 0, True)
                        chunk(0, 1, True)
                    with dve.Fori(0 if part else 1, n // 2 - 1) as i:
                        chunk(i, 0)
                        chunk(i, 1)
                    chunk(n // 2 - 1, 0)
                    chunk(n // 2 - 1, 1, last=True)
                    for q in range(n // 2):
                        m = base + n + q + 1
                        if m <= last_slot:
                            ws.rest(dve, m, m % 2)
                    for n_bank in range(8):
                        i, half = n_bank // 2, n_bank % 2
                        at = slice(half * 512, half * 512 + 512)
                        if n_bank < 7:
                            dve.wait_ge(y_up, part * 7 + n_bank + 1)
                        else:
                            dve.wait_ge(ws.used, base + n + n // 2)
                        if part == 0:
                            ins = nc.vector.tensor_copy(b.tok[:, i, at], b.ps[:, n_bank, :])
                        else:
                            if n_bank == 0:
                                dve.wait_ge(y_out, 8)
                            ins = nc.vector.tensor_tensor(b.tok[:, i, at], b.tok[:, i, at], b.ps[:, n_bank, :], ALU.add)
                        ins.then_inc(y_out, 1)

            @block.tensor
            def _(pe):
                for part in range(2):
                    base, c0, n = slots[part], firsts[part], counts[part]

                    def chunk(i, j, first=False):
                        c = i * 2 + j + c0
                        pe.wait_ge(ws.lo_done, i * 2 + j + base + 1)
                        if not first:
                            pe.wait_ge(gu_done, c - 1)
                            if late:
                                late.sums(pe, c - 2, j)
                        for m in range(2):
                            for k in range(DC):
                                ins = split_products(nc, b.ps[:, 2 * j + m, :], ws.parts(j, (m * DC + k) * P, P),
                                                     (h_hi[:, k, :], h_lo[:, k, :]), k == 0, k == DC - 1)
                        ins.then_inc(ws.used, 1)

                    if part == 0:
                        chunk(0, 0, True)
                        chunk(0, 1, True)
                    else:
                        pe.wait_ge(y_out, 8)
                    with pe.Fori(0 if part else 1, n // 2) as i:
                        chunk(i, 0)
                        chunk(i, 1)
                    pe.wait_ge(gu_lo_done, c0 + n)
                    for q in range(n // 2):
                        m = base + n + q
                        pe.wait_ge(ws.lo_done, m + 1)
                        for bank in range(8):
                            i, half = bank // 2, bank % 2
                            if late and q == 0 and bank == 6:
                                pe.wait_ge(late.out, part + 1)
                            for f in range(2):
                                k = 2 * q + f
                                tok = slice(i * P, (i + 1) * P)
                                ins = split_products(nc, b.ps[:, bank, :], (gu_hi[:, k, tok], gu_lo[:, k, tok]),
                                                     ws.parts(m % 2, f * D + half * 512, 512), k == 0, k == n - 1)
                            if bank == 7:
                                ins.then_inc(ws.used, 1)
                            elif q == n // 2 - 1:
                                ins.then_inc(y_up, 1)


def ffn(nc, b, tag, scale_at, shift_at, w_gate, w_up, w_down, row, d=None):
    late = LateModulation(nc, b, d) if d else None
    with ExitStack() as own:
        h_hi, h_lo = b.split_pair(own, f"{tag}_h", DC)
        ws = WeightStream(nc, b, own, tag, own.enter_context(nc.sbuf_tensor(f"{tag}_w_raw", [P, 2, SLOT], F32)))
        wg = w_gate.rearrange("a (k p) n -> p (a k) n", p=P)
        wu = w_up.rearrange("a (k p) n -> p (a k) n", p=P)

        ws.first = [(32, SLOT)] * 2
        stage_norm_turn(nc, b, f"{tag}_nt", scale_at, shift_at, h_hi, h_lo, 
                        prefetch=(ws, lambda sp, n: gate_up_slot(ws, sp, n, n, wg, wu, n * P, True)),
                        squared=d is None)
        stage_swiglu(nc, b, tag, wg, wu, w_down, h_hi, h_lo, ws, late)
    if late:
        stage_modulation_end(nc, b, late)
    stage_post_norm(nc, b, f"{tag}_pn", row)


def stage_project(nc, b, tag, jobs, slot_k, slots=2):
    with ExitStack() as own:
        w = own.enter_context(nc.sbuf_tensor(f"{tag}_w", [P, slots, slot_k, 512], F32))
        w_in = [b.sem(f"{tag}_w_in{j}") for j in range(slots)]
        up = b.sem(f"{tag}_up")
        out_act = b.sem(f"{tag}_out_act")
        out_dve = b.sem(f"{tag}_out_dve")
        acts = [i for i in range(TT) if i % 2 == 0]
        with nc.Block() as block:
            @block.sync
            def _(sp):
                for n, (src, nk, _l, _s) in enumerate(jobs):
                    if n >= slots:
                        sp.wait_ge(up, (n - slots + 1) * TT)
                    width = src.shape[-1]
                    sp.dma_start(w[:, n % slots, 0:nk, 0:width],
                                 src.rearrange("(k p) n -> p k n", p=P)).then_inc(w_in[n % slots], 16)

            @block.tensor
            def _(pe):
                for n, (src, nk, lhsT, _s) in enumerate(jobs):
                    width = src.shape[-1]
                    pe.wait_ge(w_in[n % slots], 16 * (n // slots + 1))
                    for i in range(TT):
                        bank = (n % 2) * TT + i
                        if n >= 2:
                            pe.wait_ge(out_act if i in acts else out_dve, (n - 2) * 2 + i // 2 + 1)
                        for k in range(nk):
                            ins = mm(nc, b.ps[:, bank, 0:width], lhsT(k, i), w[:, n % slots, k, 0:width],
                                     k == 0, k == nk - 1)
                        ins.then_inc(up, 1)

            @block.scalar
            def _(act):
                for n, (src, _n, _l, stores) in enumerate(jobs):
                    for i in acts:
                        act.wait_ge(up, n * TT + i + 1)
                        for dst, ps in stores(i, b.ps[:, (n % 2) * TT + i, 0:src.shape[-1]]):
                            ins = nc.scalar.activation(dst, ps, ACT.Copy)
                        ins.then_inc(out_act, 1)

            @block.vector
            def _(dve):
                for n, (src, _n, _l, stores) in enumerate(jobs):
                    for i in range(TT):
                        if i in acts:
                            continue
                        dve.wait_ge(up, n * TT + i + 1)
                        for dst, ps in stores(i, b.ps[:, (n % 2) * TT + i, 0:src.shape[-1]]):
                            ins = nc.vector.tensor_copy(dst, ps)
                        ins.then_inc(out_dve, 1)


def job_slot(ws, sp, jobs, m):
    HALF = DC // 2
    src = jobs[m // 2][0].rearrange("(k p) n -> p k n", p=P)
    ws.load(sp, m, m % 2, [(0, HALF, src[:, (m % 2) * HALF:(m % 2 + 1) * HALF, :])], m < 2)


def norm_and_project(nc, b, tag, scale_at, shift_at, jobs_of):
    with ExitStack() as inner:
        h = b.split_pair(inner, f"{tag}_h", DC)
        ws = WeightStream(nc, b, inner, tag, inner.enter_context(nc.sbuf_tensor(f"{tag}_w_raw", [P, 2, SLOT], F32)))
        jobs = jobs_of(h)
        ws.first = [(16, DC // 2 * jobs[0][0].shape[-1])] * 2
        stage_norm_turn(nc, b, f"{tag}_nt", scale_at, shift_at, *h, prefetch=(ws, lambda sp, n: job_slot(ws, sp, jobs, n)),
                        squared=True)
        stage_project_split(nc, b, tag, jobs, ws)


def stage_project_split(nc, b, tag, jobs, ws, add_row=None):
    HALF = DC // 2
    with ExitStack() as own:
        first = 2 if ws.first else 0
        up = b.sem(f"{tag}_up")
        out_act = b.sem(f"{tag}_out_act")
        out_dve = b.sem(f"{tag}_out_dve")
        n_slots = 2 * len(jobs)
        width = [job[0].shape[-1] for job in jobs]

        def wait_up(eng, n, i):
            if i < TT - 1:
                eng.wait_ge(up, n * (TT - 1) + i + 1)
            else:
                eng.wait_ge(ws.used, 2 * n + 2)

        def gate(dve, n):
            at = slice(n * 512, (n + 1) * 512)
            for i in range(TT):
                wait_up(dve, n, i)
                nc.vector.tensor_tensor(b.tok[:, i, at], b.ps[:, n * TT + i, :], b.rows[:, add_row, at],
                                        ALU.mult).then_inc(out_dve, 1)

        def evacuate(eng, n, mine, copy, out):
            for i in mine:
                wait_up(eng, n, i)
                for dst, ps in jobs[n][2](i, b.ps[:, (n % 2) * TT + i, 0:width[n]]):
                    ins = copy(dst, ps)
                ins.then_inc(out, 1)

        with nc.Block() as block:
            @block.sync
            def _(sp):
                for m in range(first, n_slots):
                    job_slot(ws, sp, jobs, m)

            @block.scalar
            def _(act):
                for m in range(n_slots + 2):
                    if first <= m < n_slots:
                        ws.round(act, m, m % 2, 16 * (m // 2 + 1), HALF * width[m // 2], m < 2)
                    if m >= 2 and m % 2 == 0 and add_row is None:
                        evacuate(act, m // 2 - 1, (0, 2), lambda dst, ps: nc.scalar.activation(dst, ps, ACT.Copy), out_act)

            @block.vector
            def _(dve):
                for m in range(n_slots + 2):
                    if first <= m < n_slots:
                        ws.rest(dve, m, m % 2, HALF * width[m // 2])
                    if m >= 2 and m % 2 == 0:
                        if add_row is None:
                            evacuate(dve, m // 2 - 1, (1, 3), nc.vector.tensor_copy, out_dve)
                        else:
                            gate(dve, m // 2 - 1)

            if add_row is not None:
                @block.gpsimd
                def _(pool):
                    for n in range(len(jobs)):
                        at = slice(n * 512, (n + 1) * 512)
                        for i in range(TT):
                            pool.wait_ge(out_dve, n * TT + i + 1)
                            nc.gpsimd.tensor_tensor(b.x[:, i, at], b.x[:, i, at], b.tok[:, i, at], ALU.add)

            @block.tensor
            def _(pe):
                for m in range(n_slots):
                    n, half = m // 2, m % 2
                    w = width[n]
                    pe.wait_ge(ws.lo_done, m + 1)
                    for i in range(TT):
                        if half == 0 and n >= 2:
                            pe.wait_ge(out_act if i % 2 == 0 else out_dve, (n - 2) * 2 + i // 2 + 1)
                        for k in range(HALF):
                            ins = split_products(nc, b.ps[:, (n % 2) * TT + i, 0:w], jobs[n][1](half * HALF + k, i),
                                                 ws.parts(m % 2, k * w, w), half == 0 and k == 0,
                                                 half == 1 and k == HALF - 1)
                        if i == TT - 1:
                            ins.then_inc(ws.used, 1)
                        elif half:
                            ins.then_inc(up, 1)


def stage_turn(nc, b, tag, jobs):
    NB = 8
    turned = b.sem(f"{tag}_turned")
    out_act = b.sem(f"{tag}_out_act")
    out_dve = b.sem(f"{tag}_out_dve")
    with nc.Block() as block:
        @block.tensor
        def _(pe):
            ident = b.const("identity")
            for n, (src, f, _d, _s) in enumerate(jobs):
                if n >= NB:
                    pe.wait_ge(out_act if n % 2 == 0 else out_dve, (n - NB) // 2 + 1)
                for i in range(TT):
                    ins = nc.tensor.transpose(b.ps[0:f, n % NB, i * P:(i + 1) * P], src(i), ident)
                ins.then_inc(turned, 1)

        @block.scalar
        def _(act):
            for n, (_src, f, dst, scale) in enumerate(jobs):
                if n % 2 == 0:
                    act.wait_ge(turned, n + 1)
                    nc.scalar.activation(dst, b.ps[0:f, n % NB, :], ACT.Copy,
                                         scale=1.0 if scale is None else scale).then_inc(out_act, 1)

        @block.vector
        def _(dve):
            for n, (_src, f, dst, scale) in enumerate(jobs):
                if n % 2:
                    dve.wait_ge(turned, n + 1)
                    if scale is None:
                        ins = nc.vector.tensor_copy(dst, b.ps[0:f, n % NB, :])
                    else:
                        ins = nc.vector.tensor_scalar(dst, b.ps[0:f, n % NB, :], scale, None, ALU.mult)
                    ins.then_inc(out_dve, 1)


def stage_norm_rope(nc, b, tag, norms, ropes, copies=(), decays=()):
    with ExitStack() as own:
        size = 768
        tmp = own.enter_context(nc.sbuf_tensor(f"{tag}_tmp", [P, 4, size], F32))
        stat = own.enter_context(nc.sbuf_tensor(f"{tag}_stat", [P, max(1, len(norms)), TT], F32))
        squares = b.sem(f"{tag}_squares")
        chain = b.sem(f"{tag}_chain")
        first = b.sem(f"{tag}_first_half")
        second = b.sem(f"{tag}_second_half")
        done = b.sem(f"{tag}_rope_done")
        rooted = b.sem(f"{tag}_rooted")

        def view(t, like):
            a, c = like.shape[1], like.shape[2]
            return tmp[:, t, 0:a * c].rearrange("p (a c) -> p a c", c=c)

        with nc.Block() as block:
            @block.scalar
            def _(act):
                for n, (t, w) in enumerate(norms):
                    for i in range(TT):
                        nc.scalar.activation(b.tok[:, i, n * 512:n * 512 + w], t(i), ACT.Square,
                                             accum_out=stat[:, n, i:i + 1]).then_inc(squares, 1)
                for n, (t, w) in enumerate(norms):
                    root_mean(nc, b, act, stat[:, n, :], w, squares, TT * len(norms), rooted)

            @block.vector
            def _(dve):
                link = Chain(dve, chain)
                for n, (x1, x2, cos, sin) in enumerate(ropes):
                    nc.vector.tensor_tensor(view(0, x1), x1, cos, ALU.mult)
                    nc.vector.tensor_tensor(view(1, x1), x2, sin, ALU.mult)
                    if n:
                        dve.wait_ge(done, n)
                    nc.vector.tensor_tensor(view(2, x1), x2, cos, ALU.mult).then_inc(first, 1)
                    dve.wait_ge(first, n + 1)
                    dve.wait_ge(second, n + 1)
                    link(nc.vector.tensor_tensor(x1, view(0, x1), view(1, x1), ALU.subtract))
                for n, (t, w) in enumerate(norms):
                    dve.wait_ge(rooted, n + 1)
                    link(nc.vector.reciprocal(stat[:, n, :], stat[:, n, :]))
                    for i in range(TT):
                        nc.vector.tensor_scalar(t(i), t(i), stat[:, n, i:i + 1], None, ALU.mult)
                if copies or decays:
                    dve.wait_ge(done, len(ropes))
                for dst, src in copies:
                    nc.vector.tensor_copy(dst, src)
                for t, factors in decays:
                    nc.vector.tensor_tensor(t, t, factors, ALU.mult)

            @block.gpsimd
            def _(pool):
                for n, (x1, x2, cos, sin) in enumerate(ropes):
                    nc.gpsimd.tensor_tensor(view(3, x1), x1, sin, ALU.mult).then_inc(second, 1)
                    pool.wait_ge(first, n + 1)
                    pool.wait_ge(second, n + 1)
                    nc.gpsimd.tensor_tensor(x2, view(2, x1), view(3, x1), ALU.add).then_inc(done, 1)
                    pool.wait_ge(done, n + 1)


def stage_attention(nc, b, tag, items, width, scale, beside=None):
    N = len(items)
    with ExitStack() as own:
        neg = own.enter_context(nc.sbuf_tensor(f"{tag}_neg", [P, 2, width], F32))
        prob = own.enter_context(nc.sbuf_tensor(f"{tag}_prob", [P, 2, width], F32))
        prob_t = own.enter_context(nc.sbuf_tensor(f"{tag}_prob_t", [P, 2, width], F32))
        neg_max = own.enter_context(nc.sbuf_tensor(f"{tag}_neg_max", [P, N], F32))
        total = own.enter_context(nc.sbuf_tensor(f"{tag}_total", [P, N], F32))
        inverse = own.enter_context(nc.sbuf_tensor(f"{tag}_inverse", [P, N], F32))
        score_up = b.sem(f"{tag}_score_up")
        biased = b.sem(f"{tag}_biased")
        exp_done = b.sem(f"{tag}_exp_done")
        prob_up = b.sem(f"{tag}_prob_turned")
        prob_out = b.sem(f"{tag}_prob_t_out")
        inverted = b.sem(f"{tag}_inverted")
        value_up = b.sem(f"{tag}_value_up")
        value_out = b.sem(f"{tag}_value_out")
        flat = b.ps[:, :, :].rearrange("p k n -> p (k n)")

        def score_ps(n):
            return flat[:, (n % 2) * 1024:(n % 2) * 1024 + 1024]

        turn_ps = flat[:, 2048:3072]

        def value_ps(n):
            return b.ps[:, 6 + n % 2, 0:DV]

        with nc.Block() as block:
            @block.tensor
            def _(pe):
                ident = b.const("identity")

                def scores(n):
                    if n >= 2:
                        pe.wait_ge(biased, n - 1)
                    for col, lhsT, rhs in items[n][0]:
                        ins = mm(nc, score_ps(n)[:, col:col + rhs.shape[-1]], lhsT, rhs, True, True)
                    ins.then_inc(score_up, 1)

                def turn(n):
                    pe.wait_ge(exp_done, n + 1)
                    if n >= 1:
                        pe.wait_ge(prob_out, n)
                    for k in range(items[n][2] // P):
                        ins = nc.tensor.transpose(turn_ps[:, k * P:(k + 1) * P], prob[:, n % 2, k * P:(k + 1) * P], ident)
                    ins.then_inc(prob_up, 1)

                def values(n):
                    pe.wait_ge(prob_out, n + 1)
                    if n >= 2:
                        pe.wait_ge(value_out, n - 1)
                    rhs = items[n][3]
                    for k in range(len(rhs)):
                        ins = mm(nc, value_ps(n), prob_t[:, n % 2, k * P:(k + 1) * P], rhs[k], k == 0, k == len(rhs) - 1)
                    ins.then_inc(value_up, 1)

                for n in range(N + 2):
                    if n == 1 and not beside:
                        warm_up(nc, b, 8)
                    if n < N:
                        scores(n)
                    if 0 <= n - 1 < N:
                        turn(n - 1)
                    if 0 <= n - 2:
                        values(n - 2)

            @block.vector
            def _(dve):
                for n in range(N + 1):
                    if n < N:
                        _p, bias, w, _v, _d = items[n]
                        dve.wait_ge(score_up, n + 1)
                        if n >= 2:
                            dve.wait_ge(exp_done, n - 1)
                        nc.vector.tensor_tensor_reduce(neg[:, n % 2, 0:w], score_ps(n)[:, 0:w], bias, -scale, 3e38,
                                                       ALU.add, ALU.min, neg_max[:, n:n + 1]).then_inc(biased, 1)
                        if beside:
                            beside(dve, n)
                    if n >= 1:
                        m = n - 1
                        dve.wait_ge(exp_done, m + 1)
                        nc.vector.reciprocal(inverse[:, m:m + 1], total[:, m:m + 1]).then_inc(inverted, 1)
                        if m % 2 == 0:
                            w = items[m][2]
                            dve.wait_ge(prob_up, m + 1)
                            if m >= 2:
                                dve.wait_ge(value_up, m - 1)
                            nc.vector.tensor_copy(prob_t[:, m % 2, 0:w], turn_ps[:, 0:w]).then_inc(prob_out, 1)

            @block.scalar
            def _(act):
                for n in range(N + 2):
                    if n < N:
                        w = items[n][2]
                        act.wait_ge(biased, n + 1)
                        if n >= 2:
                            act.wait_ge(prob_up, n - 1)
                        nc.scalar.activation(prob[:, n % 2, 0:w], neg[:, n % 2, 0:w], ACT.Exp, bias=neg_max[:, n:n + 1],
                                             scale=-1.0, accum_out=total[:, n:n + 1]).then_inc(exp_done, 1)
                    m = n - 1
                    if 0 <= m < N and m % 2 == 1:
                        w = items[m][2]
                        act.wait_ge(prob_up, m + 1)
                        if m >= 2:
                            act.wait_ge(value_up, m - 1)
                        nc.scalar.activation(prob_t[:, m % 2, 0:w], turn_ps[:, 0:w], ACT.Copy).then_inc(prob_out, 1)
                    m = n - 2
                    if m >= 0:
                        act.wait_ge(value_up, m + 1)
                        act.wait_ge(inverted, m + 1)
                        nc.scalar.activation(items[m][4], value_ps(m), ACT.Copy,
                                             scale=inverse[:, m:m + 1]).then_inc(value_out, 1)


def stage_index_scores(nc, b, q_idx_t, k_idx_t, w_idx, score, bias):
    FILL = -1e37
    items = [(i, h) for i in range(1, TT) for h in range(HEADS)]
    with ExitStack() as own:
        relu = own.enter_context(nc.sbuf_tensor("idx_relu", [P, 2, S], F32))
        up = b.sem("idx_up")
        relu_done = b.sem("idx_relu_done")
        added = b.sem("idx_added")
        with nc.Block() as block:
            @block.tensor
            def _(pe):
                for n, (i, h) in enumerate(items):
                    if n >= 4:
                        pe.wait_ge(relu_done, n - 3)
                    at = 32 * (h % 4)
                    mm(nc, b.ps[:, n % 4, 0:(i + 1) * P], q_idx_t[at:at + 32, h // 4, i * P:(i + 1) * P],
                       k_idx_t[at:at + 32, 0:(i + 1) * P], True, True).then_inc(up, 1)

            @block.scalar
            def _(act):
                for n, (i, h) in enumerate(items):
                    act.wait_ge(up, n + 1)
                    if n >= 2:
                        act.wait_ge(added, n - 1)
                    nc.scalar.activation(relu[:, n % 2, 0:(i + 1) * P], b.ps[:, n % 4, 0:(i + 1) * P], ACT.Relu,
                                         scale=IDX ** -0.5).then_inc(relu_done, 1)

            @block.vector
            def _(dve):
                causal = b.const("causal_bias")
                for n, (i, h) in enumerate(items):
                    w = (i + 1) * P
                    dve.wait_ge(relu_done, n + 1)
                    if h:
                        dve.wait_ge(added, n)
                        ins = nc.vector.scalar_tensor_tensor(score[:, i, 0:w], relu[:, n % 2, 0:w], w_idx(i, h),
                                                             score[:, i, 0:w], ALU.mult, ALU.add)
                    else:
                        ins = nc.vector.tensor_scalar(score[:, i, 0:w], relu[:, n % 2, 0:w], w_idx(i, h), None, ALU.mult)
                    ins.then_inc(added, 1)
                dve.wait_ge(added, len(items))
                nc.vector.tensor_copy(bias[:, 0, 0:P], causal)
                for i in range(1, TT):
                    nc.vector.scalar_tensor_tensor(score[:, i, i * P:(i + 1) * P], causal, FILL / NEG,
                                                   score[:, i, i * P:(i + 1) * P], ALU.mult, ALU.add)


class Selection:

    def __init__(self, nc, b, own, score, bias):
        self.nc, self.score, self.bias = nc, score, bias
        self.best = own.enter_context(nc.sbuf_tensor("idx_best", [P, 2, 8], F32))
        self.sem = b.sem("select_chain")
        self.link = None

    def __call__(self, dve, n):
        TAKEN = -3e38
        nc = self.nc
        self.link = self.link or Chain(dve, self.sem)
        i, h = n // HEADS + 1, n % HEADS
        if i == TT:
            return
        w = (i + 1) * P
        row = self.score[:, i, 0:w]
        for r in range(TOPK // 8 // HEADS):
            self.link(nc.vector.max(self.best[:, r % 2, :], row))
            self.link(nc.vector.match_replace(row, self.best[:, r % 2, :], row, TAKEN))
        if h == HEADS - 1:
            self.link(nc.vector.tensor_scalar(self.bias[:, i, 0:w], row, -2e38, NEG, ALU.is_gt, ALU.mult))


def stage_gated_up(nc, b, d, h, o_a, o_b, z):
    w_in_v = d["w_in"].rearrange("a (k p) n -> p (a k) n", p=P)
    up_a = d["w_up_a"].rearrange("a (k p) n -> p (a k) n", p=P)
    up_b = d["w_up_b"].rearrange("a (k p) n -> p (a k) n", p=P)
    KA, KB = o_a[0].shape[1], o_b[0].shape[1]
    with ExitStack() as own:
        ws = WeightStream(nc, b, own, "gated", b.feat_slots)
        sig = b.tok[:, 0:2, :].rearrange("p j (g n) -> p j g n", g=2)
        part = b.tok[:, 2:4, :].rearrange("p j (g n) -> p j g n", g=2)
        sig_done = b.sem("gated_sig")
        read = b.sem("gated_read")
        z_sum = b.sem("gated_z_sum")
        z_hi_done = b.sem("gated_z_hi")
        z_done = b.sem("gated_z")
        with nc.Block() as block:
            @block.sync
            def _(sp):
                for m in range(DC):
                    ws.load(sp, 2 * m, 0, [(g * DC * P, DC, w_in_v[:, :, C_GATE + g * D + m * P:C_GATE + g * D + (m + 1) * P])
                                           for g in range(2)], m == 0)
                    ws.load(sp, 2 * m + 1, 1, [(0, KA, up_a[:, :, m * P:(m + 1) * P]),
                                               (KA * P, KB, up_b[:, :, m * P:(m + 1) * P])], m == 0)

            @block.tensor
            def _(pe):
                for m in range(DC):
                    bank = 4 * (m % 2)
                    pe.wait_ge(ws.lo_done, 2 * m + 1)
                    if m >= 2:
                        pe.wait_ge(read, 2 * (m - 1))
                    for g in range(2):
                        for k in range(DC):
                            ins = split_products(nc, b.ps[:, bank + g, :], ws.parts(0, (g * DC + k) * P, P),
                                                 (h[0][:, k, :], h[1][:, k, :]), k == 0, k == DC - 1)
                    ins.then_inc(ws.used, 1)
                    pe.wait_ge(ws.lo_done, 2 * m + 2)
                    for g, (o, k0, kn) in enumerate(((o_a, 0, KA), (o_b, KA, KB))):
                        for k in range(kn):
                            ins = split_products(nc, b.ps[:, bank + 2 + g, :], ws.parts(1, (k0 + k) * P, P),
                                                 (o[0][:, k, :], o[1][:, k, :]), k == 0, k == kn - 1)
                    ins.then_inc(ws.used, 1)

            @block.scalar
            def _(act):
                ws.round(act, 0, 0, 32, first=True)
                ws.round(act, 1, 1, 32, (KA + KB) * P, first=True)
                for m in range(DC):
                    j = m % 2
                    if m + 1 < DC:
                        ws.round(act, 2 * m + 2, 0, 32 * (m + 2))
                    act.wait_ge(ws.used, 2 * m + 1)
                    if m >= 2:
                        act.wait_ge(read, 2 * (m - 1))
                    nc.scalar.activation(sig[:, j, :, :], b.ps[:, 4 * j:4 * j + 2, :], ACT.Sigmoid).then_inc(sig_done, 1)
                    if m + 1 < DC:
                        ws.round(act, 2 * m + 3, 1, 32 * (m + 2), (KA + KB) * P)
                    act.wait_ge(z_sum, m + 1)
                    nc.scalar.activation(z[0][:, m, :], part[:, j, 0, :], ACT.Copy).then_inc(z_hi_done, 1)

            @block.vector
            def _(dve):
                ws.rest(dve, 0, 0)
                ws.rest(dve, 1, 1, (KA + KB) * P)
                for m in range(DC):
                    j = m % 2
                    if m + 1 < DC:
                        ws.rest(dve, 2 * m + 2, 0)
                        ws.rest(dve, 2 * m + 3, 1, (KA + KB) * P)
                    dve.wait_ge(sig_done, m + 1)
                    dve.wait_ge(ws.used, 2 * m + 2)
                    if m >= 2:
                        dve.wait_ge(z_done, m - 1)
                    for g in range(2):
                        nc.vector.tensor_tensor(part[:, j, g, :], sig[:, j, g, :], b.ps[:, 4 * j + 2 + g, :],
                                                ALU.mult).then_inc(read, 1)

            @block.gpsimd
            def _(pool):
                for m in range(DC):
                    z_m = part[:, m % 2, 0, :]
                    pool.wait_ge(read, 2 * (m + 1))
                    nc.gpsimd.tensor_tensor(z_m, z_m, part[:, m % 2, 1, :], ALU.add).then_inc(z_sum, 1)
                    pool.wait_ge(z_sum, m + 1)
                    pool.wait_ge(z_hi_done, m + 1)
                    nc.gpsimd.tensor_tensor(z[1][:, m, :], z_m, z[0][:, m, :], ALU.subtract).then_inc(z_done, 1)


def stage_retention(nc, b, q_t, k_t, v, y):
    with ExitStack() as own:
        kept = own.enter_context(nc.sbuf_tensor("ret_scores", [P, 2, TT, S], F32))
        up = b.sem("ret_up")
        out = b.sem("ret_out")
        y_up = b.sem("ret_y_up")
        y_out = b.sem("ret_y_out")
        mask = b.const("decay_mask")
        with nc.Block() as block:
            @block.tensor
            def _(pe):
                def scores(h):
                    at = DH * (h % 2)
                    for j in range(TT):
                        n = h * TT + j
                        if n >= 4:
                            pe.wait_ge(out, n - 3)
                        w = S - j * P
                        mm(nc, b.ps[:, j, 0:w], k_t[at:at + DH, h // 2, j * P:(j + 1) * P],
                           q_t[at:at + DH, h // 2, j * P:S], True, True).then_inc(up, 1)

                def sums(h):
                    pe.wait_ge(out, (h + 1) * TT)
                    if h >= 2:
                        pe.wait_ge(y_out, h - 1)
                    for i in range(TT):
                        for j in range(i + 1):
                            ins = mm(nc, b.ps[:, 4 + h % 2, i * DH:(i + 1) * DH],
                                     kept[:, h % 2, j, (i - j) * P:(i - j + 1) * P], v[:, j, h * DH:(h + 1) * DH],
                                     j == 0, j == i)
                    ins.then_inc(y_up, 1)

                for h in range(HEADS + 1):
                    if h < HEADS:
                        scores(h)
                    if h:
                        sums(h - 1)

            @block.vector
            def _(dve):
                for h in range(HEADS):
                    if h >= 2:
                        dve.wait_ge(y_up, h - 1)
                    for j in range(TT):
                        w = S - j * P
                        dve.wait_ge(up, h * TT + j + 1)
                        nc.vector.tensor_tensor(kept[:, h % 2, j, 0:w], b.ps[:, j, 0:w], mask[:, 0:w],
                                                ALU.mult).then_inc(out, 1)

            @block.scalar
            def _(act):
                for h in range(HEADS):
                    act.wait_ge(y_up, h + 1)
                    nc.scalar.activation(y[:, :, h * DH:(h + 1) * DH],
                                         b.ps[:, 4 + h % 2, 0:TT * DH].rearrange("p (i c) -> p i c", c=DH),
                                         ACT.Copy).then_inc(y_out, 1)


def stage_retention_norm(nc, b, y, gate):
    with ExitStack() as own:
        sq = b.tok
        mean = own.enter_context(nc.sbuf_tensor("ret_mean", [P, TT * HEADS], F32))
        var = own.enter_context(nc.sbuf_tensor("ret_var", [P, TT * HEADS], F32))
        chain = b.sem("ret_norm_chain")
        silu_done = b.sem("ret_silu")
        squares = b.sem("ret_squares")
        rooted = b.sem("ret_rooted")
        y3 = y[:, :, :].rearrange("p i (h c) -> p (i h) c", c=DH)
        s3 = sq[:, :, 0:RW].rearrange("p i (h c) -> p i h c", c=DH)
        y4 = y[:, :, :].rearrange("p i (h c) -> p i h c", c=DH)
        full = [P, TT * HEADS, DH]
        with nc.Block() as block:
            @block.scalar
            def _(act):
                nc.scalar.activation(gate, gate, ACT.Silu).then_inc(silu_done, 1)
                root_mean(nc, b, act, mean[:, :], DH, squares, 1, rooted)

            @block.vector
            def _(dve):
                link = Chain(dve, chain)
                link(nc.vector.tensor_reduce(mean[:, :], y3, AX.X, ALU.add))
                link(nc.vector.tensor_scalar(mean[:, :], mean[:, :], 1.0 / DH, None, ALU.mult))
                link(nc.vector.tensor_tensor(y3, y3, mean[:, :].unsqueeze(2).to_broadcast(full), ALU.subtract))
                link(nc.vector.tensor_tensor(s3, y4, y4, ALU.mult))
                link(nc.vector.tensor_reduce(var[:, :].rearrange("p (i h) -> p i h", h=HEADS), s3, AX.X, ALU.add))
                nc.vector.tensor_copy(mean[:, :], var[:, :]).then_inc(squares, 1)
                dve.wait_ge(rooted, 1)
                link(nc.vector.reciprocal(mean[:, :], mean[:, :]))
                link(nc.vector.tensor_tensor(y3, y3, mean[:, :].unsqueeze(2).to_broadcast(full), ALU.mult))
                dve.wait_ge(silu_done, 1)
                link(nc.vector.tensor_tensor(gate, gate, y[:, :, :], ALU.mult))


def stage_key_scores(nc, b, d, q_t, s):
    G = 2 * PH
    with ExitStack() as own:
        keys = own.enter_context(nc.sbuf_tensor("peer_keys", [NKEY, 2, KH], F32))
        keys_t = own.enter_context(nc.sbuf_tensor("peer_keys_t", [KH, 2, NKEY], F32))
        keys_in = b.sem("peer_keys_in")
        keys_up = b.sem("peer_keys_up")
        keys_out = b.sem("peer_keys_out")
        s_up = b.sem("peer_s_up")
        s_out = b.sem("peer_s_out")
        with nc.Block() as block:
            @block.sync
            def _(sp):
                sp.dma_start(keys[:, :, :], d["sub_keys_2"].rearrange("a g k c -> k (a g) c")).then_inc(keys_in, 16)

            @block.tensor
            def _(pe):
                pe.wait_ge(keys_in, 16)
                for g in range(2):
                    ins = nc.tensor.transpose(b.ps[:, 0, g * P:(g + 1) * P], keys[:, g, :], b.const("identity"))
                ins.then_inc(keys_up, 1)
                pe.wait_ge(keys_out, 1)
                for n in range(4 * TT):
                    if n >= 4:
                        pe.wait_ge(s_out, n - 3)
                    i, q = n // 4, n % 4
                    for g in range(4 * q, 4 * q + 4):
                        ins = mm(nc, b.ps[:, 4 + q, (g % 4) * P:(g % 4 + 1) * P], q_t[:, g, i * P:(i + 1) * P],
                                 keys_t[:, g % 2, :], True, True)
                    ins.then_inc(s_up, 1)

            @block.scalar
            def _(act):
                act.wait_ge(keys_up, 1)
                nc.scalar.activation(keys_t[:, :, :].rearrange("p g k -> p (g k)"), b.ps[:, 0, 0:2 * P],
                                     ACT.Copy).then_inc(keys_out, 1)
                for n in range(4 * TT):
                    i, q = n // 4, n % 4
                    act.wait_ge(s_up, n + 1)
                    nc.scalar.activation(s[:, i, 4 * q:4 * q + 4, :].rearrange("p g k -> p (g k)"),
                                         b.ps[:, 4 + q, :], ACT.Copy).then_inc(s_out, 1)


def stage_experts(nc, b, d, s):
    G = 2 * PH
    R = 8
    NE = PH * PK
    STEPS = NE // R
    SHARES, HS = 4, 2
    LAST = TT - 1
    u_rows = d["expert_u_2"].rearrange("a e n -> (a e) n")
    v_rows = d["expert_v_2"].rearrange("a e n -> (a e) n")
    h2 = b.tok
    with ExitStack() as own:
        def sb(name, shape, dt=F32):
            return own.enter_context(nc.sbuf_tensor(name, shape, dt))

        expert = sb("expert", [P, TT, NE], U32)
        weight = sb("expert_weight", [P, TT, NE])
        top = sb("peer_top", [P, G, PK])
        top_i = sb("peer_top_i", [P, G, PK], U32)
        top_f = sb("peer_top_f", [P, G, PK])
        cand = sb("peer_cand", [P, PH, PK, PK])
        hot = cand
        best = sb("peer_best", [P, PH, PK])
        pos = sb("peer_pos", [P, PH, PK], U32)
        part_i = sb("peer_part_i", [P, 2, PH, PK], U32)
        part_f = sb("peer_part_f", [P, 2, PH, PK])
        chosen = sb("peer_chosen", [P, 2, PH, PK])
        sums = sb("peer_sums", [P, 2 * PH])
        u = sb("u_rows", [P, R, D])
        v = sb("v_rows", [P, R, D])
        half_sum = u[:, 0, 0:512]
        dots = sb("peer_dots", [P, NE])
        dot_cells = sb("peer_dot_cells", [P, R])
        act_w = sb("peer_act_w", [P, 2, NE])
        diag = sb("peer_diag", [P, 4, P])
        u_in = [b.sem(f"u_in{r}") for r in range(R)]
        v_in = [b.sem(f"v_in{r}") for r in range(R)]
        chain = b.sem("peer_route_chain")
        routed = b.sem("peer_routed")
        dot_done = b.sem("dot_done")
        dots_kept = b.sem("dots_kept")
        gelu_done = b.sem("gelu_done")
        act_w_done = b.sem("act_w_done")
        diag_done = b.sem("diag_done")
        v_used = b.sem("v_used")
        half_used = b.sem("v_half_used")
        y_out = b.sem("peer_y_out")
        with nc.Block() as block:
            @block.gpsimd
            def _(pool):
                def gather(i, k, rows, table, arrived, used):
                    r = k % R
                    if i * NE + k >= R:
                        pool.wait_ge(used, i * NE + k - R + 1)
                    nc.gpsimd.indirect_dma_start(
                        out=rows[:, r, :], out_offset=None, in_=table,
                        in_offset=bass.IndirectOffsetOnAxis(ap=expert[:, i, k:k + 1], axis=0),
                    ).then_inc(arrived[r], 16)

                for i in range(-1, TT):
                    for k in range(NE):
                        if i + 1 < TT:
                            if k % (NE // SHARES) == 0:
                                pool.wait_ge(routed, (i + 1) * SHARES + k // (NE // SHARES) + 1)
                            gather(i + 1, k, u, u_rows, u_in, dot_done)
                        if i >= 0:
                            if i == LAST and k >= R and k % 2:
                                pool.wait_ge(half_used, (k - R) // 2 + 1)
                            gather(i, k, v, v_rows, v_in, v_used)

            @block.vector
            def _(dve):
                link = Chain(dve, chain)

                def best_keys(i, q):
                    groups = range(2 * HS * q, 2 * HS * (q + 1))
                    for half in range(2):
                        at = slice(8 * half, 8 * half + 8)
                        for g in groups:
                            ins = nc.vector.max(top[:, g, at], s[:, i, g, :])
                        link(ins)
                        for g in groups:
                            ins = nc.vector.max_index(top_i[:, g, at], top[:, g, at], s[:, i, g, :])
                        if half:
                            link(ins)
                        else:
                            for g in groups:
                                ins = nc.vector.match_replace(s[:, i, g, :], top[:, g, at], s[:, i, g, :], -3e38)
                            link(ins)
                    at = slice(groups[0], groups[-1] + 1)
                    link(nc.vector.tensor_copy(top_f[:, at, :], top_i[:, at, :]))

                def best_pairs(i, q):
                    heads = range(HS * q, HS * (q + 1))
                    hs = slice(heads[0], heads[-1] + 1)
                    for h in heads:
                        a = top[:, 2 * h, :].unsqueeze(2).to_broadcast([P, PK, PK])
                        c = top[:, 2 * h + 1, :].unsqueeze(1).to_broadcast([P, PK, PK])
                        ins = nc.vector.tensor_tensor(cand[:, h, :, :], a, c, ALU.add)
                    link(ins)
                    rows = {h: cand[:, h, :, :].rearrange("p a c -> p (a c)") for h in heads}
                    for half in range(2):
                        at = slice(8 * half, 8 * half + 8)
                        for h in heads:
                            ins = nc.vector.max(best[:, h, at], rows[h])
                        link(ins)
                        for h in heads:
                            ins = nc.vector.max_index(pos[:, h, at], best[:, h, at], rows[h])
                        link(ins)
                        if half == 0:
                            for h in heads:
                                ins = nc.vector.match_replace(rows[h], best[:, h, at], rows[h], -3e38)
                            link(ins)
                    nc.vector.tensor_scalar(part_i[:, 0, hs, :], pos[:, hs, :], 4, None, ALU.logical_shift_right)
                    link(nc.vector.tensor_scalar(part_i[:, 1, hs, :], pos[:, hs, :], PK - 1, None, ALU.bitwise_and))
                    link(nc.vector.tensor_copy(part_f[:, :, hs, :], part_i[:, :, hs, :]))
                    iota = b.const("iota").unsqueeze(1).to_broadcast([P, HS * PK, PK])
                    hot3 = hot[:, hs, :, :].rearrange("p h k c -> p (h k) c")
                    for g in range(2):
                        rank = part_f[:, g, hs, :].rearrange("p h k -> p (h k)").unsqueeze(2).to_broadcast([P, HS * PK, PK])
                        link(nc.vector.tensor_tensor(hot3, rank, iota, ALU.is_equal))
                        key = top_f[:, 2 * HS * q + g:2 * HS * (q + 1):2, :].unsqueeze(2).to_broadcast([P, HS, PK, PK])
                        link(nc.vector.tensor_tensor(hot[:, hs, :, :], hot[:, hs, :, :], key, ALU.mult))
                        link(nc.vector.tensor_reduce(chosen[:, g, hs, :].rearrange("p h k -> p (h k)"), hot3, AX.X, ALU.add))
                    c0 = chosen[:, 0, hs, :].rearrange("p h k -> p (h k)")
                    c1 = chosen[:, 1, hs, :].rearrange("p h k -> p (h k)")
                    at = slice(q * HS * PK, (q + 1) * HS * PK)
                    nc.vector.scalar_tensor_tensor(expert[:, i, at], c0, float(NKEY), c1, ALU.mult, ALU.add)
                    w3 = weight[:, i, at].rearrange("p (h k) -> p h k", k=PK)
                    nc.vector.tensor_tensor(w3, best[:, hs, :], best[:, hs, 0:1].to_broadcast([P, HS, PK]),
                                            ALU.subtract).then_inc(routed, 1)
                    dve.wait_ge(routed, i * SHARES + q + 1)

                def route(i, q):
                    best_keys(i, q)
                    best_pairs(i, q)

                def dot_steps(i, first, last):
                    with dve.Fori(first, last) as t:
                        for r in range(R):
                            dve.wait_ge(u_in[r], (t + i * STEPS + 1) * 16)
                            nc.vector.tensor_tensor_reduce(u[:, r, :], u[:, r, :], h2[:, i, :], 1.0, 0.0, ALU.mult,
                                                           ALU.add, dot_cells[:, r:r + 1]).then_inc(dot_done, 1)
                        dve.wait_ge(dot_done, (t + i * STEPS + 1) * R)
                        nc.vector.tensor_copy(dots[:, bass.ds(t * R, R)], dot_cells[:, :]).then_inc(dots_kept, 1)
                        dve.wait_ge(dots_kept, t + i * STEPS + 1)

                def row_weights(i):
                    w3 = weight[:, i, :].rearrange("p (h k) -> p h k", k=PK)
                    dve.wait_ge(gelu_done, 2 * (i + 1))
                    link(nc.vector.tensor_reduce(sums[:, 0:PH], w3, AX.X, ALU.add))
                    link(nc.vector.reciprocal(sums[:, PH:2 * PH], sums[:, 0:PH]))
                    link(nc.vector.tensor_tensor(w3, w3, sums[:, PH:2 * PH].unsqueeze(2).to_broadcast([P, PH, PK]),
                                                 ALU.mult))
                    nc.vector.tensor_tensor(act_w[:, i % 2, :], act_w[:, i % 2, :], weight[:, i, :],
                                            ALU.mult).then_inc(act_w_done, 1)

                def half_rows(t, first=False):
                    for n, r in enumerate(range(1, R, 2)):
                        dve.wait_ge(v_in[r], (t + LAST * STEPS + 1) * 16)
                        row = v[:, r, 512:1024]
                        w = act_w[:, LAST % 2, bass.ds(t * R + r, 1)]
                        if first and n == 0:
                            ins = nc.vector.tensor_scalar(half_sum, row, w, None, ALU.mult)
                        else:
                            dve.wait_ge(half_used, t * (R // 2) + n)
                            ins = nc.vector.scalar_tensor_tensor(half_sum, row, w, half_sum, ALU.mult, ALU.add)
                        ins.then_inc(half_used, 1)

                PER = STEPS // SHARES
                route(0, 0)
                for i in range(TT):
                    for q in range(SHARES):
                        dot_steps(i, q * PER, q * PER + PER // 2)
                        if q + 1 < SHARES:
                            route(i, q + 1)
                        elif i + 1 < TT:
                            route(i + 1, 0)
                        dot_steps(i, q * PER + PER // 2, (q + 1) * PER)
                    row_weights(i)
                dve.wait_ge(act_w_done, TT)
                dve.wait_ge(dot_done, TT * NE)
                half_rows(0, first=True)
                with dve.Fori(1, STEPS) as t:
                    half_rows(t)
                dve.wait_ge(v_used, TT * NE)
                dve.wait_ge(half_used, NE // 2)
                nc.vector.tensor_tensor(b.tok[:, LAST, 512:1024], b.ps[:, 2 * (LAST % 2) + 1, :], half_sum, ALU.add)

            @block.scalar
            def _(act):
                def diagonals(i, t, g):
                    for r in range(2 * g, 2 * g + 2):
                        nc.scalar.activation(diag[:, r, :], b.const("identity"), ACT.Copy,
                                             scale=act_w[:, i % 2, bass.ds(t * 4 + r, 1)]).then_inc(diag_done, 1)

                for i in range(TT):
                    act.wait_ge(dots_kept, (i + 1) * STEPS)
                    nc.scalar.activation(act_w[:, i % 2, :], dots[:, :], ACT.Gelu).then_inc(gelu_done, 1)
                    nc.scalar.activation(weight[:, i, :], weight[:, i, :], ACT.Exp).then_inc(gelu_done, 1)
                    act.wait_ge(act_w_done, i + 1)
                    if i == 0:
                        diagonals(0, 0, 0)
                        diagonals(0, 0, 1)
                    with act.Fori(0 if i else 1, NE // 4) as t:
                        for g in range(2):
                            act.wait_ge(v_used, t * 4 + 2 * g + i * NE - 2)
                            diagonals(i, t, g)
                    act.wait_ge(v_used, (i + 1) * NE)
                    for half in range(1 if i == LAST else 2):
                        ins = nc.scalar.activation(b.tok[:, i, half * 512:half * 512 + 512],
                                                   b.ps[:, 2 * (i % 2) + half, :], ACT.Copy)
                    ins.then_inc(y_out, 1)

            @block.tensor
            def _(pe):
                def rows(t, r, i, start, stop):
                    pe.wait_ge(v_in[r], (t + i * STEPS + 1) * 16)
                    pe.wait_ge(diag_done, t * R + r + i * NE + 1)
                    for half in range(1 if i == LAST and r % 2 else 2):
                        ins = mm(nc, b.ps[:, 2 * (i % 2) + half, :], diag[:, r % 4, :],
                                 v[:, r, half * 512:half * 512 + 512], start, stop)
                    ins.then_inc(v_used, 1)

                for i in range(TT):
                    if i >= 2:
                        pe.wait_ge(y_out, i - 1)
                    for r in range(R):
                        rows(0, r, i, r == 0, False)
                    with pe.Fori(1, STEPS - 1) as t:
                        for r in range(R):
                            rows(t, r, i, False, False)
                    for r in range(R):
                        rows(STEPS - 1, r, i, False, r == R - 1 or (i == LAST and r == R - 2))


def stage_output(nc, b, tag, w_src, o, add_row=None):
    def lhsT(k, i):
        return o[0][:, k, i * P:(i + 1) * P], o[1][:, k, i * P:(i + 1) * P]

    jobs = []
    for at in (slice(0, 512), slice(512, D)):
        jobs.append((w_src[:, at], lhsT, lambda i, ps, at=at: [(b.tok[:, i, at], ps)]))
    with ExitStack() as own:
        stage_project_split(nc, b, tag, jobs, WeightStream(nc, b, own, tag, b.feat_slots), add_row)


def stage_final(nc, b, out):
    added = b.sem("final_added")
    squares = b.sem("final_squares")
    chain = b.sem("final_chain")
    ready = b.sem("final_ready")
    rooted = b.sem("final_rooted")
    rstd = b.sem("final_rstd")
    stored = b.sem("final_stored")
    dst = out.rearrange("a (i p) n -> p (a i) n", p=P)
    with nc.Block() as block:
        @block.vector
        def _(dve):
            link = Chain(dve, chain)
            for i in range(TT):
                link(nc.vector.tensor_tensor(b.tok[:, i, :], b.tok[:, i, :], b.rows[:, 4, :], ALU.mult))
                nc.vector.tensor_tensor(b.x[:, i, :], b.x[:, i, :], b.tok[:, i, :], ALU.add).then_inc(added, 1)
            dve.wait_ge(rooted, 1)
            nc.vector.reciprocal(b.stat[:, :], b.stat[:, :]).then_inc(rstd, 1)
            dve.wait_ge(rstd, 1)
            for i in range(TT):
                nc.vector.scalar_tensor_tensor(b.tok[:, i, :], b.x[:, i, :], b.stat[:, i:i + 1], b.rows[:, 5, :],
                                               ALU.mult, ALU.mult).then_inc(ready, 1)

        @block.scalar
        def _(act):
            for i in range(TT):
                act.wait_ge(added, i + 1)
                nc.scalar.activation(b.feat[:, 2 * i:2 * i + 2, :].rearrange("p a n -> p (a n)"), b.x[:, i, :],
                                     ACT.Square, accum_out=b.stat[:, i:i + 1]).then_inc(squares, 1)
            root_mean(nc, b, act, b.stat[:, :], D, squares, TT, rooted)

        @block.sync
        def _(sp):
            for i in range(TT):
                sp.wait_ge(ready, i + 1)
                sp.dma_start(dst[:, i, :], b.tok[:, i, :]).then_inc(stored, 16)
            sp.wait_ge(stored, 16 * TT)


def cols3(t, i, c0, heads, width):
    return t[:, i, c0:c0 + heads * width].rearrange("p (h c) -> p h c", c=width)


def rope_items(b, t, heads, width, at, half, table, pos):
    out = []
    for i in range(TT):
        v = t[:, i, :].rearrange("p (h c) -> p h c", c=width)
        cos = b.cos[:, pos * TT + i, table:table + half].unsqueeze(1).to_broadcast([P, heads, half])
        sin = b.sin[:, pos * TT + i, table:table + half].unsqueeze(1).to_broadcast([P, heads, half])
        out.append((v[:, :, at:at + half], v[:, :, at + half:at + 2 * half], cos, sin))
    return out


def mixer_one(nc, b, d):
    w_in = d["w_in"].rearrange("a k n -> (a k) n")
    HQ = GRP * HB
    with ExitStack() as mix:
        latents = mix.enter_context(ExitStack())
        lat = latents.enter_context(nc.sbuf_tensor("latents", [P, TT, C_QKV], F32))
        oa_t = b.tok[:, 0:2, :].rearrange("p a (c n) -> p (a c) n", n=S)
        ob_t = b.tok[:, 2, :].rearrange("p (c n) -> p c n", n=S)
        with ExitStack() as dil:
            qk = dil.enter_context(nc.sbuf_tensor("dil_qk", [P, TT, 2 * HQ * DH], F32))
            v = dil.enter_context(nc.sbuf_tensor("dil_v", [P, TT, HQ * DH], F32))

            def jobs_of(h):
                def plain(k, i):
                    return h[0][:, k, i * P:(i + 1) * P], h[1][:, k, i * P:(i + 1) * P]

                def strided(k, r):
                    return h[0][:, k, r:S:TT], h[1][:, k, r:S:TT]

                jobs = []
                for at, w in ((0, 512), (512, C_QKV - 512)):
                    jobs.append((w_in[:, at:at + w], plain, lambda i, ps, at=at, w=w: [(lat[:, i, at:at + w], ps)]))
                for n in range(3):
                    at = C_QKV + 512 * n
                    jobs.append((w_in[:, at:at + 512], plain,
                                 lambda i, ps, n=n: [(qk[:, i, 512 * n:512 * n + 512], ps)]))
                for n in range(2):
                    at = C_QKV + 2 * HQ * DH + 384 * n
                    jobs.append((w_in[:, at:at + 384], strided,
                                 lambda i, ps, n=n: [(v[:, i, 384 * n:384 * n + 384], ps)]))
                return jobs

            norm_and_project(nc, b, "in1", 1, 3, jobs_of)

            ropes = []
            ropes += rope_items(b, qk, 2 * HQ, DH, 0, DH // 2, ROPE_A // 2, 0)
            ropes += rope_items(b, lat[:, :, C_KR:C_KR + ROPE_A], 1, ROPE_A, 0, ROPE_A // 2, 0, 0)
            ropes += rope_items(b, lat[:, :, C_KI:C_KI + IDX], 1, IDX, 0, IDX // 2, 0, 0)
            norms = [(lambda i: lat[:, i, 0:QL], QL), (lambda i: lat[:, i, C_CKV:C_CKV + KVL], KVL)]
            stage_norm_rope(nc, b, "nr1", norms, ropes)

            with ExitStack() as att:
                qk_t = att.enter_context(nc.sbuf_tensor("dil_qk_t", [P, HQ, S], F32))
                bias = att.enter_context(nc.sbuf_tensor("dil_bias", [P, TT, S + 2 * P], F32))
                o = att.enter_context(nc.sbuf_tensor("dil_o", [P, TT, HB * DH], F32))
                bias_in = b.sem("dil_bias_in")
                with nc.Block() as block:
                    @block.sync
                    def _(sp):
                        sp.dma_start(bias[:, :, :], d["dilated_bias"].rearrange("p (r n) -> p r n", r=TT)).then_inc(bias_in, 16)
                        sp.wait_ge(bias_in, 16)
                stage_turn(nc, b, "dqk", [(lambda i, n=n: qk[:, i, n * P:(n + 1) * P], P, qk_t[:, n, :], None)
                                          for n in range(HQ)])
                items = []
                for r in range(TT):
                    for h in range(HB):
                        prods, vals = [], []
                        for g in range(GRP):
                            hq = g * HB + h
                            at = DH * (hq % 2)
                            q = qk_t[at:at + DH, hq // 2, r:S:TT]
                            kc = (HQ + hq) // 2
                            if g == 0:
                                for r2 in range(TT):
                                    prods.append((r2 * P, q, qk_t[at:at + DH, kc, r2:S:TT]))
                                    vals.append(v[:, r2, hq * DH:(hq + 1) * DH])
                            else:
                                prods.append((S + (g - 1) * P, q, qk_t[at:at + DH, kc, r:S:TT]))
                                vals.append(v[:, r, hq * DH:(hq + 1) * DH])
                        items.append((prods, bias[:, r, :], S + 2 * P, vals, o[:, r, h * DH:(h + 1) * DH]))
                stage_attention(nc, b, "dil", items, S + 2 * P, DH ** -0.5)
                with nc.Block() as block:
                    o_up = b.sem("dil_o_up")

                    @block.tensor
                    def _(pe):
                        for k in range(2):
                            for r in range(TT):
                                ins = nc.tensor.transpose(b.ps[:, k, r * P:(r + 1) * P], o[:, r, k * P:(k + 1) * P],
                                                          b.const("identity"))
                            ins.then_inc(o_up, 1)

                    @block.vector
                    def _(dve):
                        for k in range(2):
                            dve.wait_ge(o_up, k + 1)
                            nc.vector.tensor_copy(ob_t[:, k, :].rearrange("p (n r) -> p r n", r=TT),
                                                  b.ps[:, k, :].rearrange("p (r n) -> p r n", r=TT))

        with ExitStack() as dsa:
            q_t = dsa.enter_context(nc.sbuf_tensor("dsa_q_t", [DQ, HEADS, S], F32))
            k_t = dsa.enter_context(nc.sbuf_tensor("dsa_k_t", [DQ, HEADS, S], F32))
            v = dsa.enter_context(nc.sbuf_tensor("dsa_v", [P, TT, HEADS * DV], F32))
            qi_t = dsa.enter_context(nc.sbuf_tensor("idx_q_t", [P, 2, S], F32))
            ki_t = dsa.enter_context(nc.sbuf_tensor("idx_k_t", [P, S], F32))
            with ExitStack() as prep:
                lat_t = prep.enter_context(nc.sbuf_tensor("lat_t", [P, 5, S], F32))
                q = prep.enter_context(nc.sbuf_tensor("dsa_q", [P, TT, HEADS * DQ], F32))
                kk = prep.enter_context(nc.sbuf_tensor("dsa_k", [P, TT, HEADS * DQ], F32))
                qi = prep.enter_context(nc.sbuf_tensor("idx_q", [P, TT, HEADS * IDX], F32))
                ki = prep.enter_context(nc.sbuf_tensor("idx_k", [P, TT, P], F32))
                gq, gkv = VEC_AT["g_cq"], VEC_AT["g_ckv"]
                jobs = [(lambda i, n=n: lat[:, i, n * P:(n + 1) * P], P, lat_t[:, n, :],
                         b.vec[:, gq + n:gq + n + 1] if n < 3 else b.vec[:, gkv + n - 3:gkv + n - 2]) for n in range(5)]
                stage_turn(nc, b, "lat1", jobs)
                w_uq = d["w_uq"].rearrange("a k h c -> (a k) (h c)")
                w_uk = d["w_uk"].rearrange("a k h c -> (a k) (h c)")
                w_uv = d["w_uv"].rearrange("a k h c -> (a k) (h c)")
                w_iq = d["w_iq"].rearrange("a k h c -> (a k) (h c)")

                def from_q(k, i):
                    return lat_t[:, k, i * P:(i + 1) * P]

                def from_kv(k, i):
                    return lat_t[:, 3 + k, i * P:(i + 1) * P]

                jobs = [(w_uq[:, n * 384:n * 384 + 384], 3, from_q,
                         lambda i, ps, n=n: [(q[:, i, n * 384:n * 384 + 384], ps)]) for n in range(2)]
                jobs.append((w_iq, 3, from_q, lambda i, ps: [(qi[:, i, :], ps)]))
                jobs.append((w_uk, 2, from_kv,
                             lambda i, ps: [(cols3(kk, i, 0, HEADS, DQ)[:, :, 0:NOPE],
                                             ps.rearrange("p (h c) -> p h c", c=NOPE))]))
                jobs.append((w_uv, 2, from_kv, lambda i, ps: [(v[:, i, :], ps)]))
                stage_project(nc, b, "uq1", jobs, 3)
                ropes = rope_items(b, q, HEADS, DQ, NOPE, ROPE_A // 2, 0, 0)
                ropes += rope_items(b, qi, HEADS, IDX, 0, IDX // 2, 0, 0)
                copies = []
                for i in range(TT):
                    copies.append((cols3(kk, i, 0, HEADS, DQ)[:, :, NOPE:DQ],
                                   lat[:, i, C_KR:C_KR + ROPE_A].unsqueeze(1).to_broadcast([P, HEADS, ROPE_A])))
                    copies.append((ki[:, i, :].rearrange("p (a c) -> p a c", c=IDX),
                                   lat[:, i, C_KI:C_KI + IDX].unsqueeze(1).to_broadcast([P, 4, IDX])))
                stage_norm_rope(nc, b, "nr2", [], ropes, copies)
                jobs = [(lambda i, n=n: qi[:, i, n * P:(n + 1) * P], P, qi_t[:, n, :], None) for n in range(2)]
                jobs.append((lambda i: ki[:, i, :], P, ki_t[:, :], None))
                for src, dst in ((q, q_t), (kk, k_t)):
                    jobs += [(lambda i, h=h, src=src: src[:, i, h * DQ:(h + 1) * DQ], DQ, dst[:, h, :], None)
                             for h in range(HEADS)]
                stage_turn(nc, b, "dsaqk", jobs)
            with ExitStack() as att:
                bias = att.enter_context(nc.sbuf_tensor("dsa_bias", [P, TT, S], F32))
                wi = att.enter_context(nc.sbuf_tensor("idx_w", [P, TT, HEADS], F32))
                with nc.Block() as block:
                    @block.vector
                    def _(dve):
                        nc.vector.tensor_scalar(wi[:, :, :], lat[:, :, C_WI:C_WI + HEADS], float(HEADS ** -0.5), None, ALU.mult)
                score = att.enter_context(nc.sbuf_tensor("idx_score", [P, TT, S], F32))
                stage_index_scores(nc, b, qi_t, ki_t, lambda i, h: wi[:, i, h:h + 1], score, bias)
                latent_attention(nc, b, "dsa", q_t, k_t, v, lambda i: bias[:, i, 0:(i + 1) * P], oa_t,
                                 Selection(nc, b, att, score, bias))
        latents.close()
        z = b.split_pair(mix, "z", DC)
        with ExitStack() as gated:
            h = b.split_pair(gated, "gated_h", DC)
            o_a = b.split_pair(gated, "branch_a", 4)
            o_b = b.split_pair(gated, "branch_b", 2)
            stage_split(nc, b, "gated_split", [(b.feat, *h), (oa_t, *o_a), (ob_t, *o_b)])
            stage_gated_up(nc, b, d, h, o_a, o_b, z)
        stage_output(nc, b, "o1", d["w_o"].rearrange("a k n -> (a k) n"), z)


def latent_attention(nc, b, tag, q_t, k_t, v, bias, o_t, beside=None):
    with ExitStack() as own:
        o = own.enter_context(nc.sbuf_tensor(f"{tag}_o", [P, TT, HEADS * DV], F32))
        items = []
        for i in range(TT):
            for h in range(HEADS):
                w = (i + 1) * P
                items.append(([(0, q_t[:, h, i * P:w], k_t[:, h, 0:w])], bias(i), w,
                              [v[:, k, h * DV:(h + 1) * DV] for k in range(i + 1)], o[:, i, h * DV:(h + 1) * DV]))
        stage_attention(nc, b, tag, items, S, DQ ** -0.5, beside)
        stage_turn(nc, b, f"{tag}o", [(lambda i, n=n: o[:, i, n * P:(n + 1) * P], P, o_t[:, n, :], None)
                                      for n in range(4)])


def mixer_two(nc, b, d):
    w_in = d["w_in_2"].rearrange("a k n -> (a k) n")
    with ExitStack() as mix:
        y_t = b.tok[:, :, :].rearrange("p i (a n) -> p (i a) n", n=S)
        lat = mix.enter_context(nc.sbuf_tensor("latents2", [P, TT, C2_RET], F32))
        with ExitStack() as heads:
            rq = heads.enter_context(nc.sbuf_tensor("ret_q", [P, TT, RW], F32))
            rk = heads.enter_context(nc.sbuf_tensor("ret_k", [P, TT, RW], F32))
            rv = heads.enter_context(nc.sbuf_tensor("ret_v", [P, TT, RW], F32))
            rg = heads.enter_context(nc.sbuf_tensor("ret_g", [P, TT, RW], F32))

            def jobs_of(h):
                def plain(k, i):
                    return h[0][:, k, i * P:(i + 1) * P], h[1][:, k, i * P:(i + 1) * P]

                jobs = [(w_in[:, 0:C2_RET], plain, lambda i, ps: [(lat[:, i, :], ps)])]
                for n, t in enumerate((rq, rk, rv, rg)):
                    at = C2_RET + n * RW
                    jobs.append((w_in[:, at:at + RW], plain, lambda i, ps, t=t: [(t[:, i, :], ps)]))
                return jobs

            norm_and_project(nc, b, "in2", 3, 9, jobs_of)
            ropes = rope_items(b, rq, HEADS, DH, 0, DH // 2, ROPE_A // 2, 1)
            ropes += rope_items(b, rk, HEADS, DH, 0, DH // 2, ROPE_A // 2, 1)
            ropes += rope_items(b, lat[:, :, C2_KR:C2_KR + ROPE_A], 1, ROPE_A, 0, ROPE_A // 2, 0, 1)
            norms = [(lambda i: lat[:, i, 0:QL2], QL2), (lambda i: lat[:, i, QL2:QL2 + KVL2], KVL2)]
            decays = []
            for t, name in ((rq, "q_decay"), (rk, "k_decay")):
                for i in range(TT):
                    f = b.const(name)[:, i * HEADS:(i + 1) * HEADS].unsqueeze(2).to_broadcast([P, HEADS, DH])
                    decays.append((cols3(t, i, 0, HEADS, DH), f))
            stage_norm_rope(nc, b, "nr3", norms, ropes, (), decays)
            with ExitStack() as ret:
                q_t = ret.enter_context(nc.sbuf_tensor("ret_q_t", [P, 4, S], F32))
                k_t = ret.enter_context(nc.sbuf_tensor("ret_k_t", [P, 4, S], F32))
                stage_turn(nc, b, "ret", [(lambda i, n=n, t=t: t[:, i, n * P:(n + 1) * P], P, dst[:, n, :], None)
                                          for t, dst in ((rq, q_t), (rk, k_t)) for n in range(4)])
                stage_retention(nc, b, q_t, k_t, rv, rq)
            stage_retention_norm(nc, b, rq, rg[:, :, :])
            g = VEC_AT["g_ret_norm_2"]
            stage_turn(nc, b, "reto", [(lambda i, n=n: rg[:, i, n * P:(n + 1) * P], P, y_t[:, 4 + n, :],
                                        b.vec[:, g + n:g + n + 1]) for n in range(4)])
        with ExitStack() as mla:
            q_t = mla.enter_context(nc.sbuf_tensor("mla_q_t", [DQ, HEADS, S], F32))
            k_t = mla.enter_context(nc.sbuf_tensor("mla_k_t", [DQ, HEADS, S], F32))
            v = mla.enter_context(nc.sbuf_tensor("mla_v", [P, TT, HEADS * DV], F32))
            with ExitStack() as prep:
                lat_t = prep.enter_context(nc.sbuf_tensor("lat2_t", [P, 3, S], F32))
                q = prep.enter_context(nc.sbuf_tensor("mla_q", [P, TT, HEADS * DQ], F32))
                kk = prep.enter_context(nc.sbuf_tensor("mla_k", [P, TT, HEADS * DQ], F32))
                gq, gkv = VEC_AT["g_q_norm_2"], VEC_AT["g_kv_norm_2"]
                jobs = [(lambda i, n=n: lat[:, i, n * P:(n + 1) * P], P, lat_t[:, n, :],
                         b.vec[:, gq + n:gq + n + 1] if n < 2 else b.vec[:, gkv:gkv + 1]) for n in range(3)]
                stage_turn(nc, b, "lat2", jobs)
                w_uq = d["w_uq_2"].rearrange("a k n -> (a k) n")
                w_ukv = d["w_ukv_2"].rearrange("a k n -> (a k) n")

                def from_q(k, i):
                    return lat_t[:, k, i * P:(i + 1) * P]

                def from_kv(k, i):
                    return lat_t[:, 2, i * P:(i + 1) * P]

                def split_kv(n):
                    def stores(i, ps):
                        ps3 = ps.rearrange("p (h c) -> p h c", c=NOPE + DV)
                        k3 = cols3(kk, i, 0, HEADS, DQ)[:, 4 * n:4 * n + 4, 0:NOPE]
                        v3 = cols3(v, i, 0, HEADS, DV)[:, 4 * n:4 * n + 4, :]
                        return [(k3, ps3[:, :, 0:NOPE]), (v3, ps3[:, :, NOPE:NOPE + DV])]
                    return stores

                jobs = [(w_uq[:, n * 384:n * 384 + 384], 2, from_q,
                         lambda i, ps, n=n: [(q[:, i, n * 384:n * 384 + 384], ps)]) for n in range(2)]
                jobs += [(w_ukv[:, n * 512:n * 512 + 512], 1, from_kv, split_kv(n)) for n in range(2)]
                stage_project(nc, b, "uq2", jobs, 2)
                ropes = rope_items(b, q, HEADS, DQ, NOPE, ROPE_A // 2, 0, 1)
                copies = [(cols3(kk, i, 0, HEADS, DQ)[:, :, NOPE:DQ],
                           lat[:, i, C2_KR:C2_KR + ROPE_A].unsqueeze(1).to_broadcast([P, HEADS, ROPE_A]))
                          for i in range(TT)]
                stage_norm_rope(nc, b, "nr4", [], ropes, copies)
                jobs = []
                for src, dst in ((q, q_t), (kk, k_t)):
                    jobs += [(lambda i, h=h, src=src: src[:, i, h * DQ:(h + 1) * DQ], DQ, dst[:, h, :], None)
                             for h in range(HEADS)]
                stage_turn(nc, b, "mlaqk", jobs)
            with ExitStack() as att:
                bias = att.enter_context(nc.sbuf_tensor("mla_bias", [P, S + P], F32))
                with nc.Block() as block:
                    @block.vector
                    def _(dve):
                        nc.vector.memset(bias[:, 0:S - P], 0.0)
                        nc.vector.tensor_copy(bias[:, S - P:S], b.const("causal_bias"))
                latent_attention(nc, b, "mla", q_t, k_t, v, lambda i: bias[:, S - (i + 1) * P:S], y_t[:, 0:4, :])
        y = b.split_pair(mix, "y", DC)
        stage_split(nc, b, "y_split", [(y_t, *y)])
        stage_output(nc, b, "o2", d["w_out_2"].rearrange("a k n -> (a k) n"), y, add_row=3)


def peer(nc, b, d):
    with ExitStack() as own:
        scores = own.enter_context(nc.sbuf_tensor("peer_s", [P, TT, 2 * PH, NKEY], F32))
        with ExitStack() as route:
            q_t = route.enter_context(nc.sbuf_tensor("peer_q_t", [P, 2 * PH, S], F32))
            with ExitStack() as query:
                h_hi, h_lo = b.split_pair(query, "query_h", DC)
                stage_norm_turn(nc, b, "nt5", 4, 12, h_hi, h_lo, keep_tokens=b.tok)
                stage_queries(nc, b, d["w_query_2"], q_t, h_hi, h_lo)
            stage_key_scores(nc, b, d, q_t, scores)
        stage_experts(nc, b, d, scores)


def stage_queries(nc, b, w_query, q_t, h_hi, h_lo):
    NS = PH
    src = w_query.rearrange("a (k p) n -> p (a k) n", p=P)
    with ExitStack() as own:
        ws = WeightStream(nc, b, own, "query", b.feat_slots)
        first_up = b.sem("query_first_up")
        out = b.sem("query_out")
        with nc.Block() as block:
            @block.sync
            def _(sp):
                for m in range(NS):
                    ws.load(sp, m, m % 2, [(g * DC * P, DC, src[:, :, (2 * m + g) * P:(2 * m + g + 1) * P])
                                           for g in range(2)], m < 2)

            @block.tensor
            def _(pe):
                for m in range(NS):
                    pe.wait_ge(ws.lo_done, m + 1)
                    for g in range(2):
                        if m >= 2:
                            pe.wait_ge(out, 2 * m + g - 3)
                        for k in range(DC):
                            ins = split_products(nc, b.ps[:, (2 * m + g) % 4, :], ws.parts(m % 2, (g * DC + k) * P, P),
                                                 (h_hi[:, k, :], h_lo[:, k, :]), k == 0, k == DC - 1)
                        ins.then_inc(ws.used if g else first_up, 1)

            @block.scalar
            def _(act):
                for m in range(NS + 1):
                    if m < NS:
                        ws.round(act, m, m % 2, 32 * (m // 2 + 1), first=m < 2)
                    if m >= 1:
                        for g in range(2):
                            act.wait_ge(ws.used if g else first_up, m)
                            nc.scalar.activation(q_t[:, 2 * m - 2 + g, :], b.ps[:, (2 * m - 2 + g) % 4, :],
                                                 ACT.Copy).then_inc(out, 1)

            @block.vector
            def _(dve):
                for m in range(NS):
                    ws.rest(dve, m, m % 2)


def build_program(nc, d, out, upto=99):
    b = Bufs(nc)
    b.n_freq = ROPE_A // 2 + DH // 2
    with ExitStack() as ctx:
        def sb(name, shape, dt=F32):
            return ctx.enter_context(nc.sbuf_tensor(name, shape, dt))

        b.consts = sb("consts", [P, CONST_PACK.shape[1]])
        b.x = sb("residual", [P, TT, D])
        b.tok = sb("tok", [P, TT, D])
        b.feat = sb("feat", [P, DC, S])
        b.feat_slots = b.feat[:, :, :].rearrange("p (j a) n -> p j (a n)", j=2)
        b.rows = sb("gate_rows", [P, 6, D])
        b.vec = sb("vec_cols", [P, NVEC])
        b.mod = sb("mod_cols", [P, NMOD])
        b.scale_cols = sb("scale_cols", [P, 5, DC])
        b.silu_c = sb("silu_c", [P, 2 * DC])
        b.sin = sb("sin", [P, 2 * TT, b.n_freq])
        b.cos = sb("cos", [P, 2 * TT, b.n_freq])
        b.stat = sb("stat", [P, TT])
        b.post_stat = sb("post_stat", [P, TT])
        b.ps = ctx.enter_context(nc.psum_tensor("ps", [P, 8, 512], F32))

        def const(name):
            at, n = CONSTS[name]
            return b.consts[:, at:at + n]

        b.const = const
        with ExitStack() as early:
            w = early.enter_context(nc.sbuf_tensor("mod_w", [P, EARLY_SLOTS, DC, MOD_W], F32))
            w_in = [b.sem(f"mod_w_in{j}") for j in range(EARLY_SLOTS)]
            stage_setup(nc, b, d, lambda sp, which: [load_early(sp, d, w, w_in, n) for n in which])
            stage_modulation_early(nc, b, d, w, w_in)
        if upto >= 1:
            b.end_of_part()
            ffn(nc, b, "ffn1", 0, 0, d["w_gate1"], d["w_up1"], d["w_down1"], 0, d)
        if upto >= 2:
            b.end_of_part()
            mixer_one(nc, b, d)
            stage_post_norm(nc, b, "pn2", 1)
        if upto >= 3:
            b.end_of_part()
            ffn(nc, b, "ffn2", 2, 6, d["w_gate2"], d["w_up2"], d["w_down2"], 2)
        if upto >= 4:
            b.end_of_part()
            mixer_two(nc, b, d)
        if upto >= 5:
            b.end_of_part()
            peer(nc, b, d)
        if upto >= 5:
            stage_final(nc, b, out)


_INS = ["x", "c", "positions", "w_mod", "b_mod", "g_pre_ffn1", "w_gate1", "w_up1", "w_down1", "g_post_ffn1",
        "g_pre_mix", "w_in", "g_cq", "g_ckv", "w_uq", "w_uk", "w_uv", "w_iq", "w_up_a", "w_up_b", "w_o",
        "g_post_mix", "g_pre_ffn2", "w_gate2", "w_up2", "w_down2", "g_post_ffn2", "c_2", "positions_2",
        "w_ada_2", "b_ada_2", "g_norm1_2", "w_in_2", "g_q_norm_2", "w_uq_2", "g_kv_norm_2", "w_ukv_2",
        "g_ret_norm_2", "w_out_2", "g_norm2_2", "w_query_2", "sub_keys_2", "expert_u_2", "expert_v_2",
        "g_final_2"]


def kernel(**inputs):
    import numpy as _np
    import concourse.bacc as _bacc
    from concourse import mybir as _mybir
    from concourse.bass_utils import run_bass_kernel_spmd as _run

    nc = _bacc.Bacc("TRN2", target_bir_lowering=False, num_devices=1)
    given = {name: _np.ascontiguousarray(inputs[name]) for name in _INS}
    given["const_pack"] = CONST_PACK
    given["dilated_bias"] = DILATED_BIAS
    arrays, d = {}, {}
    for name, a in given.items():
        arrays[f"in_{name}"] = a
        d[name] = nc.dram_tensor(f"in_{name}", a.shape, _mybir.dt.from_np(a.dtype), kind="ExternalInput").ap()
    out = nc.dram_tensor("out_0", (1, S, D), F32, kind="ExternalOutput").ap()
    build_program(nc, d, out)
    r = _run(nc, [arrays], core_ids=[0])
    return r.results[0]["out_0"]
```
